# Optimizing a Trainium2 kernel written in Bass

```python
import jax, jax.numpy as jnp
from jax import lax
import numpy as np

D_MODEL = 1024
BATCH = 1
SEQ = 1024
DEPTH = 2

NUM_MIXERS = 3
HEAD_DIM = 128
D_INNER = 2 * D_MODEL
MEM_HEADS = 4
MEM_LEN = 256
MIX_HEADS = D_INNER // HEAD_DIM - MEM_HEADS
A_KV_HEADS = MIX_HEADS // 3
A_GROUP = MIX_HEADS // A_KV_HEADS
A_WINDOW = 128
B_GROUPS = ((128, 1), (512, 4), (2048, 16))
NA_ROWS = 8
NA_COLS = 16
GRID_W = 64
ROPE_THETA = 500000.0
ROPE_DIMS = HEAD_DIM // 4
LN_EPS = 1e-5
ALPHA = (2 * DEPTH) ** 0.25
BETA = (8 * DEPTH) ** -0.25
NEG_INF = -1e30
N_A = len(range(0, DEPTH, NUM_MIXERS))
N_B = len(range(1, DEPTH, NUM_MIXERS))
N_C = len(range(2, DEPTH, NUM_MIXERS))
SPLIT_A = (MIX_HEADS * HEAD_DIM, A_KV_HEADS * HEAD_DIM, A_KV_HEADS * HEAD_DIM, MEM_HEADS * HEAD_DIM, D_INNER)
SPLIT_B = (len(B_GROUPS) * MIX_HEADS * HEAD_DIM, MIX_HEADS * HEAD_DIM, MIX_HEADS * HEAD_DIM, MEM_HEADS * HEAD_DIM, D_INNER)
SPLIT_C = (MIX_HEADS * HEAD_DIM, MIX_HEADS * HEAD_DIM, MIX_HEADS * HEAD_DIM, MEM_HEADS * HEAD_DIM, D_INNER)

kernel_name = "hybrid_window_dilated_neighborhood_encoder"

def layer_norm(x, g, b):
    xf = x.astype(jnp.float32)
    mu = jnp.mean(xf, axis=-1, keepdims=True)
    var = jnp.mean(jnp.square(xf - mu), axis=-1, keepdims=True)
    y = (xf - mu) * lax.rsqrt(var + LN_EPS) * g.astype(jnp.float32) + b.astype(jnp.float32)
    return y.astype(x.dtype)

def split_proj(h, sizes):
    idx = np.cumsum(sizes)[:-1].tolist()
    return jnp.split(h, idx, axis=-1)

def to_heads(t, n):
    b, l, _ = t.shape
    return t.reshape(b, l, n, HEAD_DIM).transpose(0, 2, 1, 3)

def apply_rope(x, pos):
    half = ROPE_DIMS // 2
    inv = ROPE_THETA ** (-jnp.arange(half, dtype=jnp.float32) / half)
    ang = pos.astype(jnp.float32)[:, None] * inv[None, :]
    cos, sin = jnp.cos(ang).astype(x.dtype), jnp.sin(ang).astype(x.dtype)
    x1, x2, rest = x[..., :half], x[..., half:ROPE_DIMS], x[..., ROPE_DIMS:]
    return jnp.concatenate([x1 * cos - x2 * sin, x2 * cos + x1 * sin, rest], axis=-1)

def band_attention(q, k, v, w, sink=None, return_lse=False):
    L, dh = q.shape[-2], q.shape[-1]
    nb = -(-L // w)
    pad = nb * w - L
    lead_q, lead_k = q.shape[:-2], k.shape[:-2]
    qb = jnp.pad(q, [(0, 0)] * len(lead_q) + [(0, pad), (0, 0)]).reshape(lead_q + (nb, w, dh))

    def blocks3(t):
        tp = jnp.pad(t, [(0, 0)] * len(lead_k) + [(w, w + pad), (0, 0)]).reshape(lead_k + (nb + 2, w, dh))
        return jnp.concatenate([tp[..., :-2, :, :], tp[..., 1:-1, :, :], tp[..., 2:, :, :]], axis=-2)

    kb, vb = blocks3(k), blocks3(v)
    s = jnp.einsum('...gnid,...njd->...gnij', qb, kb).astype(jnp.float32) * (dh ** -0.5)
    blk = jnp.arange(nb)[:, None, None]
    t_pos = blk * w + jnp.arange(w)[None, :, None]
    s_pos = (blk - 1) * w + jnp.arange(3 * w)[None, None, :]
    valid = (jnp.abs(s_pos - t_pos) <= w) & (s_pos >= 0) & (s_pos < L)
    s = jnp.where(valid, s, NEG_INF)
    m = jnp.max(s, axis=-1, keepdims=True)
    if sink is not None:
        m = jnp.maximum(m, sink)
    p = jnp.exp(s - m)
    z = jnp.sum(p, axis=-1, keepdims=True)
    if sink is not None:
        z = z + jnp.exp(sink - m)
    o = jnp.einsum('...gnij,...njd->...gnid', (p / z).astype(v.dtype), vb)
    o = o.reshape(lead_q + (nb * w, dh))[..., :L, :]
    if return_lse:
        lse = (m + jnp.log(z))[..., 0].reshape(lead_q + (nb * w,))[..., :L]
        return o, lse
    return o

def dilate(t, d):
    L, D = t.shape[-2], t.shape[-1]
    return t.reshape(t.shape[:-2] + (L // d, d, D)).swapaxes(-3, -2)

def undilate(t, d):
    n, D = t.shape[-2], t.shape[-1]
    return t.swapaxes(-3, -2).reshape(t.shape[:-3] + (n * d, D))

def undilate_rows(t, d):
    n = t.shape[-1]
    return t.swapaxes(-2, -1).reshape(t.shape[:-2] + (n * d,))

def mixer_a(q, k, v, sink, pos):
    b, _, l, _ = q.shape
    q, k = apply_rope(q, pos), apply_rope(k, pos)
    qg = q.reshape(b, A_KV_HEADS, A_GROUP, l, HEAD_DIM)
    s = sink.astype(jnp.float32).reshape(A_KV_HEADS, A_GROUP, 1, 1, 1)
    o = band_attention(qg, k, v, A_WINDOW, sink=s)
    return o.reshape(b, MIX_HEADS, l, HEAD_DIM)

def mixer_b(q, k, v, pos):
    q, k = apply_rope(q, pos), apply_rope(k, pos)
    outs, lses = [], []
    for g, (window, dil) in enumerate(B_GROUPS):
        qg = q[:, g * MIX_HEADS:(g + 1) * MIX_HEADS]
        o, lse = band_attention(dilate(qg, dil)[..., None, :, :], dilate(k, dil), dilate(v, dil),
                                window // (2 * dil), return_lse=True)
        outs.append(undilate(o[..., 0, :, :], dil))
        lses.append(undilate_rows(lse[..., 0, :], dil))
    wts = jax.nn.softmax(jnp.stack(lses), axis=0)
    o = jnp.einsum('gbhl,gbhld->bhld', wts, jnp.stack(outs).astype(jnp.float32))
    return o.astype(q.dtype)

def mixer_c(q, k, v, rpb):
    b, h, L, dh = q.shape
    rows = L // GRID_W
    kh, kw = min(NA_ROWS, rows), NA_COLS
    kr, kc = 2 * kh - 1, 2 * kw - 1
    nrb, ncb = -(-rows // kh), GRID_W // kw
    qg = jnp.pad(q.reshape(b, h, rows, GRID_W, dh), ((0, 0), (0, 0), (0, nrb * kh - rows), (0, 0), (0, 0)))
    qb = qg.reshape(b, h, nrb, kh, ncb, kw, dh).transpose(0, 1, 2, 4, 3, 5, 6)
    qrow = jnp.arange(nrb * kh)
    qcol = jnp.arange(GRID_W)
    rs = jnp.clip(qrow - kh // 2, 0, rows - kh)
    cs = jnp.clip(qcol - kw // 2, 0, GRID_W - kw)
    krow = rs[::kh][:, None] + jnp.arange(kr)[None, :]
    kcol = cs[::kw][:, None] + jnp.arange(kc)[None, :]
    ridx = jnp.minimum(krow, rows - 1)
    cidx = jnp.minimum(kcol, GRID_W - 1)
    kg = k.reshape(b, h, rows, GRID_W, dh)
    vg = v.reshape(b, h, rows, GRID_W, dh)
    gi_r, gi_c = ridx[:, None, :, None], cidx[None, :, None, :]
    kb = kg[:, :, gi_r, gi_c].reshape(b, h, nrb, ncb, kr * kc, dh)
    vb = vg[:, :, gi_r, gi_c].reshape(b, h, nrb, ncb, kr * kc, dh)
    qr = qrow.reshape(nrb, kh)
    qc = qcol.reshape(ncb, kw)
    rsq, csq = rs.reshape(nrb, kh), cs.reshape(ncb, kw)
    rv = (krow[:, None, :] >= rsq[:, :, None]) & (krow[:, None, :] < rsq[:, :, None] + kh)
    cv = (kcol[:, None, :] >= csq[:, :, None]) & (kcol[:, None, :] < csq[:, :, None] + kw)
    mask = rv[:, None, :, None, :, None] & cv[None, :, None, :, None, :]
    dri = jnp.clip(krow[:, None, :] - qr[:, :, None] + NA_ROWS - 1, 0, 2 * NA_ROWS - 2)
    dci = jnp.clip(kcol[:, None, :] - qc[:, :, None] + NA_COLS - 1, 0, 2 * NA_COLS - 2)
    bias = rpb.astype(jnp.float32)[:, dri[:, None, :, None, :, None], dci[None, :, None, :, None, :]]
    s = jnp.einsum('bhnmijd,bhnmkd->bhnmijk', qb, kb).astype(jnp.float32) * (dh ** -0.5)
    s = s + bias.reshape((h, nrb, ncb, kh, kw, kr * kc))[None]
    s = jnp.where(mask.reshape(nrb, ncb, kh, kw, kr * kc), s, NEG_INF)
    p = jax.nn.softmax(s, axis=-1).astype(v.dtype)
    o = jnp.einsum('bhnmijk,bhnmkd->bhnmijd', p, vb)
    o = o.transpose(0, 1, 2, 4, 3, 5, 6).reshape(b, h, nrb * kh, GRID_W, dh)[:, :, :rows]
    return o.reshape(b, h, L, dh)

def memory_attention(mq, mem, w_mkv):
    mk, mv = jnp.split(jnp.einsum('bmd,de->bme', mem, w_mkv), 2, axis=-1)
    mk, mv = to_heads(mk, MEM_HEADS), to_heads(mv, MEM_HEADS)
    s = jnp.einsum('bhld,bhmd->bhlm', mq, mk).astype(jnp.float32) * (HEAD_DIM ** -0.5)
    p = jax.nn.softmax(s, axis=-1).astype(mv.dtype)
    return jnp.einsum('bhlm,bhmd->bhld', p, mv)

def setup_inputs(seed: int = 0) -> dict:
    key = jax.random.key(seed)
    ks = jax.random.split(key, 12)
    nrm = jax.random.normal
    f32 = jnp.float32
    x = nrm(ks[0], (BATCH, SEQ, D_MODEL), f32)
    mem = nrm(ks[1], (BATCH, MEM_LEN, D_MODEL), f32)
    w_in_a = nrm(ks[2], (N_A, D_MODEL, sum(SPLIT_A)), f32) * D_MODEL ** -0.5
    sink_a = nrm(ks[3], (N_A, MIX_HEADS), f32)
    w_in_b = nrm(ks[4], (N_B, D_MODEL, sum(SPLIT_B)), f32) * D_MODEL ** -0.5
    w_in_c = nrm(ks[5], (N_C, D_MODEL, sum(SPLIT_C)), f32) * D_MODEL ** -0.5
    rpb_c = nrm(ks[6], (N_C, MIX_HEADS, 2 * NA_ROWS - 1, 2 * NA_COLS - 1), f32) * 0.1
    w_mkv = nrm(ks[7], (DEPTH, D_MODEL, 2 * MEM_HEADS * HEAD_DIM), f32) * D_MODEL ** -0.5
    w_out = nrm(ks[8], (DEPTH, D_INNER, D_MODEL), f32) * (D_INNER ** -0.5 * BETA)
    ln_g = 1.0 + 0.05 * nrm(ks[9], (DEPTH, D_MODEL), f32)
    ln_b = 0.02 * nrm(ks[10], (DEPTH, D_MODEL), f32)
    return {"x": x, "mem": mem, "w_in_a": w_in_a, "sink_a": sink_a, "w_in_b": w_in_b,
            "w_in_c": w_in_c, "rpb_c": rpb_c, "w_mkv": w_mkv, "w_out": w_out,
            "ln_g": ln_g, "ln_b": ln_b}

def reference(x, mem, w_in_a, sink_a, w_in_b, w_in_c, rpb_c, w_mkv, w_out, ln_g, ln_b):
    b, L, _ = x.shape
    pos = jnp.arange(L)
    for i in range(DEPTH):
        kind, j = i % NUM_MIXERS, i // NUM_MIXERS
        if kind == 0:
            q, k, v, mq, gate = split_proj(jnp.einsum('bld,de->ble', x, w_in_a[j]), SPLIT_A)
            o_mix = mixer_a(to_heads(q, MIX_HEADS), to_heads(k, A_KV_HEADS), to_heads(v, A_KV_HEADS), sink_a[j], pos)
        elif kind == 1:
            q, k, v, mq, gate = split_proj(jnp.einsum('bld,de->ble', x, w_in_b[j]), SPLIT_B)
            o_mix = mixer_b(to_heads(q, len(B_GROUPS) * MIX_HEADS), to_heads(k, MIX_HEADS), to_heads(v, MIX_HEADS), pos)
        else:
            q, k, v, mq, gate = split_proj(jnp.einsum('bld,de->ble', x, w_in_c[j]), SPLIT_C)
            o_mix = mixer_c(to_heads(q, MIX_HEADS), to_heads(k, MIX_HEADS), to_heads(v, MIX_HEADS), rpb_c[j])
        o_mem = memory_attention(to_heads(mq, MEM_HEADS), mem, w_mkv[i])
        y = jnp.concatenate([o_mix, o_mem], axis=1).transpose(0, 2, 1, 3).reshape(b, L, D_INNER)
        y = y * jax.nn.silu(gate)
        branch = jnp.einsum('ble,ed->bld', y, w_out[i])
        x = layer_norm(ALPHA * x + branch, ln_g[i], ln_b[i])
    return x


_drawn_inputs = setup_inputs


def setup_inputs(seed=0):
    import zlib

    import numpy as np

    out = dict(_drawn_inputs(seed))
    spreads = {}
    factors = {'mem': 3.847, 'sink_a': 8.0, 'w_mkv': 3.595}
    for name, (base, spread) in spreads.items():
        noise = np.random.default_rng([zlib.crc32(name.encode()), seed]).standard_normal(out[name].shape)
        drawn = base * np.exp(spread * noise) if base else spread * noise
        out[name] = __import__('jax').numpy.asarray(drawn.astype(out[name].dtype))
    for name, factor in factors.items():
        out[name] = (out[name] * factor).astype(out[name].dtype)
    return out
```

```python
from contextlib import ExitStack

import numpy as np

import concourse.bass as bass
from concourse import mybir

F32 = mybir.dt.float32
F32R = mybir.dt.float32r
ALU = mybir.AluOpType
ACT = mybir.ActivationFunctionType

P = 128
D = 1024
L = 1024
MEM = 256
DH = 128
HEADS = 12
MEM_HEADS = 4
KV = 4
GROUP = HEADS // KV
D_INNER = 2 * D
DEPTH = 2
ALPHA = (2 * DEPTH) ** 0.25
LN_EPS = 1e-5
ROPE = DH // 4
THETA = 500000.0
SCALE = DH ** -0.5
NEG = -1e30
KT = D // P
HALF = 512
TILES = L // P
NE = D_INNER // P
W_A = 128
W_B = 64
DIL = (1, 4, 16)

A_Q, A_K = 0, HEADS * DH
A_V = A_K + KV * DH
A_MQ = A_V + KV * DH
A_G = A_MQ + MEM_HEADS * DH
B_Q, B_K = 0, 3 * HEADS * DH
B_V = B_K + HEADS * DH
B_MQ = B_V + HEADS * DH
B_G = B_MQ + MEM_HEADS * DH

C_A = 2 * DEPTH * MEM_HEADS
C_MA = C_A + 8 * KV
C_OA = C_MA + 2 * MEM_HEADS
C_B = C_OA + 2 * NE
C_MB = C_B + 6 * HEADS
C_OB = C_MB + 2 * MEM_HEADS
C_END = C_OB + 2 * NE
U_A = DEPTH * MEM_HEADS
U_MA = U_A + 8 * KV
U_B = U_MA + 2 * MEM_HEADS
U_MB = U_B + 6 * HEADS
U_END = U_MB + 2 * MEM_HEADS
T_A = 0
T_MA = T_A + GROUP * TILES * KV
T_B = T_MA + TILES * MEM_HEADS
T_MB = T_B + 3 * TILES * HEADS
T_END = T_MB + TILES * MEM_HEADS
X_A_PER = 2 + GROUP * TILES
X_B_G = (0, 3 + TILES, 6 + 2 * TILES)
X_B_PER = 8 + 3 * TILES
X_A = 2 * DEPTH * MEM_HEADS
X_MA = X_A + X_A_PER * KV
X_B = X_MA + TILES * MEM_HEADS
X_MB = X_B + X_B_PER * HEADS
X_END = X_MB + TILES * MEM_HEADS
O_A = 0
O_MA = O_A + 2 * GROUP * KV
O_B = O_MA + 2 * MEM_HEADS
O_MB = O_B + 12 * HEADS
O_END = O_MB + 2 * MEM_HEADS
R_A = 0
R_B = R_A + 8 * KV
G_A = 0
G_MA = G_A + GROUP * KV
G_B = G_MA + MEM_HEADS
G_MB = G_B + HEADS


class Job:

    def __init__(self, a, x, x_odd, o, stat, tiles, vbuf, fills=(), sink=None, queries=None,
                 v_use=None, mem_unit=None, group=0, out=0, stored=None):
        self.a, self.x, self.x_odd, self.o, self.stat = a, x, x_odd, o, stat
        self.tiles, self.vbuf, self.fills, self.sink = tiles, vbuf, fills, sink
        self.queries, self.v_use, self.mem_unit = queries, v_use, mem_unit
        self.group, self.out, self.stored = group, out, stored


class Segment:

    def __init__(self, c, slot, next_full, u, to=None, order=1, also=None, rope=None, gate=None,
                 job=None, combine=None, y=False):
        self.c, self.slot, self.next_full, self.u = c, slot, next_full, u
        self.to, self.order, self.also, self.rope, self.gate = to, order, also, rope, gate
        self.job, self.combine, self.y = job, combine, y


STEPS = 2 * KT
LEAD, LAG_T, LAG_PV = 4, 6, 8
COMB_STEPS = 13


def riding(job, s):
    if job is None:
        return None, None, None, None

    def due(lag):
        return s - lag if 0 <= s - lag < TILES else None

    return (s - 1 if 1 <= s <= len(job.fills) else None), due(LEAD), due(LAG_T), due(LAG_PV)


def dilated(v, d):
    return v.rearrange("p (n r) -> p r n", r=d)


def encoder(nc, x, mem, w_in_a, sink_a, w_in_b, w_mkv, w_out, ln_g, ln_b,
            rope_cos, rope_sin, mask_a, mask_b, mask_b2, identity, out):
    ctx = ExitStack()
    with ctx:
        def sb(name, shape, dt=F32):
            return ctx.enter_context(nc.sbuf_tensor(name, shape, dt))

        def sem(name):
            return ctx.enter_context(nc.semaphore(name))

        xT = sb("xT", [P, 2, KT, L], F32R)
        w_split = sb("w_split", [P, 2, 2, D], F32R)
        w_raw = sb("w_raw", [P, 2, D])
        y_split = sb("y_split", [P, 2, 2, HALF], F32R)
        mem_k = sb("mem_k", [P, DEPTH * MEM_HEADS, MEM])
        mem_v = sb("mem_v", [P, DEPTH * MEM_HEADS, MEM])
        head_mk = sb("head_mk", [P, MEM])
        head_mv = sb("head_mv", [P, MEM])
        cosb = sb("cosb", [ROPE, L])
        sinb = sb("sinb", [ROPE, L])
        m_a = sb("m_a", [P, 3 * W_A])
        m_b = sb("m_b", [P, 2 * P])
        m_b2 = sb("m_b2", [P, P])
        m_0 = sb("m_0", [P, MEM])
        ident = sb("ident", [P, P])
        ones = sb("ones", [P, P])
        diag = sb("diag", [P, 2, 4, P])
        sinks = sb("sinks", [P, HEADS])
        sinks_raw = sb("sinks_raw", [P, HEADS])
        sinks_neg = sb("sinks_neg", [P, HEADS])
        rmax = sb("rmax", [P, 3, TILES])
        nmax = sb("nmax", [P, 3, TILES])
        zsum = sb("zsum", [P, 3, TILES])
        zinv = sb("zinv", [P, 3, TILES])
        lnz = sb("lnz", [P, 3, TILES])
        lse = sb("lse", [P, 3, TILES])
        stats = sb("stats", [P, TILES, 2, 6])
        mv = sb("mv", [P, TILES, 2])
        rstd = sb("rstd", [P, TILES, 2])
        power = sb("power", [P, 2])
        WORDS = 19 * L + 512
        work = sb("work", [P, WORDS])
        at = [0]

        def take(n):
            at[0] += n
            return work[:, at[0] - n:at[0]]

        kT = take(L)
        qT = [take(L), take(L)]
        vT = take(L)
        vT16 = take(L)
        vbuf = [take(12 * DH), take(12 * DH)]
        s_sb = [take(388), take(388)]
        p_sb = [take(388), take(388)]
        pT = [take(3 * P), take(3 * P)]
        oT = [take(L) for _ in range(3)]
        lT = [take(L) for _ in range(3)]
        gate = take(L)
        top = take(L)
        rope_a = take(HALF)
        rope_b = take(HALF)
        assert at[0] <= WORDS
        rows = work[:, 0:TILES * D].rearrange("p (t d) -> p t d", t=TILES)
        mem_rows = work[:, TILES * D:(TILES + 2) * D].rearrange("p (t d) -> p t d", t=2)
        mem_vT = gate[:, 0:MEM]
        y_raw = work[:, 10 * D:11 * D].rearrange("p (s n) -> p s n", s=2)
        g_row = work[:, 11 * D:12 * D]
        b_row = work[:, 12 * D:13 * D]

        bank = [ctx.enter_context(nc.psum_tensor(f"bank{i}", [P, HALF], F32)) for i in range(8)]
        PB, SB, TB, OB = bank[0:2], bank[2:4], bank[4:6], bank[6:8]

        y_dram = nc.dram_tensor("y_scratch", [NE, P, L], F32, kind="Internal").ap()
        x1_dram = nc.dram_tensor("x1_scratch", [TILES, P, D], F32, kind="Internal").ap()

        const_in = sem("const_in")
        row_in = sem("row_in")
        consts = sem("consts")
        sink_consts = sem("sink_consts")
        w_full = [sem("w_full0"), sem("w_full1")]
        w_hi = sem("w_hi")
        w_lo = sem("w_lo")
        p_ready = [sem("p_ready0"), sem("p_ready1")]
        p_free = [sem("p_free0"), sem("p_free1")]
        xt_ready = sem("xt_ready")
        xt_hi = sem("xt_hi")
        xt_lo = sem("xt_lo")
        rope_turned = sem("rope_turned")
        rope_sine = sem("rope_sine")
        rope_done = sem("rope_done")
        t_ready = sem("t_ready")
        t_free = sem("t_free")
        s_ready = sem("s_ready")
        s_free = sem("s_free")
        negmax = sem("negmax")
        exp_done = sem("exp_done")
        zinv_done = sem("zinv_done")
        p_done = sem("p_done")
        pv_done = sem("pv_done")
        o_free = sem("o_free")
        tanh_done = sem("tanh_done")
        y_done = sem("y_done")
        stored = [sem(f"stored{j}") for j in range(3)]
        memkv = sem("memkv")
        lnz_done = sem("lnz_done")
        lse_done = sem("lse_done")
        diag_done = sem("diag_done")
        bc_done = sem("bc_done")
        comb = sem("comb")
        comb_act = sem("comb_act")
        y_full = [sem("y_full0"), sem("y_full1")]
        y_hi = sem("y_hi")
        y_lo = sem("y_lo")
        out_step = sem("out_step")
        br_ready = sem("br_ready")
        z_free = sem("z_free")
        res_in = sem("res_in")
        gb_in = sem("gb_in")
        ln_stat = sem("ln_stat")
        ln_aggr = sem("ln_aggr")
        ln_eps = sem("ln_eps")
        ln_rstd = sem("ln_rstd")
        ln_step = sem("ln_step")
        ln_done = sem("ln_done")
        rows_out = sem("rows_out")
        held = sem("held")

        def a_tiles():
            tiles = []
            for t in range(TILES):
                lo, hi = max(t - 1, 0), min(t + 2, TILES)
                m0 = (lo - t + 1) * P
                tiles.append((qT[0][:, t * P:(t + 1) * P], kT[:, lo * P:hi * P], (hi - lo) * P,
                              m_a[:, m0:m0 + (hi - lo) * P],
                              [(b, P, (b - lo) * P) for b in range(lo, hi)]))
            return tiles

        def mem_tiles():
            return [(qT[0][:, t * P:(t + 1) * P], head_mk[:, :], MEM, m_0[:, :],
                     [(0, P, 0), (1, P, P)]) for t in range(TILES)]

        def b_tiles(g):
            q = qT[g % 2]
            tiles = []
            if g == 0:
                for t in range(TILES):
                    lo, hi = max(t * P - W_B, 0), min((t + 1) * P + W_B, L)
                    m0 = lo - (t * P - W_B)
                    chunks = [(t - 1, P, 0)] if t > 0 else []
                    chunks += [(t, P, P if t else W_B)] if t < TILES - 1 else []
                    chunks += [(7, W_B, 0)] if t == 0 else []
                    chunks += [(8, W_B, P)] if t == TILES - 1 else []
                    tiles.append((q[:, t * P:(t + 1) * P], kT[:, lo:hi], hi - lo,
                                  m_b[:, m0:m0 + hi - lo], chunks))
            elif g == 1:
                qd, kd = dilated(q, 4), dilated(kT, 4)
                for r in range(4):
                    tiles.append((qd[:, r, 0:P], kd[:, r, 0:P + W_B], P + W_B,
                                  m_b[:, W_B:2 * P], [(2 * r, P, 0), (2 * r + 1, W_B, P)]))
                    tiles.append((qd[:, r, P:2 * P], kd[:, r, W_B:2 * P], P + W_B,
                                  m_b[:, 0:P + W_B], [(2 * r + 1, P, W_B), (8 + r, W_B, 0)]))
            else:
                kd = dilated(kT, 16)
                for j in range(TILES):
                    tiles.append((q[:, j * P:(j + 1) * P], kd[:, 2 * j:2 * j + 2, :], P,
                                  m_b2[:, :], [(j, P, 0)]))
            return tiles

        def whole_tiles(v, first, last):
            return [(v[:, t * P:(t + 1) * P], P) for t in range(first, last)]

        def b_fills(g):
            if g == 0:
                s = [(vT[:, W_B + i * P:W_B + (i + 1) * P], P) for i in range(TILES - 1)]
                return [s[0:4], s[4:7], [(vT[:, 0:W_B], W_B), (vT[:, L - W_B:L], W_B)]]
            if g == 1:
                d = dilated(vT, 4)
                s = [(d[:, r, n * P:(n + 1) * P], P) for r in range(4) for n in range(2)]
                return [s[0:4], s[4:8], [(d[:, r, W_B:P], W_B) for r in range(4)]]
            return [whole_tiles(vT16, 0, 4), whole_tiles(vT16, 4, 8)]

        def half_in_order(v, d, h):
            if d == 1:
                return v[:, h * HALF:(h + 1) * HALF]
            n = HALF // d
            return v.rearrange("p (r n) -> p r n", r=d)[:, :, h * n:(h + 1) * n]

        def like_order(v, d):
            return v if d == 1 else dilated(v, d)

        def unit_a(i):
            def seg(k, **kw):
                return Segment(C_A + k + i * 8, k % 2, 16 * ((C_A + k + 1) // 2 + 1) + i * 64,
                               U_A + k + i * 8, **kw)

            r = R_A + i * 8
            segs = [seg(0, to=kT, rope=r), seg(1, to=vT)]
            for j in range(GROUP):
                segs.append(seg(2 + 2 * j, to=qT[0], rope=r + 2 + 2 * j))
                fills = [whole_tiles(vT, 0, 4), whole_tiles(vT, 4, 8)] if j == 0 else []
                x0 = 0 if j == 0 else 2 + j * TILES
                job = Job(T_A + j * TILES + i * 24, X_A + x0 + i * X_A_PER, x0 % 2,
                          O_A + 2 * j + i * 6, j, a_tiles(), vbuf[0], fills, sink=i * GROUP + j,
                          queries=r + 5 + 2 * j, v_use=U_A + 3 + i * 8, out=j,
                          stored=16 + i * 16)
                segs.append(seg(3 + 2 * j, job=job, gate=G_A + j + i * GROUP, y=True))
            return segs

        def unit_mem(layer, i):
            c, u = (C_MA, C_MB)[layer], (U_MA, U_MB)[layer]
            before = KV if layer == 0 else KV + MEM_HEADS + HEADS
            job = Job((T_MA, T_MB)[layer] + i * TILES, (X_MA, X_MB)[layer] + i * TILES, 0,
                      (O_MA, O_MB)[layer] + i * 2, 0, mem_tiles(), head_mv,
                      queries=u + 2 + i * 2, mem_unit=i + layer * MEM_HEADS, out=0,
                      stored=16 + 16 * before + i * 16)
            return [Segment(c + i * 2, 0, 16 * ((c + 1) // 2 + 1) + i * 16, u + i * 2, to=qT[0]),
                    Segment(c + 1 + i * 2, 1, 16 * ((c + 2) // 2 + 1) + i * 16, u + 1 + i * 2,
                            job=job, gate=(G_MA, G_MB)[layer] + i, y=True)]

        def b_seg(i, k, **kw):
            return Segment(C_B + k + i * 6, k % 2, 16 * ((C_B + k + 1) // 2 + 1) + i * 48,
                           U_B + k + i * 6, **kw)

        def front_b(i, combine=None):
            r = R_B + i * 8
            part = [None if combine is None else (combine, n) for n in range(3)]
            return [b_seg(i, 0, to=kT, rope=r, combine=part[0]),
                    b_seg(i, 1, to=vT, also=vT16, combine=part[1]),
                    b_seg(i, 2, to=qT[0], rope=r + 2, combine=part[2])]

        def back_b(i):
            segs = []
            for g in range(3):
                job = Job(T_B + g * TILES + i * 24, X_B + X_B_G[g] + i * X_B_PER, X_B_G[g] % 2,
                          O_B + 2 * g + i * 12, g, b_tiles(g), vbuf[g % 2], b_fills(g),
                          queries=R_B + 5 + 2 * g + i * 8, v_use=U_B + 3 + i * 6, group=g, out=g,
                          stored=16 + 16 * (KV + MEM_HEADS) + i * 16 if g == 0 else None)
                if g < 2:
                    segs.append(b_seg(i, 3 + g, to=qT[(g + 1) % 2], order=(1, 16)[g],
                                      rope=R_B + 4 + 2 * g + i * 8, job=job))
                else:
                    segs.append(b_seg(i, 5, job=job, gate=G_B + i))
            return segs

        block = ctx.enter_context(nc.Block())

        @block.sync
        def _(sp):
            nc.sync.dma_start(mem_rows, mem[0].rearrange("(t p) d -> p t d", p=P)
                              ).then_inc(row_in, 16)
            nc.sync.dma_start(ident[:, :], identity).then_inc(const_in, 16)

            def load(c, slot, src):
                sp.wait_ge(w_lo, c + 1)
                sp.sem_inc(held, 1)
                nc.sync.dma_start(w_raw[:, slot, :].rearrange("p (k n) -> p k n", k=KT),
                                  src).then_inc(w_full[slot], 16)

            def columns(w, col):
                return w.rearrange("(k p) n -> p k n", p=P)[:, :, bass.ds(col, P)]

            def store(j, row, y):
                sp.wait_ge(y_done, y + 2)
                sp.sem_inc(held, 1)
                nc.sync.dma_start(y_dram[bass.ds(row, 1)].rearrange("a p n -> p (a n)"),
                                  oT[j]).then_inc(stored[j], 16)

            for layer in range(DEPTH):
                with sp.Fori(0, MEM_HEADS) as h:
                    c = h * 2 + layer * MEM_HEADS * 2
                    load(c, 0, columns(w_mkv[layer], h * DH))
                    load(c + 1, 1, columns(w_mkv[layer], h * DH + MEM_HEADS * DH))
                if layer == 0:
                    nc.sync.dma_start(rows, x[0].rearrange("(t p) d -> p t d", p=P)
                                      ).then_inc(row_in, 16)
                    for t, src in ((cosb, rope_cos), (sinb, rope_sin), (m_a, mask_a), (m_b, mask_b),
                                   (m_b2, mask_b2)):
                        nc.sync.dma_start(t[:, :], src).then_inc(const_in, 16)
                    nc.sync.dma_start(sinks[:, :], sink_a[0].partition_broadcast(P)
                                      ).then_inc(const_in, 16)

            def a_head(i, j):
                c = C_A + 2 + 2 * j + i * 8
                load(c, 0, columns(w_in_a[0], i * (GROUP * DH) + (A_Q + j * DH)))
                load(c + 1, 1, columns(w_in_a[0], i * (GROUP * DH) + (A_G + j * DH)))

            def a_key_value(i):
                load(C_A + i * 8, 0, columns(w_in_a[0], i * DH + A_K))
                load(C_A + 1 + i * 8, 1, columns(w_in_a[0], i * DH + A_V))

            def a_heads(i):
                a_head(i, 0)
                for j in range(1, GROUP):
                    a_head(i, j)
                    store(j - 1, i * GROUP + (j - 1), G_A + (j - 1) + i * GROUP)

            def mem_head(layer, i):
                w, mq, g = ((w_in_a[0], A_MQ, A_G), (w_in_b[0], B_MQ, B_G))[layer]
                c = (C_MA, C_MB)[layer] + i * 2
                load(c, 0, columns(w, i * DH + mq))
                load(c + 1, 1, columns(w, i * DH + (g + HEADS * DH)))

            a_key_value(0)
            with sp.Fori(0, KV - 1) as i:
                a_heads(i)
                a_key_value(i + 1)
                store(GROUP - 1, i * GROUP + (GROUP - 1), G_A + (GROUP - 1) + i * GROUP)
            a_heads(KV - 1)
            mem_head(0, 0)
            store(GROUP - 1, HEADS - 1, G_A + HEADS - 1)

            def mem_heads(layer):
                with sp.Fori(1, MEM_HEADS) as i:
                    mem_head(layer, i)
                    store(0, i + (HEADS - 1), (G_MA, G_MB)[layer] - 1 + i)

            def branch(layer, totals, residual, ahead, dst):
                w = w_out[layer].rearrange("(e p) n -> e p n", p=P)
                c0, y0 = (C_OA, C_OB)[layer], layer * 2 * NE

                def load_w(h, e, s):
                    sp.wait_ge(w_lo, h * NE + e + (c0 + s + 1))
                    sp.sem_inc(held, 1)
                    nc.sync.dma_start(w_raw[:, s, :], w[bass.ds(e + s, 1)]
                                      .rearrange("a p n -> p (a n)")).then_inc(w_full[s], 16)

                def load_y(h, e, s):
                    sp.wait_ge(y_lo, h * NE + e + (y0 + s + 1))
                    sp.sem_inc(held, 1)
                    nc.sync.dma_start(y_raw[:, s, :], y_dram[bass.ds(e + s, 1)]
                                      .rearrange("a p n -> p (a n)")[:, bass.ds(h * HALF, HALF)]
                                      ).then_inc(y_full[s], 16)

                def load_pairs(h, first, last):
                    with sp.Fori(first // 2, last // 2) as pair:
                        for s in range(2):
                            load_w(h, pair * 2, s)
                            load_y(h, pair * 2, s)

                load_w(0, 0, 0)
                load_w(0, 0, 1)
                store(0, NE - 1, (G_MA, G_MB)[layer] + MEM_HEADS - 1)
                for j in range(3):
                    sp.wait_ge(stored[j], 16 + 16 * totals[j])
                load_y(0, 0, 0)
                load_y(0, 0, 1)
                if layer == 1:
                    sp.wait_ge(rows_out, 16 * TILES)
                load_pairs(0, 2, 8)
                nc.sync.dma_start(rows[:, 0:4, :], residual[:, 0:4, :]).then_inc(res_in, 16)
                nc.sync.dma_start(g_row, ln_g[layer].partition_broadcast(P)).then_inc(gb_in, 16)
                nc.sync.dma_start(b_row, ln_b[layer].partition_broadcast(P)).then_inc(gb_in, 16)
                load_pairs(0, 8, NE)
                load_pairs(1, 0, 8)
                nc.sync.dma_start(rows[:, 4:8, :], residual[:, 4:8, :]).then_inc(res_in, 16)
                load_pairs(1, 8, NE)
                ahead()
                with sp.Fori(0, TILES) as t:
                    sp.wait_ge(ln_done, t + (layer * TILES + 1))
                    sp.sem_inc(held, 1)
                    nc.sync.dma_start(dst[bass.ds(t, 1)].rearrange("a p d -> p (a d)"),
                                      rows[:, bass.ds(t, 1), :].rearrange("p a d -> p (a d)")
                                      ).then_inc(rows_out, 16)

            def b_load(i, k, col):
                load(C_B + k + i * 6, k % 2, columns(w_in_b[0], i * DH + col))

            def b_front(i):
                b_load(i, 0, B_K)
                b_load(i, 1, B_V)
                b_load(i, 2, B_Q)

            def b_back(i, before=None):
                b_load(i, 3, B_Q + HEADS * DH)
                b_load(i, 4, B_Q + 2 * HEADS * DH)
                if before is not None:
                    store(0, before, G_B + before)
                b_load(i, 5, B_G)

            mem_heads(0)
            branch(0, (KV + MEM_HEADS, KV, KV), x[0].rearrange("(t p) d -> p t d", p=P),
                   lambda: (b_load(0, 0, B_K), b_load(0, 1, B_V)), x1_dram)
            b_load(0, 2, B_Q)
            b_back(0)
            b_front(1)
            with sp.Fori(1, HEADS - 1) as i:
                b_back(i, i - 1)
                b_front(i + 1)
            b_back(HEADS - 1, HEADS - 2)
            mem_head(1, 0)
            store(0, HEADS - 1, G_B + HEADS - 1)
            mem_heads(1)
            branch(1, (KV + MEM_HEADS + HEADS + MEM_HEADS, KV, KV),
                   x1_dram.rearrange("t p d -> p t d"), lambda: None,
                   out[0].rearrange("(t p) d -> t p d", p=P))
            sp.wait_ge(rows_out, 16 * TILES * DEPTH)

        @block.gpsimd
        def _(pool):
            nc.gpsimd.memset(m_0[:, :], 0.0).then_inc(consts, 1)
            nc.gpsimd.memset(ones[:, :], 1.0).then_inc(consts, 1)
            nc.gpsimd.memset(power[:, 0:1], LN_EPS).then_inc(consts, 1)
            nc.gpsimd.memset(power[:, 1:2], -0.5).then_inc(consts, 1)
            pool.wait_ge(consts, 4)
            pool.wait_ge(t_free, X_A + 2)

            def mem_heads(layer):
                with pool.Fori(0, MEM_HEADS) as i:
                    pool.wait_ge(pv_done, (T_MA, T_MB)[layer] + i * TILES)
                    pool.sem_inc(held, 1)
                    src = i + layer * MEM_HEADS
                    nc.gpsimd.tensor_copy(head_mk[:, :], mem_k[:, bass.ds(src, 1), :]
                                          .rearrange("p a n -> p (a n)")).then_inc(memkv, 1)
                    nc.gpsimd.tensor_copy(head_mv[:, :], mem_v[:, bass.ds(src, 1), :]
                                          .rearrange("p a n -> p (a n)")).then_inc(memkv, 1)

            def norms(layer):
                for t in range(TILES):
                    n = layer * TILES + t
                    pool.wait_ge(ln_aggr, n + 1)
                    nc.gpsimd.tensor_tensor(rstd[:, t, 0:1], mv[:, t, 1:2], power[:, 0:1],
                                            ALU.add).then_inc(ln_eps, 1)
                    pool.wait_ge(ln_eps, n + 1)
                    nc.gpsimd.tensor_tensor(rstd[:, t, 1:2], rstd[:, t, 0:1], power[:, 1:2],
                                            ALU.pow).then_inc(ln_rstd, 1)

            mem_heads(0)
            norms(0)
            pool.wait_ge(const_in, 16 * 7)
            with pool.Fori(0, HEADS) as i:
                pool.wait_ge(lse_done, i + 1)
                for n in range(6):
                    g, h = n // 2, n % 2
                    pool.wait_ge(bc_done, i * 6 + (n + 1))
                    nc.gpsimd.tensor_tensor(
                        diag[:, n % 2], ident[:, :].unsqueeze(1).broadcast_to([P, 4, P]),
                        lse[:, g, 4 * h:4 * h + 4].unsqueeze(2).broadcast_to([P, 4, P]),
                        ALU.mult).then_inc(diag_done, 1)
            mem_heads(1)
            norms(1)

        @block.tensor
        def _(pe):
            pe.sem_inc(bc_done, 2)
            pe.wait_ge(consts, 4)

            def rows_to_columns(src, tiles, first, ready):
                for f in range(2 * tiles):
                    t, k0 = f // 2, 4 * (f % 2)
                    ready(t)
                    pe.wait_ge(xt_lo, first + f + 1)
                    for k in range(4):
                        mm = nc.tensor.transpose(TB[f % 2][:, k * P:(k + 1) * P],
                                                 src[:, t, (k0 + k) * P:(k0 + k + 1) * P],
                                                 ident[:, :])
                    mm.then_inc(xt_ready, 1)

            def step(dst, cols, slot, k):
                w_h = w_split[:, slot, 0, k * P:(k + 1) * P]
                w_l = w_split[:, slot, 1, k * P:(k + 1) * P]
                nc.tensor.matmul(dst, w_h, xT[:, 0, k, cols], start=(k == 0), stop=False)
                nc.tensor.matmul(dst, w_h, xT[:, 1, k, cols], start=False, stop=False)
                return nc.tensor.matmul(dst, w_l, xT[:, 0, k, cols], start=False,
                                        stop=(k == KT - 1))

            def values(job, f):
                if f == 0:
                    pe.wait_ge(p_free[0], job.v_use)
                    pe.wait_ge(p_free[1], job.v_use)
                pe.wait_ge(t_free, job.x + (f + 1))
                if job.fills[f][0][1] < P:
                    pe.sem_inc(held, 1)
                for n, (src, rows_) in enumerate(job.fills[f]):
                    mm = nc.tensor.transpose(TB[(job.x_odd + f) % 2][0:rows_, n * P:(n + 1) * P],
                                             src, ident[:, :])
                mm.then_inc(t_ready, 1)

            def scores(job, t):
                q, k, n, _, _ = job.tiles[t]
                if t == 0 and job.mem_unit is None:
                    pe.wait_ge(rope_done, job.queries)
                elif t == 0:
                    pe.wait_ge(p_free[0], job.queries)
                    pe.wait_ge(p_free[1], job.queries)
                    pe.wait_ge(memkv, job.mem_unit * 2 + 2)
                pe.wait_ge(s_free, job.a + (t + 1))
                nc.tensor.matmul(SB[t % 2][:, 0:n], q, k, start=True, stop=True).then_inc(s_ready, 1)

            def transposes(job, t):
                n = len(job.fills) + t
                pe.wait_ge(t_free, job.x + (n + 1))
                pe.wait_ge(p_done, job.a + (t + 1))
                for c, (_, keys, k0) in enumerate(job.tiles[t][4]):
                    mm = nc.tensor.transpose(TB[(job.x_odd + n) % 2][0:keys, c * P:(c + 1) * P],
                                             p_sb[t % 2][:, 1 + k0:1 + k0 + keys], ident[:, :])
                mm.then_inc(t_ready, 1)

            def outputs(job, t):
                h, chunks = t // 4, job.tiles[t][4]
                if t % 4 == 0:
                    pe.wait_ge(o_free, job.o + (h + 1))
                pe.wait_ge(t_free, job.x + (len(job.fills) + t + 3))
                for c, (v, keys, _) in enumerate(chunks):
                    mm = nc.tensor.matmul(OB[h][:, (t % 4) * P:(t % 4 + 1) * P],
                                          job.vbuf[0:keys, v * DH:(v + 1) * DH],
                                          pT[t % 2][0:keys, c * P:(c + 1) * P],
                                          start=(c == 0), stop=(c == len(chunks) - 1))
                mm.then_inc(pv_done, 1)

            def broadcast(i, n):
                pe.wait_ge(o_free, i * 12 + (O_B + 7 + n))
                pe.wait_ge(diag_done, i * 6 + (n + 1))
                nc.tensor.matmul(OB[n % 2][:, :], ones[:, :],
                                 diag[:, n % 2].rearrange("p a n -> p (a n)"),
                                 start=True, stop=True).then_inc(bc_done, 1)

            def run(seg):
                pe.wait_ge(w_lo, seg.c + 3)
                for s in range(STEPS):
                    h, k = s // KT, s % KT
                    if k == 0:
                        pe.wait_ge(p_free[h], seg.u + 1)
                    mm = step(PB[h][:, :], slice(h * HALF, (h + 1) * HALF), seg.slot, k)
                    if k == KT - 1:
                        mm.then_inc(p_ready[h], 1)
                    if seg.combine is not None and seg.combine[1] == 0 and 6 <= s < 12:
                        broadcast(seg.combine[0], s - 6)
                    fill, t_s, t_t, t_o = riding(seg.job, s)
                    if fill is not None:
                        values(seg.job, fill)
                    if t_o is not None:
                        outputs(seg.job, t_o)
                    if t_t is not None:
                        transposes(seg.job, t_t)
                    if t_s is not None:
                        scores(seg.job, t_s)

            def branch(layer):
                c0, y0 = (C_OA, C_OB)[layer], layer * 2 * NE

                def out_e(h, e, slot, first, last):
                    pe.wait_ge(w_lo, h * NE + e + (c0 + 3))
                    pe.wait_ge(y_lo, h * NE + e + (y0 + 3))
                    for b in range(8):
                        t, cols = b // 2, slice((b % 2) * HALF, (b % 2 + 1) * HALF)
                        if first:
                            pe.wait_ge(z_free, h * 8 + (layer * 16 + b + 1))
                        y_h = y_split[:, slot, 0, t * P:(t + 1) * P]
                        y_l = y_split[:, slot, 1, t * P:(t + 1) * P]
                        mm = nc.tensor.matmul(bank[b][:, :], y_h, w_split[:, slot, 0, cols],
                                              start=first, stop=False)
                        if b == 0:
                            mm.then_inc(out_step, 1)
                        nc.tensor.matmul(bank[b][:, :], y_h, w_split[:, slot, 1, cols],
                                         start=False, stop=False)
                        mm = nc.tensor.matmul(bank[b][:, :], y_l, w_split[:, slot, 0, cols],
                                              start=False, stop=last)
                        if last:
                            mm.then_inc(br_ready, 1)

                pe.wait_ge(p_free[0], (U_MA, U_MB)[layer] + 2 * MEM_HEADS + 1)
                pe.wait_ge(p_free[1], (U_MA, U_MB)[layer] + 2 * MEM_HEADS + 1)
                pe.wait_ge(s_free, (T_MA, T_MB)[layer] + MEM_HEADS * TILES + 2)
                pe.wait_ge(t_free, (X_MA, X_MB)[layer] + MEM_HEADS * TILES + 2)
                pe.wait_ge(o_free, (O_MA, O_MB)[layer] + 2 * MEM_HEADS + 2)
                with pe.Fori(0, 2) as h:
                    out_e(h, 0, 0, True, False)
                    with pe.Fori(1, NE - 1, 2) as e:
                        out_e(h, e, 1, False, False)
                        out_e(h, e + 1, 0, False, False)
                    out_e(h, NE - 1, 1, False, True)

            pe.wait_ge(row_in, 16)
            pe.wait_ge(const_in, 16)
            rows_to_columns(mem_rows, 2, 0, lambda t: None)
            pe.wait_ge(xt_lo, 4 + 2)
            with pe.Fori(0, DEPTH * MEM_HEADS) as i:
                for kv in range(2):
                    pe.wait_ge(w_lo, i * 2 + (kv + 3))
                    pe.wait_ge(p_free[kv], i + 1)
                    for k in range(KT):
                        mm = step(PB[kv][:, 0:MEM], slice(0, MEM), kv, k)
                    mm.then_inc(p_ready[kv], 1)
                pe.wait_ge(p_free[1], i + 2)
                for f in range(2):
                    pe.wait_ge(t_free, i * 2 + (f + 1))
                    nc.tensor.transpose(TB[f][:, 0:P], mem_vT[:, f * P:(f + 1) * P],
                                        ident[:, :]).then_inc(t_ready, 1)
            pe.wait_ge(row_in, 32)
            pe.wait_ge(const_in, 16 * 7)
            pe.wait_ge(t_free, X_A + 2)
            rows_to_columns(rows, TILES, 4, lambda t: None)
            pe.wait_ge(xt_lo, 4 + 16 + 2)
            with pe.Fori(0, KV) as i:
                for seg in unit_a(i):
                    run(seg)
            with pe.Fori(0, MEM_HEADS) as i:
                for seg in unit_mem(0, i):
                    run(seg)
            branch(0)
            pe.wait_ge(z_free, 8 + 8 + 6)
            rows_to_columns(rows, TILES, 20, lambda t: pe.wait_ge(ln_done, t + 1))
            pe.wait_ge(z_free, 8 + 16)
            pe.wait_ge(xt_lo, 4 + 16 + 16 + 2)
            for seg in front_b(0):
                run(seg)
            with pe.Fori(0, HEADS - 1) as i:
                for seg in back_b(i) + front_b(i + 1, combine=i):
                    run(seg)
            for seg in back_b(HEADS - 1):
                run(seg)
            for n in range(6):
                broadcast(HEADS - 1, n)
            with pe.Fori(0, MEM_HEADS) as i:
                for seg in unit_mem(1, i):
                    run(seg)
            branch(1)

        @block.scalar
        def _(act):
            act.sem_inc(p_free[0], 1)
            act.sem_inc(p_free[1], 1)
            act.sem_inc(t_free, 2)
            act.sem_inc(o_free, 2)
            for j in range(3):
                act.sem_inc(stored[j], 16)

            def split_hi(slot, full):
                act.wait_ge(w_full[slot], full)
                nc.scalar.copy(w_split[:, slot, 0, :], w_raw[:, slot, :]).then_inc(w_hi, 1)

            def columns_hi(tiles, first, column0):
                for f in range(2 * tiles):
                    t, k0 = f // 2, 4 * (f % 2)
                    act.wait_ge(xt_ready, first + f + 1)
                    nc.scalar.copy(xT[:, 0, k0:k0 + 4, t * P:(t + 1) * P],
                                   TB[f % 2][:, :].rearrange("p (k n) -> p k n", k=4)
                                   ).then_inc(xt_hi, 1)

            def values(job, f):
                rows_ = job.fills[f][0][1]
                n = len(job.fills[f]) * P
                v0 = sum(len(g) for g in job.fills[:f]) * DH
                act.wait_ge(t_ready, job.x + (f + 1))
                nc.scalar.copy(job.vbuf[0:rows_, v0:v0 + n],
                               TB[(job.x_odd + f) % 2][0:rows_, 0:n]).then_inc(t_free, 1)

            def exponential(job, t):
                n = job.tiles[t][2]
                c0 = 1 if job.sink is None else 0
                act.wait_ge(negmax, job.a + (t + 1))
                nc.scalar.activation(p_sb[t % 2][:, c0:1 + n], s_sb[t % 2][:, c0:1 + n], ACT.Exp,
                                     bias=nmax[:, job.stat, t:t + 1], scale=SCALE,
                                     accum_out=zsum[:, job.stat, t:t + 1]).then_inc(exp_done, 1)

            def transposed(job, t):
                n = len(job.fills) + t
                src, chunks = TB[(job.x_odd + n) % 2], job.tiles[t][4]
                whole = sum(keys == P for _, keys, _ in chunks)
                act.wait_ge(t_ready, job.x + (n + 1))
                cp = nc.scalar.copy(pT[t % 2][:, 0:whole * P], src[:, 0:whole * P])
                if whole < len(chunks):
                    cp = nc.scalar.copy(pT[t % 2][0:W_B, whole * P:(whole + 1) * P],
                                        src[0:W_B, whole * P:(whole + 1) * P])
                cp.then_inc(t_free, 1)

            def in_group_order(v, g, h):
                d = DIL[g]
                if d == 1:
                    return v[:, h * HALF:(h + 1) * HALF]
                return dilated(v, d)[:, h * d // 2:(h + 1) * d // 2, :]

            def group_bank(b, g):
                d = DIL[g]
                return b[:, :] if d == 1 else b[:, :].rearrange("p (r n) -> p r n", r=d // 2)

            def output_half(job, h):
                if h == 0 and job.stored is not None:
                    act.wait_ge(stored[job.out], job.stored)
                act.wait_ge(pv_done, job.a + 4 * (h + 1))
                nc.scalar.copy(in_group_order(oT[job.out], job.group, h),
                               group_bank(OB[h], job.group)).then_inc(o_free, 1)

            def project_half(seg, h):
                act.wait_ge(p_ready[h], seg.u + 1)
                if seg.gate is not None:
                    if h == 0:
                        act.wait_ge(y_done, seg.gate + 1)
                    nc.scalar.activation(gate[:, h * HALF:(h + 1) * HALF], PB[h][:, :], ACT.Tanh,
                                         scale=0.5).then_inc(tanh_done, 1)
                    return
                cp = nc.scalar.copy(half_in_order(seg.to, seg.order, h),
                                    like_order(PB[h][:, :], seg.order))
                if seg.also is not None:
                    cp = nc.scalar.copy(half_in_order(seg.also, 16, h), like_order(PB[h][:, :], 16))
                cp.then_inc(p_free[h], 1)

            def log_denominators(i):
                act.wait_ge(exp_done, i * 24 + (T_B + 24))
                nc.scalar.activation(lnz[:, :, :], zsum[:, :, :], ACT.Ln).then_inc(lnz_done, 1)

            def broadcast(i, n):
                g, h = n // 2, n % 2
                act.wait_ge(bc_done, i * 6 + (n + 3))
                nc.scalar.copy(in_group_order(lT[g], g, h), group_bank(OB[h], g)
                               ).then_inc(o_free, 1)

            def weights(i):
                for g in range(3):
                    act.wait_ge(comb, i * COMB_STEPS + (3 + g))
                    nc.scalar.activation(lT[g], lT[g], ACT.Exp).then_inc(comb_act, 1)
                act.wait_ge(comb, i * COMB_STEPS + 7)
                nc.scalar.activation(top, top, ACT.Ln).then_inc(comb_act, 1)
                act.wait_ge(comb_act, i * 5 + 4)
                nc.scalar.activation(top, top, ACT.Exp, scale=-1.0).then_inc(comb_act, 1)

            def run(seg):
                split_hi((seg.slot + 1) % 2, seg.next_full)
                for s in range(STEPS):
                    fill, t_s, t_t, t_o = riding(seg.job, s)
                    if fill is not None:
                        values(seg.job, fill)
                    if seg.combine is not None:
                        i, part = seg.combine
                        if part == 0 and s == 0:
                            log_denominators(i)
                        if part == 0 and 6 <= s < 12:
                            broadcast(i, s - 6)
                        if part == 1 and s == 9:
                            weights(i)
                    if s == KT:
                        project_half(seg, 0)
                    if t_t is not None:
                        transposed(seg.job, t_t)
                    if t_s is not None:
                        exponential(seg.job, t_s)
                    if seg.job is not None and s == LAG_PV + 4:
                        output_half(seg.job, 0)
                project_half(seg, 1)
                if seg.job is not None:
                    output_half(seg.job, 1)

            def branch(layer, more):
                c0, y0 = (C_OA, C_OB)[layer], layer * 2 * NE

                def y_tile(n, slot, full):
                    act.wait_ge(y_full[slot], full)
                    nc.scalar.copy(y_split[:, slot, 0, :], y_raw[:, slot, :]).then_inc(y_hi, 1)

                def next_w(n, slot, full):
                    act.wait_ge(out_step, n + (y0 + 1))
                    act.wait_ge(w_full[slot], full)
                    nc.scalar.copy(w_split[:, slot, 0, :], w_raw[:, slot, :]).then_inc(w_hi, 1)

                f_w, f_y = 16 * (c0 // 2), 16 * (y0 // 2)
                y_tile(0, 0, f_y + 16)
                with act.Fori(0, 2 * NE - 2, 2) as n:
                    next_w(n, 1, n * 8 + (f_w + 16))
                    y_tile(n + 1, 1, n * 8 + (f_y + 16))
                    next_w(n + 1, 0, n * 8 + (f_w + 32))
                    y_tile(n + 2, 0, n * 8 + (f_y + 32))
                n = 2 * NE - 2
                next_w(n, 1, n * 8 + (f_w + 16))
                y_tile(n + 1, 1, n * 8 + (f_y + 16))
                if more:
                    next_w(n + 1, 0, n * 8 + (f_w + 32))
                act.wait_ge(br_ready, 16 * (layer + 1))

            split_hi(0, 16)
            columns_hi(2, 0, 0)
            with act.Fori(0, DEPTH * MEM_HEADS) as i:
                for kv in range(2):
                    if kv == 0:
                        split_hi(1, i * 16 + 16)
                    else:
                        split_hi(0, i * 16 + 32)
                    act.wait_ge(p_ready[kv], i + 1)
                    if kv == 0:
                        nc.scalar.copy(mem_k[:, bass.ds(i, 1), :].rearrange("p a n -> p (a n)"),
                                       PB[0][:, 0:MEM]).then_inc(p_free[0], 1)
                    else:
                        nc.scalar.copy(mem_vT, PB[1][:, 0:MEM]).then_inc(p_free[1], 1)
                for f in range(2):
                    act.wait_ge(t_ready, i * 2 + (f + 1))
                    nc.scalar.copy(mem_v[:, bass.ds(i, 1), f * P:(f + 1) * P]
                                   .rearrange("p a n -> p (a n)"), TB[f][:, 0:P]
                                   ).then_inc(t_free, 1)
            columns_hi(TILES, 4, 0)
            with act.Fori(0, KV) as i:
                for seg in unit_a(i):
                    run(seg)
            with act.Fori(0, MEM_HEADS) as i:
                for seg in unit_mem(0, i):
                    run(seg)
            branch(0, True)
            columns_hi(TILES, 20, 0)
            act.wait_ge(rows_out, 16 * TILES)
            for seg in front_b(0):
                run(seg)
            with act.Fori(0, HEADS - 1) as i:
                for seg in back_b(i) + front_b(i + 1, combine=i):
                    run(seg)
            for seg in back_b(HEADS - 1):
                run(seg)
            log_denominators(HEADS - 1)
            for n in range(6):
                broadcast(HEADS - 1, n)
            weights(HEADS - 1)
            with act.Fori(0, MEM_HEADS) as i:
                for seg in unit_mem(1, i):
                    run(seg)
            branch(1, False)

        @block.vector
        def _(dve):
            dve.sem_inc(w_lo, 2)
            dve.sem_inc(xt_lo, 2)
            dve.sem_inc(s_free, 2)
            dve.sem_inc(y_done, 1)
            dve.sem_inc(y_lo, 2)
            dve.sem_inc(z_free, 8)
            dve.sem_inc(rope_done, 1)

            def split_lo(slot, c):
                dve.wait_ge(w_hi, c + 1)
                nc.vector.tensor_tensor(w_split[:, slot, 1, :], w_raw[:, slot, :],
                                        w_split[:, slot, 0, :].bitcast(F32),
                                        ALU.subtract).then_inc(w_lo, 1)

            def columns_lo(tiles, first):
                for f in range(2 * tiles):
                    t, k0 = f // 2, 4 * (f % 2)
                    dve.wait_ge(xt_hi, first + f + 1)
                    nc.vector.tensor_tensor(xT[:, 1, k0:k0 + 4, t * P:(t + 1) * P],
                                            TB[f % 2][:, :].rearrange("p (k n) -> p k n", k=4),
                                            xT[:, 0, k0:k0 + 4, t * P:(t + 1) * P].bitcast(F32),
                                            ALU.subtract).then_inc(xt_lo, 1)

            swap = [(i + ROPE // 2) % ROPE for i in range(ROPE)]

            def rotate(seg, h):
                r = seg.rope + h
                v = half_in_order(seg.to[0:ROPE, :], seg.order, h)
                cos_h = like_order(cosb[:, h * HALF:(h + 1) * HALF], seg.order)
                sin_h = like_order(sinb[:, h * HALF:(h + 1) * HALF], seg.order)
                a, b = rope_a[0:ROPE, :], rope_b[0:ROPE, :]
                if seg.order > 1:
                    a = a.rearrange("p (r n) -> p r n", r=seg.order)
                    b = b.rearrange("p (r n) -> p r n", r=seg.order)
                dve.wait_ge(rope_done, r + 1)
                dve.wait_ge(p_free[h], seg.u + 2)
                nc.vector.tensor_tensor(a, v, cos_h, ALU.mult)
                nc.vector.stream_shuffle(b, v, swap).then_inc(rope_turned, 1)
                dve.wait_ge(rope_turned, r + 1)
                nc.vector.tensor_tensor(b, b, sin_h, ALU.mult).then_inc(rope_sine, 1)
                dve.wait_ge(rope_sine, r + 1)
                nc.vector.tensor_tensor(v, a, b, ALU.add).then_inc(rope_done, 1)

            def project_half(seg, h):
                if seg.rope is not None:
                    rotate(seg, h)
                if seg.gate is not None:
                    cols = slice(h * HALF, (h + 1) * HALF)
                    dve.wait_ge(tanh_done, seg.gate * 2 + (h + 1))
                    nc.vector.scalar_tensor_tensor(out=gate[:, cols], in0=gate[:, cols], scalar=1.0,
                                                   in1=PB[h][:, :], op0=ALU.add, op1=ALU.mult
                                                   ).then_inc(p_free[h], 1)

            def mask(job, t):
                n, m = job.tiles[t][2], job.tiles[t][3]
                dve.wait_ge(s_ready, job.a + (t + 1))
                dve.sem_inc(held, 1)
                src = SB[t % 2][:, 0:n]
                if m.ndim != src.ndim:
                    raise AssertionError
                nc.vector.tensor_tensor_reduce(s_sb[t % 2][:, 1:1 + n], src, m, 1.0, -3.0e38,
                                               ALU.add, ALU.max, rmax[:, job.stat, t:t + 1]
                                               ).then_inc(s_free, 1)

            def bias(job, t):
                dve.wait_ge(s_free, job.a + (t + 3))
                r, n = rmax[:, job.stat, t:t + 1], nmax[:, job.stat, t:t + 1]
                if job.sink is None:
                    ts = nc.vector.tensor_scalar(n, r, -SCALE, None, ALU.mult)
                else:
                    ts = nc.vector.tensor_scalar(n, r, -SCALE, sinks_neg[:, bass.ds(job.sink, 1)],
                                                 ALU.mult, ALU.min)
                ts.then_inc(negmax, 1)

            def invert(job, t):
                dve.wait_ge(exp_done, job.a + (t + 1))
                nc.vector.reciprocal(zinv[:, job.stat, t:t + 1], zsum[:, job.stat, t:t + 1]
                                     ).then_inc(zinv_done, 1)

            def normalise(job, t):
                n = job.tiles[t][2]
                dve.wait_ge(zinv_done, job.a + (t + 1))
                nc.vector.tensor_scalar(p_sb[t % 2][:, 1:1 + n], p_sb[t % 2][:, 1:1 + n],
                                        zinv[:, job.stat, t:t + 1], None, ALU.mult
                                        ).then_inc(p_done, 1)

            def log_sum_exp(i):
                dve.wait_ge(lnz_done, i + 1)
                nc.vector.tensor_tensor(lse[:, :, :], lnz[:, :, :], nmax[:, :, :],
                                        ALU.subtract).then_inc(lse_done, 1)

            def combine_weights(i):
                n = i * COMB_STEPS
                dve.wait_ge(o_free, i * 12 + (O_B + 14))
                nc.vector.tensor_tensor(top, lT[0], lT[1], ALU.max).then_inc(comb, 1)
                dve.wait_ge(comb, n + 1)
                nc.vector.tensor_tensor(top, top, lT[2], ALU.max).then_inc(comb, 1)
                dve.wait_ge(comb, n + 2)
                for g in range(3):
                    nc.vector.tensor_tensor(lT[g], lT[g], top, ALU.subtract).then_inc(comb, 1)
                dve.wait_ge(comb_act, i * 5 + 2)
                dve.wait_ge(comb, n + 5)
                nc.vector.tensor_tensor(top, lT[0], lT[1], ALU.add).then_inc(comb, 1)
                dve.wait_ge(comb_act, i * 5 + 3)
                dve.wait_ge(comb, n + 6)
                nc.vector.tensor_tensor(top, top, lT[2], ALU.add).then_inc(comb, 1)

            def combine_outputs(i, y):
                n = i * COMB_STEPS
                dve.wait_ge(comb_act, i * 5 + 3)
                for g in range(3):
                    nc.vector.tensor_tensor(oT[g], oT[g], lT[g], ALU.mult).then_inc(comb, 1)
                dve.wait_ge(comb, n + 9)
                nc.vector.tensor_tensor(oT[0], oT[0], oT[1], ALU.add).then_inc(comb, 1)
                dve.wait_ge(comb, n + 11)
                nc.vector.tensor_tensor(oT[0], oT[0], oT[2], ALU.add).then_inc(comb, 1)
                dve.wait_ge(comb, n + 12)
                nc.vector.scalar_tensor_tensor(out=oT[0], in0=oT[0], scalar=0.5, in1=gate,
                                               op0=ALU.mult, op1=ALU.mult).then_inc(comb, 1)
                dve.wait_ge(comb_act, i * 5 + 5)
                dve.wait_ge(comb, n + 13)
                nc.vector.tensor_tensor(oT[0], oT[0], top, ALU.mult).then_inc(y_done, 1)

            def run(seg):
                split_lo((seg.slot + 1) % 2, seg.c + 1)
                job = seg.job
                for s in range(STEPS):
                    if seg.combine is not None:
                        i, part = seg.combine
                        if part == 0 and s == 0:
                            log_sum_exp(i)
                        if part == 1 and s == 0:
                            combine_weights(i)
                        if part == 2 and s == 0:
                            combine_outputs(i, G_B + i)
                    _, t, _, _ = riding(job, s)
                    if job is not None and job.sink is not None and s == LEAD - 1:
                        for b in range(2):
                            nc.vector.tensor_copy(s_sb[b][:, 0:1],
                                                  sinks_raw[:, bass.ds(job.sink, 1)])
                    if job is not None and LEAD <= s <= LEAD + TILES:
                        if t is not None:
                            mask(job, t)
                        if s > LEAD:
                            invert(job, s - LEAD - 1)
                        if t is not None:
                            bias(job, t)
                        if s > LEAD:
                            normalise(job, s - LEAD - 1)
                    if s == KT + 1:
                        project_half(seg, 0)
                project_half(seg, 1)
                if seg.y:
                    dve.wait_ge(o_free, job.o + 4)
                    dve.wait_ge(p_free[1], seg.u + 2)
                    nc.vector.scalar_tensor_tensor(out=oT[job.out], in0=oT[job.out], scalar=0.5,
                                                   in1=gate, op0=ALU.mult, op1=ALU.mult
                                                   ).then_inc(y_done, 1)

            def branch(layer, more):
                c0, y0 = (C_OA, C_OB)[layer], layer * 2 * NE

                def y_tile(n, slot):
                    dve.wait_ge(y_hi, n + (y0 + 1))
                    nc.vector.tensor_tensor(y_split[:, slot, 1, :], y_raw[:, slot, :],
                                            y_split[:, slot, 0, :].bitcast(F32),
                                            ALU.subtract).then_inc(y_lo, 1)

                def step(n, slot):
                    split_lo(slot, n + (c0 + 1))
                    y_tile(n + 1, slot)

                def add(h):
                    dve.wait_ge(res_in, 16 * (2 * layer + h + 1))
                    for b in range(8):
                        t, cols = 4 * h + b // 2, slice((b % 2) * HALF, (b % 2 + 1) * HALF)
                        dve.wait_ge(br_ready, layer * 16 + h * 8 + b + 1)
                        nc.vector.scalar_tensor_tensor(out=rows[:, t, cols], in0=rows[:, t, cols],
                                                       scalar=ALPHA, in1=bank[b][:, :],
                                                       op0=ALU.mult, op1=ALU.add
                                                       ).then_inc(z_free, 1)

                def statistics(t):
                    n = layer * TILES + t
                    dve.wait_ge(z_free, 8 + 2 * n + 2)
                    for k in range(2):
                        nc.vector.bn_stats(stats[:, t, k, :], rows[:, t, k * HALF:(k + 1) * HALF]
                                           ).then_inc(ln_stat, 1)
                    dve.wait_ge(ln_stat, 2 * n + 2)
                    nc.vector.bn_aggr(mv[:, t, :], stats[:, t, :, :].rearrange("p a b -> p (a b)")
                                      ).then_inc(ln_aggr, 1)

                def norm(t):
                    n = layer * TILES + t
                    dve.wait_ge(ln_rstd, n + 1)
                    nc.vector.tensor_scalar(rows[:, t, :], rows[:, t, :], mv[:, t, 0:1],
                                            rstd[:, t, 1:2], ALU.subtract, ALU.mult
                                            ).then_inc(ln_step, 1)
                    dve.wait_ge(ln_step, 2 * n + 1)
                    dve.wait_ge(gb_in, 32 * (layer + 1))
                    nc.vector.tensor_tensor(rows[:, t, :], rows[:, t, :], g_row,
                                            ALU.mult).then_inc(ln_step, 1)
                    dve.wait_ge(ln_step, 2 * n + 2)
                    nc.vector.tensor_tensor(rows[:, t, :], rows[:, t, :], b_row,
                                            ALU.add).then_inc(ln_done, 1)

                y_tile(0, 0)
                with dve.Fori(0, NE - 2, 2) as n:
                    step(n, 1)
                    step(n + 1, 0)
                step(NE - 2, 1)
                step(NE - 1, 0)
                add(0)
                for n in range(8):
                    step(NE + n, (n + 1) % 2)
                    if n < 4:
                        statistics(n)
                    else:
                        norm(n - 4)
                with dve.Fori(NE + 8, 2 * NE - 2, 2) as n:
                    step(n, 1)
                    step(n + 1, 0)
                step(2 * NE - 2, 1)
                if more:
                    split_lo(0, c0 + 2 * NE)
                add(1)
                for t in range(4, TILES + 1):
                    if t < TILES:
                        statistics(t)
                    if t > 4:
                        norm(t - 1)

            split_lo(0, 0)
            columns_lo(2, 0)
            with dve.Fori(0, DEPTH * MEM_HEADS) as i:
                split_lo(1, i * 2 + 1)
                split_lo(0, i * 2 + 2)
            columns_lo(TILES, 4)
            dve.wait_ge(const_in, 16 * 7)
            nc.vector.tensor_scalar(sinks_raw[:, :], sinks[:, :], 1.0 / SCALE, None,
                                    ALU.mult).then_inc(sink_consts, 1)
            nc.vector.tensor_scalar(sinks_neg[:, :], sinks[:, :], -1.0, None,
                                    ALU.mult).then_inc(sink_consts, 1)
            dve.wait_ge(sink_consts, 2)
            with dve.Fori(0, KV) as i:
                for seg in unit_a(i):
                    run(seg)
            with dve.Fori(0, MEM_HEADS) as i:
                for seg in unit_mem(0, i):
                    run(seg)
            branch(0, True)
            columns_lo(TILES, 20)
            for seg in front_b(0):
                run(seg)
            with dve.Fori(0, HEADS - 1) as i:
                for seg in back_b(i) + front_b(i + 1, combine=i):
                    run(seg)
            for seg in back_b(HEADS - 1):
                run(seg)
            log_sum_exp(HEADS - 1)
            combine_weights(HEADS - 1)
            combine_outputs(HEADS - 1, G_B + HEADS - 1)
            with dve.Fori(0, MEM_HEADS) as i:
                for seg in unit_mem(1, i):
                    run(seg)
            branch(1, False)


def shape_constants():
    half = ROPE // 2
    inv = (np.float64(THETA) ** (-np.arange(half, dtype=np.float32) / np.float32(half))
           ).astype(np.float32)
    ang = (np.arange(L, dtype=np.float32)[None, :] * inv[:, None]).astype(np.float32)
    cos, sin = np.cos(ang.astype(np.float64)), np.sin(ang.astype(np.float64))
    q = np.arange(P)[:, None]
    ka, kb, k2 = np.arange(3 * P)[None, :], np.arange(2 * P)[None, :], np.arange(P)[None, :]

    def masked(valid):
        return np.where(valid, 0.0, NEG).astype(np.float32)

    return {
        "rope_cos": np.concatenate([cos, cos]).astype(np.float32),
        "rope_sin": np.concatenate([-sin, sin]).astype(np.float32),
        "mask_a": masked(np.abs(ka - P - q) <= W_A),
        "mask_b": masked(np.abs(kb - W_B - q) <= W_B),
        "mask_b2": masked(q // W_B == k2 // W_B),
        "identity": np.eye(P, dtype=np.float32),
    }


_INS = ["x", "mem", "w_in_a", "sink_a", "w_in_b", "w_mkv", "w_out", "ln_g", "ln_b"]


def kernel(**inputs):
    import concourse.bacc as _bacc
    from concourse.bass_utils import run_bass_kernel_spmd as _run

    nc = _bacc.Bacc("TRN2", target_bir_lowering=False, num_devices=1,
                    dynamic_dma_scratch_size=1024)
    arrays, args = {}, []
    given = {name: np.ascontiguousarray(inputs[name]) for name in _INS}
    for name, a in {**given, **shape_constants()}.items():
        arrays[f"in_{name}"] = a
        args.append(nc.dram_tensor(f"in_{name}", a.shape, mybir.dt.from_np(a.dtype),
                                   kind="ExternalInput").ap())
    args.append(nc.dram_tensor("out_0", (1, L, D), F32, kind="ExternalOutput").ap())
    encoder(nc, *args)
    r = _run(nc, [arrays], core_ids=[0])
    return r.results[0]["out_0"]
```

```python
from contextlib import ExitStack

import numpy as np

import concourse.bass as bass
from concourse import mybir

F32 = mybir.dt.float32
F32R = mybir.dt.float32r
ALU = mybir.AluOpType
ACT = mybir.ActivationFunctionType

P = 128
D = 1024
L = 1024
MEM = 256
DH = 128
HEADS = 12
MEM_HEADS = 4
KV = 4
GROUP = HEADS // KV
D_INNER = 2 * D
DEPTH = 2
ALPHA = (2 * DEPTH) ** 0.25
LN_EPS = 1e-5
ROPE = DH // 4
THETA = 500000.0
SCALE = DH ** -0.5
NEG = -1e30
KT = D // P
HALF = 512
TILES = L // P
NE = D_INNER // P
W_A = 128
BLOCKS = 16
W_B = 64
DIL = (1, 4, 16)

A_Q, A_K = 0, HEADS * DH
A_V = A_K + KV * DH
A_MQ = A_V + KV * DH
A_G = A_MQ + MEM_HEADS * DH
B_Q, B_K = 0, 3 * HEADS * DH
B_V = B_K + HEADS * DH
B_MQ = B_V + HEADS * DH
B_G = B_MQ + MEM_HEADS * DH

C_A = 2 * DEPTH * MEM_HEADS
C_MA = C_A + 8 * KV
C_OA = C_MA + 2 * MEM_HEADS
C_B = C_OA + 2 * NE
C_MB = C_B + 6 * HEADS
C_OB = C_MB + 2 * MEM_HEADS
C_END = C_OB + 2 * NE
U_A = DEPTH * MEM_HEADS
U_MA = U_A + 8 * KV
U_B = U_MA + 2 * MEM_HEADS
U_MB = U_B + 6 * HEADS
U_END = U_MB + 2 * MEM_HEADS
T_A = 0
T_MA = T_A + GROUP * TILES * KV
T_B = T_MA + TILES * MEM_HEADS
T_MB = T_B + 3 * TILES * HEADS
T_END = T_MB + TILES * MEM_HEADS
X_A_PER = 2 + GROUP * TILES
X_B_G = (0, 3 + TILES, 6 + 2 * TILES)
X_B_PER = 8 + 3 * TILES
X_A = 2 * DEPTH * MEM_HEADS
X_MA = X_A + X_A_PER * KV
X_B = X_MA + TILES * MEM_HEADS
X_MB = X_B + X_B_PER * HEADS
X_END = X_MB + TILES * MEM_HEADS
O_A = 0
O_MA = O_A + 2 * GROUP * KV
O_B = O_MA + 2 * MEM_HEADS
O_MB = O_B + 8 * HEADS
O_END = O_MB + 2 * MEM_HEADS
R_A = 0
R_B = R_A + 8 * KV
S_A = 0
S_MA = S_A + 2 * (GROUP + 1) * KV
S_MB = S_MA + 3 * MEM_HEADS
G_A = 0
G_MA = G_A + GROUP * KV
G_B = G_MA + MEM_HEADS
G_MB = G_B + HEADS


MEM_B_ORDER = (("q", 0), ("q", 1), ("q", 2), ("g", 0), ("g", 1), ("g", 2), ("q", 3), ("g", 3))


class Job:

    def __init__(self, a, x, x_odd, o, stat, tiles, vbuf, fills=(), sink=None, queries=None,
                 v_use=None, split=None, copied=None, combined=None, group=0, out=0, stored=None):
        self.a, self.x, self.x_odd, self.o, self.stat = a, x, x_odd, o, stat
        self.tiles, self.vbuf, self.fills, self.sink = tiles, vbuf, fills, sink
        self.queries, self.v_use, self.split, self.copied = queries, v_use, split, copied
        self.combined = combined
        self.group, self.out, self.stored = group, out, stored


class Part:

    def __init__(self, slot, n, dst, first, size, src, rope=None, u=None, bank=0):
        self.slot, self.n, self.dst, self.first, self.size = slot, n, dst, first, size
        self.src, self.rope, self.u, self.bank = src, rope, u, bank


class Segment:

    def __init__(self, c, slot, next_full, u, to=None, order=1, also=None, rope=None, gate=None,
                 job=None, combine=None, y=False, parts=()):
        self.c, self.slot, self.next_full, self.u = c, slot, next_full, u
        self.to, self.order, self.also, self.rope, self.gate = to, order, also, rope, gate
        self.job, self.combine, self.y = job, combine, y
        self.parts = parts
        self.split = 0 if combine is not None and combine[1] == 2 else 12 if job is None else 11


STEPS = 2 * KT
LEAD, LAG_T, LAG_PV = 3, 6, 8
BANKS_X = 4
COMB_STEPS = 16


def riding(job, s):
    if job is None:
        return None, None, None, None

    def due(lag):
        return s - lag if 0 <= s - lag < TILES else None

    return (s - 1 if 1 <= s <= len(job.fills) else None), due(LEAD), due(LAG_T), due(LAG_PV)


def dilated(v, d):
    return v.rearrange("p (n r) -> p r n", r=d)


def encoder(nc, x, mem, w_in_a, sink_a, w_in_b, w_mkv, w_out, ln_g, ln_b,
            rope_cos, rope_sin, mask_a, mask_b, mask_b2, identity, out):
    ctx = ExitStack()
    with ctx:
        def sb(name, shape, dt=F32):
            return ctx.enter_context(nc.sbuf_tensor(name, shape, dt))

        def sem(name):
            return ctx.enter_context(nc.semaphore(name))

        xT = sb("xT", [P, 2, KT, L], F32R)
        w_split = sb("w_split", [P, 2, 2, D], F32R)
        w_raw = sb("w_raw", [P, 2, D])
        y_split = sb("y_split", [P, 2, 2, HALF], F32R)
        mem_k = sb("mem_k", [P, DEPTH * MEM_HEADS, MEM])
        mem_v = sb("mem_v", [P, DEPTH * MEM_HEADS, MEM])
        head_mv = sb("head_mv", [P, MEM])
        qk_split = sb("qk_split", [P, 2, 2, L], F32R)
        cosb = sb("cosb", [ROPE, L])
        sinb = sb("sinb", [ROPE, L])
        m_a = sb("m_a", [P, 3 * W_A])
        m_b = sb("m_b", [P, 2 * P])
        m_b2 = sb("m_b2", [P, P])
        m_0 = sb("m_0", [P, MEM])
        ident = sb("ident", [P, P])
        sinks = sb("sinks", [P, HEADS])
        sinks_raw = sb("sinks_raw", [P, HEADS])
        sinks_neg = sb("sinks_neg", [P, HEADS])
        rmax = sb("rmax", [P, 3, TILES])
        soft = sb("soft", [P, 2, 3, TILES])
        nmax = soft[:, 0]
        zsum = soft[:, 1]
        zinv = sb("zinv", [P, 3, TILES])
        soft_rows = sb("soft_rows", [3 * TILES, 2, P])
        soft_in = sb("soft_in", [BLOCKS, 2, 3, L // BLOCKS])
        soft_tok = sb("soft_tok", [BLOCKS, 2, 3, L // BLOCKS])
        weight = sb("weight", [BLOCKS, 3, L // BLOCKS])
        w_sum = sb("w_sum", [BLOCKS, L // BLOCKS])
        y_raw = sb("y_raw", [P, 2, HALF])
        stats = sb("stats", [P, TILES, 2, 6])
        mv = sb("mv", [P, TILES, 2])
        rstd = sb("rstd", [P, TILES, 2])
        power = sb("power", [P, 2])
        WORDS = 16 * L + 256
        work = sb("work", [P, WORDS])
        at = [0]

        def take(n):
            at[0] += n
            return work[:, at[0] - n:at[0]]

        kT = take(L)
        qT = [take(L), take(L)]
        vT = take(L)
        vT16 = take(L)
        wT_all = take(3 * L)
        wT = [wT_all[:, g * L:(g + 1) * L] for g in range(3)]
        vbuf = [wT_all[:, 0:12 * DH], wT_all[:, 12 * DH:24 * DH]]
        s_sb = [take(388) for _ in range(3)]
        p_sb = [take(388) for _ in range(3)]
        pT = [take(3 * P), take(3 * P)]
        oT = [take(L) for _ in range(3)]
        gate = take(L)
        rope_a = take(HALF)
        rope_b = take(HALF)
        assert at[0] <= WORDS
        rows = work[:, 0:TILES * D].rearrange("p (t d) -> p t d", t=TILES)
        mem_rows = work[:, TILES * D:(TILES + 2) * D].rearrange("p (t d) -> p t d", t=2)
        mem_vT = gate[:, 0:MEM]
        g_row = work[:, 11 * D:12 * D]
        b_row = work[:, 12 * D:13 * D]

        bank = [ctx.enter_context(nc.psum_tensor(f"bank{i}", [P, HALF], F32)) for i in range(8)]
        PB, SB, TB, OB = bank[0:2], bank[2:4], bank[4:6], bank[6:8]
        XB = bank[4:8]

        y_dram = nc.dram_tensor("y_scratch", [NE, P, L], F32, kind="Internal").ap()
        soft_dram = nc.dram_tensor("soft_scratch", [2, 3 * TILES, P], F32, kind="Internal").ap()
        weight_dram = nc.dram_tensor("weight_scratch", [3, L], F32, kind="Internal").ap()
        x1_dram = nc.dram_tensor("x1_scratch", [TILES, P, D], F32, kind="Internal").ap()

        const_in = sem("const_in")
        mem_in = [sem("mem_in0"), sem("mem_in1")]
        row_in = sem("row_in")
        consts = sem("consts")
        sink_consts = sem("sink_consts")
        w_full = [sem("w_full0"), sem("w_full1")]
        w_hi = sem("w_hi")
        w_lo = sem("w_lo")
        p_ready = [sem("p_ready0"), sem("p_ready1")]
        p_free = [sem("p_free0"), sem("p_free1")]
        xt_ready = sem("xt_ready")
        xt_hi = sem("xt_hi")
        xt_lo = sem("xt_lo")
        rope_turned = sem("rope_turned")
        rope_sine = sem("rope_sine")
        rope_done = sem("rope_done")
        t_ready = sem("t_ready")
        t_free = sem("t_free")
        s_ready = sem("s_ready")
        s_free = sem("s_free")
        negmax = sem("negmax")
        exp_done = sem("exp_done")
        zinv_done = sem("zinv_done")
        p_done = sem("p_done")
        pv_done = sem("pv_done")
        o_free = sem("o_free")
        tanh_done = sem("tanh_done")
        y_done = sem("y_done")
        stored = [sem(f"stored{j}") for j in range(3)]
        part_hi = sem("part_hi")
        part_lo = sem("part_lo")
        memkv = sem("memkv")
        soft_t = sem("soft_t")
        soft_out = sem("soft_out")
        soft_back = sem("soft_back")
        comb = sem("comb")
        comb_exp = sem("comb_exp")
        weight_out = sem("weight_out")
        weight_in = sem("weight_in")
        y_full = [sem("y_full0"), sem("y_full1")]
        y_hi = sem("y_hi")
        y_lo = sem("y_lo")
        out_step = sem("out_step")
        br_ready = sem("br_ready")
        z_free = sem("z_free")
        res_in = sem("res_in")
        gb_in = sem("gb_in")
        ln_stat = sem("ln_stat")
        ln_aggr = sem("ln_aggr")
        ln_eps = sem("ln_eps")
        ln_rstd = sem("ln_rstd")
        ln_step = sem("ln_step")
        ln_done = sem("ln_done")
        rows_out = sem("rows_out")
        held = sem("held")

        def a_tiles():
            tiles = []
            for t in range(TILES):
                lo, hi = max(t - 1, 0), min(t + 2, TILES)
                m0 = (lo - t + 1) * P
                tiles.append((qT[0][:, t * P:(t + 1) * P], kT[:, lo * P:hi * P], (hi - lo) * P,
                              m_a[:, m0:m0 + (hi - lo) * P],
                              [(b, P, (b - lo) * P) for b in range(lo, hi)], (t * P, lo * P)))
            return tiles

        def mem_tiles(q):
            return [(q[:, t * P:(t + 1) * P], None, MEM, m_0[:, :],
                     [(0, P, 0), (1, P, P)], (t * P, 0)) for t in range(TILES)]

        def b_tiles(g):
            q = qT[g % 2]
            tiles = []
            if g == 0:
                for t in range(TILES):
                    lo, hi = max(t * P - W_B, 0), min((t + 1) * P + W_B, L)
                    m0 = lo - (t * P - W_B)
                    chunks = [(t - 1, P, 0)] if t > 0 else []
                    chunks += [(t, P, P if t else W_B)] if t < TILES - 1 else []
                    chunks += [(7, W_B, 0)] if t == 0 else []
                    chunks += [(8, W_B, P)] if t == TILES - 1 else []
                    tiles.append((q[:, t * P:(t + 1) * P], kT[:, lo:hi], hi - lo,
                                  m_b[:, m0:m0 + hi - lo], chunks, None))
            elif g == 1:
                qd, kd = dilated(q, 4), dilated(kT, 4)
                for r in range(4):
                    tiles.append((qd[:, r, 0:P], kd[:, r, 0:P + W_B], P + W_B,
                                  m_b[:, W_B:2 * P], [(2 * r, P, 0), (2 * r + 1, W_B, P)], None))
                    tiles.append((qd[:, r, P:2 * P], kd[:, r, W_B:2 * P], P + W_B,
                                  m_b[:, 0:P + W_B], [(2 * r + 1, P, W_B), (8 + r, W_B, 0)],
                                  None))
            else:
                kd = dilated(kT, 16)
                for j in range(TILES):
                    tiles.append((q[:, j * P:(j + 1) * P], kd[:, 2 * j:2 * j + 2, :], P,
                                  m_b2[:, :], [(j, P, 0)], None))
            return tiles

        def whole_tiles(v, first, last):
            return [(v[:, t * P:(t + 1) * P], P) for t in range(first, last)]

        def b_fills(g):
            if g == 0:
                s = [(vT[:, W_B + i * P:W_B + (i + 1) * P], P) for i in range(TILES - 1)]
                return [s[0:4], s[4:7], [(vT[:, 0:W_B], W_B), (vT[:, L - W_B:L], W_B)]]
            if g == 1:
                d = dilated(vT, 4)
                s = [(d[:, r, n * P:(n + 1) * P], P) for r in range(4) for n in range(2)]
                return [s[0:4], s[4:8], [(d[:, r, W_B:P], W_B) for r in range(4)]]
            return [whole_tiles(vT16, 0, 4), whole_tiles(vT16, 4, 8)]

        def half_in_order(v, d, h):
            if d == 1:
                return v[:, h * HALF:(h + 1) * HALF]
            n = HALF // d
            return v.rearrange("p (r n) -> p r n", r=d)[:, :, h * n:(h + 1) * n]

        def like_order(v, d):
            return v if d == 1 else dilated(v, d)

        def half(slot, n, dst, h, src, **kw):
            return Part(slot, n, dst, h * HALF, HALF, src[:, h * HALF:(h + 1) * HALF], bank=h, **kw)

        def unit_a(i):
            def seg(k, **kw):
                return Segment(C_A + k + i * 8, k % 2, 16 * ((C_A + k + 1) // 2 + 1) + i * 64,
                               U_A + k + i * 8, **kw)

            r, n = R_A + i * 8, S_A + i * 8
            segs = [seg(0, to=kT, rope=r, parts=[half(13, n, 1, 0, kT, rope=r + 2)]),
                    seg(1, to=vT, parts=[half(3, n + 1, 1, 1, kT, rope=r + 3)])]
            for j in range(GROUP):
                segs.append(seg(2 + 2 * j, to=qT[0], rope=r + 2 + 2 * j, parts=[
                    half(13, n + 2 + 2 * j, 0, 0, qT[0], rope=r + 4 + 2 * j)]))
                fills = [whole_tiles(vT, 0, 4), whole_tiles(vT, 4, 8)] if j == 0 else []
                x0 = 0 if j == 0 else 2 + j * TILES
                job = Job(T_A + j * TILES + i * 24, X_A + x0 + i * X_A_PER, x0 % 2,
                          O_A + 2 * j + i * 6, j, a_tiles(), vbuf[0], fills, sink=i * GROUP + j,
                          queries=r + 5 + 2 * j, split=n + 3 + 2 * j, v_use=U_A + 3 + i * 8,
                          out=j, stored=16 + i * 16)
                segs.append(seg(3 + 2 * j, job=job, gate=G_A + j + i * GROUP, y=True, parts=[
                    half(3, n + 3 + 2 * j, 0, 1, qT[0], rope=r + 5 + 2 * j)]))
            return segs

        def mem_job(layer, i, q, values, copied=None):
            before = KV if layer == 0 else KV + MEM_HEADS + HEADS
            return Job((T_MA, T_MB)[layer] + i * TILES, (X_MA, X_MB)[layer] + i * TILES, 0,
                       (O_MA, O_MB)[layer] + i * 2, 0, mem_tiles(q), values,
                       split=(S_MA, S_MB)[layer] + 2 + i * 3, copied=copied,
                       stored=16 + 16 * before + i * 16)

        def mem_parts(layer, i, slot, q, u):
            n, head = (S_MA, S_MB)[layer] + i * 3, i + layer * MEM_HEADS
            keys = mem_k[:, bass.ds(head, 1), :].rearrange("p a n -> p (a n)")
            return ([Part(slot, n, 1, 0, MEM, keys), half(slot, n + 1, 0, 0, q, u=u)],
                    [half(1, n + 2, 0, 1, q, u=u)])

        def unit_mem(i):
            job = mem_job(0, i, qT[0], head_mv, copied=i + 1)
            first, second = mem_parts(0, i, 12, qT[0], U_MA + 2 + i * 2)
            return [Segment(C_MA + i * 2, 0, 16 * ((C_MA + 1) // 2 + 1) + i * 16, U_MA + i * 2,
                            to=qT[0], parts=first),
                    Segment(C_MA + 1 + i * 2, 1, 16 * ((C_MA + 2) // 2 + 1) + i * 16,
                            U_MA + 1 + i * 2, job=job, gate=G_MA + i, y=True, parts=second)]

        def memory_b():
            queries = [qT[0], qT[1], kT, qT[0]]
            place, segs = {}, []
            for n, (what, i) in enumerate(MEM_B_ORDER):
                if what == "q":
                    place[i] = n
                    kw = dict(to=queries[i], combine=(HEADS - 1, n) if n < 3 else None, parts=[])
                else:
                    job = mem_job(1, i, queries[i], mem_v[:, MEM_HEADS + i, :])
                    first, second = mem_parts(1, i, 13, queries[i], U_MB + place[i] + 2)
                    segs[-1].parts += first
                    kw = dict(job=job, gate=G_MB + i, y=True, parts=second)
                segs.append(Segment(C_MB + n, n % 2, 16 * ((C_MB + n + 1) // 2 + 1), U_MB + n, **kw))
            return segs

        def b_seg(i, k, **kw):
            return Segment(C_B + k + i * 6, k % 2, 16 * ((C_B + k + 1) // 2 + 1) + i * 48,
                           U_B + k + i * 6, **kw)

        def front_b(i, combine=None):
            r = R_B + i * 8
            part = [None if combine is None else (combine, n) for n in range(3)]
            return [b_seg(i, 0, to=kT, rope=r, combine=part[0]),
                    b_seg(i, 1, to=vT, also=vT16, combine=part[1]),
                    b_seg(i, 2, to=qT[0], rope=r + 2, combine=part[2])]

        def back_b(i):
            segs = []
            for g in range(3):
                job = Job(T_B + g * TILES + i * 24, X_B + X_B_G[g] + i * X_B_PER, X_B_G[g] % 2,
                          O_B + 2 * g + i * 8, g, b_tiles(g), vbuf[g % 2], b_fills(g),
                          queries=R_B + 5 + 2 * g + i * 8, v_use=U_B + 3 + i * 6, group=g, out=g,
                          combined=i + (G_B + 1) if g == 0 else None,
                          stored=16 + 16 * (KV + MEM_HEADS) + i * 16 if g == 0 else None)
                if g < 2:
                    segs.append(b_seg(i, 3 + g, to=qT[(g + 1) % 2], order=(1, 16)[g],
                                      rope=R_B + 4 + 2 * g + i * 8, job=job))
                else:
                    segs.append(b_seg(i, 5, job=job, gate=G_B + i))
            return segs

        block = ctx.enter_context(nc.Block())

        @block.sync
        def _(sp):
            nc.sync.dma_start(ident[:, :], identity).then_inc(const_in, 16)
            for t in range(MEM // P):
                nc.sync.dma_start(mem_rows[:, t, :], mem[0, t * P:(t + 1) * P, :]
                                  ).then_inc(mem_in[t], 16)

            def load(c, slot, src):
                sp.wait_ge(w_lo, c + 1)
                sp.sem_inc(held, 1)
                nc.sync.dma_start(w_raw[:, slot, :].rearrange("p (k n) -> p k n", k=KT),
                                  src).then_inc(w_full[slot], 16)

            def columns(w, col):
                return w.rearrange("(k p) n -> p k n", p=P)[:, :, bass.ds(col, P)]

            def store(j, row, y):
                sp.wait_ge(y_done, y + 2)
                sp.sem_inc(held, 1)
                nc.sync.dma_start(y_dram[bass.ds(row, 1)].rearrange("a p n -> p (a n)"),
                                  oT[j]).then_inc(stored[j], 16)

            x_rows = x[0].rearrange("(t p) d -> p t d", p=P)
            for layer in range(DEPTH):
                with sp.Fori(0, MEM_HEADS) as h:
                    c = h * 2 + layer * MEM_HEADS * 2
                    load(c, 0, columns(w_mkv[layer], h * DH + MEM_HEADS * DH))
                    load(c + 1, 1, columns(w_mkv[layer], h * DH))
                    if layer == 1:
                        nc.sync.dma_start(rows[:, bass.ds(h * 2, 2), :],
                                          x_rows[:, bass.ds(h * 2, 2), :]).then_inc(row_in, 16)
                if layer == 0:
                    for t, src in ((cosb, rope_cos), (sinb, rope_sin), (m_a, mask_a), (m_b, mask_b),
                                   (m_b2, mask_b2)):
                        nc.sync.dma_start(t[:, :], src).then_inc(const_in, 16)
                    nc.sync.dma_start(sinks[:, :], sink_a[0].partition_broadcast(P)
                                      ).then_inc(const_in, 16)

            def a_head(i, j):
                c = C_A + 2 + 2 * j + i * 8
                load(c, 0, columns(w_in_a[0], i * (GROUP * DH) + (A_Q + j * DH)))
                load(c + 1, 1, columns(w_in_a[0], i * (GROUP * DH) + (A_G + j * DH)))

            def a_key_value(i):
                load(C_A + i * 8, 0, columns(w_in_a[0], i * DH + A_K))
                load(C_A + 1 + i * 8, 1, columns(w_in_a[0], i * DH + A_V))

            def a_heads(i):
                a_head(i, 0)
                for j in range(1, GROUP):
                    a_head(i, j)
                    store(j - 1, i * GROUP + (j - 1), G_A + (j - 1) + i * GROUP)

            def mem_head(i):
                c = C_MA + i * 2
                load(c, 0, columns(w_in_a[0], i * DH + A_MQ))
                load(c + 1, 1, columns(w_in_a[0], i * DH + (A_G + HEADS * DH)))

            a_key_value(0)
            with sp.Fori(0, KV - 1) as i:
                a_heads(i)
                a_key_value(i + 1)
                store(GROUP - 1, i * GROUP + (GROUP - 1), G_A + (GROUP - 1) + i * GROUP)
            a_heads(KV - 1)
            mem_head(0)
            store(GROUP - 1, HEADS - 1, G_A + HEADS - 1)

            with sp.Fori(1, MEM_HEADS) as i:
                mem_head(i)
                store(0, i + (HEADS - 1), i + (G_MA - 1))

            def branch(layer, totals, residual, ahead, dst):
                w = w_out[layer].rearrange("(e p) n -> e p n", p=P)
                c0, y0 = (C_OA, C_OB)[layer], layer * 2 * NE

                def load_w(h, e, s):
                    sp.wait_ge(w_lo, h * NE + e + (c0 + s + 1))
                    sp.sem_inc(held, 1)
                    nc.sync.dma_start(w_raw[:, s, :], w[bass.ds(e + s, 1)]
                                      .rearrange("a p n -> p (a n)")).then_inc(w_full[s], 16)

                def load_y(h, e, s):
                    sp.wait_ge(y_lo, h * NE + e + (y0 + s + 1))
                    sp.sem_inc(held, 1)
                    nc.sync.dma_start(y_raw[:, s, :], y_dram[bass.ds(e + s, 1)]
                                      .rearrange("a p n -> p (a n)")[:, bass.ds(h * HALF, HALF)]
                                      ).then_inc(y_full[s], 16)

                def load_pairs(h, first, last):
                    with sp.Fori(first // 2, last // 2) as pair:
                        for s in range(2):
                            load_w(h, pair * 2, s)
                            load_y(h, pair * 2, s)

                load_w(0, 0, 0)
                load_w(0, 0, 1)
                for j in range(3):
                    sp.wait_ge(stored[j], 16 * totals[j] + (16 if j > 0 else 0))
                load_y(0, 0, 0)
                load_y(0, 0, 1)
                store(0, NE - 1, (G_MA, G_MB)[layer] + MEM_HEADS - 1)
                load_pairs(0, 2, 8)
                sp.wait_ge(stored[0], 16 + 16 * totals[0])
                if layer == 1:
                    sp.wait_ge(rows_out, 16 * TILES)
                nc.sync.dma_start(rows[:, 0:4, :], residual[:, 0:4, :]).then_inc(res_in, 16)
                nc.sync.dma_start(g_row, ln_g[layer].partition_broadcast(P)).then_inc(gb_in, 16)
                nc.sync.dma_start(b_row, ln_b[layer].partition_broadcast(P)).then_inc(gb_in, 16)
                load_pairs(0, 8, NE)
                load_pairs(1, 0, 8)
                nc.sync.dma_start(rows[:, 4:8, :], residual[:, 4:8, :]).then_inc(res_in, 16)
                load_pairs(1, 8, NE)
                ahead()
                with sp.Fori(0, TILES) as t:
                    sp.wait_ge(ln_done, t + (layer * TILES + 1))
                    sp.sem_inc(held, 1)
                    nc.sync.dma_start(dst[bass.ds(t, 1)].rearrange("a p d -> p (a d)"),
                                      rows[:, bass.ds(t, 1), :].rearrange("p a d -> p (a d)")
                                      ).then_inc(rows_out, 16)

            def b_load(i, k, col):
                load(C_B + k + i * 6, k % 2, columns(w_in_b[0], i * DH + col))

            def exchange_statistics(i):
                sp.wait_ge(o_free, i * 8 + (O_B + 8 + 2))
                sp.sem_inc(held, 1)
                nc.sync.dma_start(soft_dram.rearrange("a g n -> g a n"), soft_rows[:, :, :]
                                  ).then_inc(soft_out, 16)
                sp.wait_ge(soft_out, i * 16 + 32)
                sp.sem_inc(held, 1)
                for g, d in enumerate(DIL):
                    for a in range(2):
                        src = soft_dram[a, g * TILES:(g + 1) * TILES, :].rearrange("t n -> (t n)")
                        nc.sync.dma_start(
                            soft_in[:, a, g, :].rearrange("b (r m) -> b r m", r=d),
                            src.rearrange("(r b m) -> b r m", r=d, b=BLOCKS)
                        ).then_inc(soft_back, 16)

            def exchange_weights(i):
                sp.wait_ge(comb, i * COMB_STEPS + 11)
                sp.sem_inc(held, 1)
                nc.sync.dma_start(weight_dram.rearrange("g (b m) -> b g m", b=BLOCKS),
                                  weight[:, :, :]).then_inc(weight_out, 16)
                sp.wait_ge(weight_out, i * 16 + 16)
                sp.sem_inc(held, 1)
                nc.sync.dma_start(wT_all, weight_dram.rearrange("g n -> (g n)")
                                  .partition_broadcast(P)).then_inc(weight_in, 16)

            branch(0, (KV + MEM_HEADS, KV, KV), x[0].rearrange("(t p) d -> p t d", p=P),
                   lambda: (b_load(0, 0, B_K), b_load(0, 1, B_V)), x1_dram)
            b_load(0, 2, B_Q)
            b_load(0, 3, B_Q + HEADS * DH)
            b_load(0, 4, B_Q + 2 * HEADS * DH)
            b_load(0, 5, B_G)
            with sp.Fori(0, HEADS - 1) as i:
                b_load(i + 1, 0, B_K)
                b_load(i + 1, 1, B_V)
                b_load(i + 1, 2, B_Q)
                exchange_statistics(i)
                b_load(i + 1, 3, B_Q + HEADS * DH)
                exchange_weights(i)
                b_load(i + 1, 4, B_Q + 2 * HEADS * DH)
                store(0, i, i + G_B)
                b_load(i + 1, 5, B_G)

            def mem_load(n):
                what, i = MEM_B_ORDER[n]
                col = B_MQ + i * DH if what == "q" else B_G + (HEADS + i) * DH
                load(C_MB + n, n % 2, columns(w_in_b[0], col))

            for n in range(3):
                mem_load(n)
            exchange_statistics(HEADS - 1)
            mem_load(3)
            exchange_weights(HEADS - 1)
            mem_load(4)
            store(0, HEADS - 1, G_B + HEADS - 1)
            mem_load(5)
            for i in range(MEM_HEADS - 1):
                store(0, HEADS + i, G_MB + i)
                if i < 2:
                    mem_load(6 + i)
            branch(1, (KV + MEM_HEADS + HEADS + MEM_HEADS, KV, KV),
                   x1_dram.rearrange("t p d -> p t d"), lambda: None,
                   out[0].rearrange("(t p) d -> t p d", p=P))
            sp.wait_ge(rows_out, 16 * TILES * DEPTH)

        @block.gpsimd
        def _(pool):
            nc.gpsimd.memset(m_0[:, :], 0.0).then_inc(consts, 1)
            nc.gpsimd.memset(power[:, 0:1], LN_EPS).then_inc(consts, 1)
            nc.gpsimd.memset(power[:, 1:2], -0.5).then_inc(consts, 1)
            pool.wait_ge(consts, 3)
            pool.wait_ge(t_free, X_A + 2)

            with pool.Fori(0, MEM_HEADS) as i:
                pool.wait_ge(pv_done, i * TILES + T_MA)
                pool.sem_inc(held, 1)
                nc.gpsimd.tensor_copy(head_mv[:, :], mem_v[:, bass.ds(i, 1), :]
                                      .rearrange("p a n -> p (a n)")).then_inc(memkv, 1)

            def norms(layer):
                def last_step(t):
                    pool.wait_ge(ln_step, 2 * (layer * TILES + t + 1))
                    nc.gpsimd.tensor_tensor(rows[:, t, :], rows[:, t, :], b_row,
                                            ALU.add).then_inc(ln_done, 1)

                for t in range(TILES):
                    n = layer * TILES + t
                    if t == 4:
                        last_step(3)
                    pool.wait_ge(ln_aggr, n + 1)
                    nc.gpsimd.tensor_tensor(rstd[:, t, 0:1], mv[:, t, 1:2], power[:, 0:1],
                                            ALU.add).then_inc(ln_eps, 1)
                    pool.wait_ge(ln_eps, n + 1)
                    nc.gpsimd.tensor_tensor(rstd[:, t, 1:2], rstd[:, t, 0:1], power[:, 1:2],
                                            ALU.pow).then_inc(ln_rstd, 1)
                    if t % 4 > 0:
                        last_step(t - 1)
                last_step(TILES - 1)

            norms(0)
            norms(1)

        @block.tensor
        def _(pe):

            def rows_to_columns(src, f0, f1, first, ready=None):
                for f in range(f0, f1):
                    t, k0 = f // 2, 4 * (f % 2)
                    if ready is not None:
                        ready(f)
                    pe.wait_ge(xt_lo, first + f + 1)
                    for k in range(4):
                        mm = nc.tensor.transpose(XB[f % BANKS_X][:, k * P:(k + 1) * P],
                                                 src[:, t, (k0 + k) * P:(k0 + k + 1) * P],
                                                 ident[:, :])
                    mm.then_inc(xt_ready, 1)

            def step(dst, cols, slot, k):
                w_h = w_split[:, slot, 0, k * P:(k + 1) * P]
                w_l = w_split[:, slot, 1, k * P:(k + 1) * P]
                nc.tensor.matmul(dst, w_h, xT[:, 0, k, cols], start=(k == 0), stop=False)
                nc.tensor.matmul(dst, w_h, xT[:, 1, k, cols], start=False, stop=False)
                return nc.tensor.matmul(dst, w_l, xT[:, 0, k, cols], start=False,
                                        stop=(k == KT - 1))

            def values(job, f):
                if f == 0:
                    pe.wait_ge(p_free[0], job.v_use)
                    pe.wait_ge(p_free[1], job.v_use)
                pe.wait_ge(t_free, job.x + (f + 1))
                if job.fills[f][0][1] < P:
                    pe.sem_inc(held, 1)
                for n, (src, rows_) in enumerate(job.fills[f]):
                    mm = nc.tensor.transpose(TB[(job.x_odd + f) % 2][0:rows_, n * P:(n + 1) * P],
                                             src, ident[:, :])
                mm.then_inc(t_ready, 1)

            def scores(job, t):
                q, k, n, _, _, at = job.tiles[t]
                if t == 0 and job.copied is not None:
                    pe.wait_ge(memkv, job.copied)
                if job.queries is not None:
                    if DIL[job.group] > 1:
                        if t == 0:
                            pe.wait_ge(rope_done, job.queries)
                    elif t % 4 == 0:
                        pe.wait_ge(rope_done, job.queries - 1 + t // 4)
                if job.split is not None and t % 4 == 0:
                    pe.wait_ge(part_lo, job.split + t // 4)
                pe.wait_ge(s_free, job.a + (t + 1))
                dst = SB[t % 2][:, 0:n]
                if job.split is None:
                    nc.tensor.matmul(dst, q, k, start=True, stop=True).then_inc(s_ready, 1)
                    return
                (q_h, q_l), (k_h, k_l) = ([qk_split[:, w, part, at[w]:at[w] + size]
                                           for part in range(2)] for w, size in ((0, P), (1, n)))
                nc.tensor.matmul(dst, q_h, k_h, start=True, stop=False)
                nc.tensor.matmul(dst, q_h, k_l, start=False, stop=False)
                nc.tensor.matmul(dst, q_l, k_h, start=False, stop=True).then_inc(s_ready, 1)

            def transposes(job, t):
                n = len(job.fills) + t
                pe.wait_ge(t_free, job.x + (n + 1))
                pe.wait_ge(p_done, job.a + (t + 1))
                for c, (_, keys, k0) in enumerate(job.tiles[t][4]):
                    mm = nc.tensor.transpose(TB[(job.x_odd + n) % 2][0:keys, c * P:(c + 1) * P],
                                             p_sb[t % 3][:, 1 + k0:1 + k0 + keys], ident[:, :])
                mm.then_inc(t_ready, 1)

            def outputs(job, t):
                h, chunks = t // 4, job.tiles[t][4]
                if t % 4 == 0:
                    pe.wait_ge(o_free, job.o + (h + 1))
                pe.wait_ge(t_free, job.x + (len(job.fills) + t + 3))
                for c, (v, keys, _) in enumerate(chunks):
                    mm = nc.tensor.matmul(OB[h][:, (t % 4) * P:(t % 4 + 1) * P],
                                          job.vbuf[0:keys, v * DH:(v + 1) * DH],
                                          pT[t % 2][0:keys, c * P:(c + 1) * P],
                                          start=(c == 0), stop=(c == len(chunks) - 1))
                mm.then_inc(pv_done, 1)

            def statistics(i, a):
                pe.wait_ge(o_free, i * 8 + (O_B + 7 + a))
                if a == 0:
                    pe.wait_ge(exp_done, i * 24 + (T_B + 24))
                pe.sem_inc(held, 1)
                nc.tensor.transpose(OB[a][0:3 * TILES, 0:P],
                                    soft[:, a].rearrange("p g t -> p (g t)"), ident[:, :]
                                    ).then_inc(soft_t, 1)

            def run(seg, second_half=None):
                pe.wait_ge(w_lo, seg.c + 3)
                for s in range(STEPS):
                    h, k = s // KT, s % KT
                    if s == KT and second_half is not None:
                        second_half()
                    if k == 0:
                        pe.wait_ge(p_free[h], seg.u + 1)
                    mm = step(PB[h][:, :], slice(h * HALF, (h + 1) * HALF), seg.slot, k)
                    if k == KT - 1:
                        mm.then_inc(p_ready[h], 1)
                    if seg.combine is not None and seg.combine[1] == 0 and 1 <= s < 3:
                        statistics(seg.combine[0], s - 1)
                    fill, t_s, t_t, t_o = riding(seg.job, s)
                    if fill is not None:
                        values(seg.job, fill)
                    if t_o is not None:
                        outputs(seg.job, t_o)
                    if t_t is not None:
                        transposes(seg.job, t_t)
                    if t_s is not None:
                        scores(seg.job, t_s)

            def branch(layer):
                c0, y0 = (C_OA, C_OB)[layer], layer * 2 * NE

                def out_e(h, e, slot, first, last):
                    pe.wait_ge(w_lo, h * NE + e + (c0 + 3))
                    pe.wait_ge(y_lo, h * NE + e + (y0 + 3))
                    for b in range(8):
                        t, cols = b // 2, slice((b % 2) * HALF, (b % 2 + 1) * HALF)
                        if first:
                            pe.wait_ge(z_free, h * 8 + (layer * 16 + b + 1))
                        y_h = y_split[:, slot, 0, t * P:(t + 1) * P]
                        y_l = y_split[:, slot, 1, t * P:(t + 1) * P]
                        mm = nc.tensor.matmul(bank[b][:, :], y_h, w_split[:, slot, 0, cols],
                                              start=first, stop=False)
                        if b == 0:
                            mm.then_inc(out_step, 1)
                        nc.tensor.matmul(bank[b][:, :], y_h, w_split[:, slot, 1, cols],
                                         start=False, stop=False)
                        mm = nc.tensor.matmul(bank[b][:, :], y_l, w_split[:, slot, 0, cols],
                                              start=False, stop=last)
                        if last:
                            mm.then_inc(br_ready, 1)

                pe.wait_ge(p_free[0], (U_MA, U_MB)[layer] + 2 * MEM_HEADS + 1)
                pe.wait_ge(p_free[1], (U_MA, U_MB)[layer] + 2 * MEM_HEADS + 1)
                pe.wait_ge(s_free, (T_MA, T_MB)[layer] + MEM_HEADS * TILES + 2)
                pe.wait_ge(t_free, (X_MA, X_MB)[layer] + MEM_HEADS * TILES + 2)
                pe.wait_ge(o_free, (O_MA, O_MB)[layer] + 2 * MEM_HEADS + 2)
                with pe.Fori(0, 2) as h:
                    out_e(h, 0, 0, True, False)
                    with pe.Fori(1, NE - 1, 2) as e:
                        out_e(h, e, 1, False, False)
                        out_e(h, e + 1, 0, False, False)
                    out_e(h, NE - 1, 1, False, True)

            pe.wait_ge(const_in, 16)
            rows_to_columns(mem_rows, 0, 4, 0, lambda f: pe.wait_ge(mem_in[f // 2], 16))
            pe.wait_ge(xt_lo, 4 + BANKS_X)
            with pe.Fori(0, DEPTH * MEM_HEADS) as i:
                for kv in range(2):
                    pe.wait_ge(w_lo, i * 2 + (kv + 3))
                    pe.wait_ge(p_free[kv], i + 1)
                    for k in range(KT):
                        mm = step(PB[kv][:, 0:MEM], slice(0, MEM), kv, k)
                    mm.then_inc(p_ready[kv], 1)
                pe.wait_ge(p_free[0], i + 2)
                for f in range(2):
                    pe.wait_ge(t_free, i * 2 + (f + 1))
                    nc.tensor.transpose(TB[f][:, 0:P], mem_vT[:, f * P:(f + 1) * P],
                                        ident[:, :]).then_inc(t_ready, 1)
            pe.wait_ge(row_in, 16 * 4)
            pe.wait_ge(const_in, 16 * 7)
            pe.wait_ge(t_free, X_A + 2)
            def x_half(first, h, ready=None):
                rows_to_columns(rows, h * TILES, (h + 1) * TILES, first, ready)
                pe.wait_ge(xt_lo, first + (h + 1) * TILES + BANKS_X)

            x_half(4, 0)
            run(unit_a(0)[0], lambda: x_half(4, 1))
            for seg in unit_a(0)[1:]:
                run(seg)
            with pe.Fori(1, KV) as i:
                for seg in unit_a(i):
                    run(seg)
            with pe.Fori(0, MEM_HEADS) as i:
                for seg in unit_mem(i):
                    run(seg)
            branch(0)
            def row_ready(f):
                pe.wait_ge(ln_done, f // 2 + 1)
                if f < BANKS_X:
                    pe.wait_ge(z_free, 8 + 8 + 5 + f)

            x_half(20, 0, row_ready)
            run(front_b(0)[0], lambda: x_half(20, 1, row_ready))
            for seg in front_b(0)[1:]:
                run(seg)
            with pe.Fori(0, HEADS - 1) as i:
                for seg in back_b(i) + front_b(i + 1, combine=i):
                    run(seg)
            for seg in back_b(HEADS - 1):
                run(seg)
            for seg in memory_b():
                run(seg)
            branch(1)

        @block.scalar
        def _(act):
            act.sem_inc(p_free[0], 1)
            act.sem_inc(p_free[1], 1)
            act.sem_inc(t_free, 2)
            act.sem_inc(o_free, 2)
            act.sem_inc(soft_out, 16)
            for j in range(3):
                act.sem_inc(stored[j], 16)

            def split_hi(slot, full):
                act.wait_ge(w_full[slot], full)
                nc.scalar.copy(w_split[:, slot, 0, :], w_raw[:, slot, :]).then_inc(w_hi, 1)

            def columns_hi(tiles, first, column0):
                for f in range(2 * tiles):
                    t, k0 = f // 2, 4 * (f % 2)
                    act.wait_ge(xt_ready, first + f + 1)
                    nc.scalar.copy(xT[:, 0, k0:k0 + 4, t * P:(t + 1) * P],
                                   XB[f % BANKS_X][:, :].rearrange("p (k n) -> p k n", k=4)
                                   ).then_inc(xt_hi, 1)

            def operand_hi(part):
                if part.rope is not None:
                    act.wait_ge(rope_done, part.rope)
                if part.u is not None:
                    act.wait_ge(p_free[part.bank], part.u)
                nc.scalar.copy(qk_split[:, part.dst, 0, part.first:part.first + part.size],
                               part.src).then_inc(part_hi, 1)

            def values(job, f):
                rows_ = job.fills[f][0][1]
                n = len(job.fills[f]) * P
                v0 = sum(len(g) for g in job.fills[:f]) * DH
                if f == 0 and job.combined is not None:
                    act.wait_ge(y_done, job.combined)
                act.wait_ge(t_ready, job.x + (f + 1))
                nc.scalar.copy(job.vbuf[0:rows_, v0:v0 + n],
                               TB[(job.x_odd + f) % 2][0:rows_, 0:n]).then_inc(t_free, 1)

            def exponential(job, t):
                n = job.tiles[t][2]
                c0 = 1 if job.sink is None else 0
                act.wait_ge(negmax, job.a + (t + 1))
                nc.scalar.activation(p_sb[t % 3][:, c0:1 + n], s_sb[t % 3][:, c0:1 + n], ACT.Exp,
                                     bias=nmax[:, job.stat, t:t + 1], scale=SCALE,
                                     accum_out=zsum[:, job.stat, t:t + 1]).then_inc(exp_done, 1)

            def transposed(job, t):
                n = len(job.fills) + t
                src, chunks = TB[(job.x_odd + n) % 2], job.tiles[t][4]
                whole = sum(keys == P for _, keys, _ in chunks)
                act.wait_ge(t_ready, job.x + (n + 1))
                cp = nc.scalar.copy(pT[t % 2][:, 0:whole * P], src[:, 0:whole * P])
                if whole < len(chunks):
                    cp = nc.scalar.copy(pT[t % 2][0:W_B, whole * P:(whole + 1) * P],
                                        src[0:W_B, whole * P:(whole + 1) * P])
                cp.then_inc(t_free, 1)

            def in_group_order(v, g, h):
                d = DIL[g]
                if d == 1:
                    return v[:, h * HALF:(h + 1) * HALF]
                return dilated(v, d)[:, h * d // 2:(h + 1) * d // 2, :]

            def group_bank(b, g):
                d = DIL[g]
                return b[:, :] if d == 1 else b[:, :].rearrange("p (r n) -> p r n", r=d // 2)

            def output_half(job, h):
                if h == 0 and job.stored is not None:
                    act.wait_ge(stored[job.out], job.stored)
                act.wait_ge(pv_done, job.a + 4 * (h + 1))
                nc.scalar.copy(in_group_order(oT[job.out], job.group, h),
                               group_bank(OB[h], job.group)).then_inc(o_free, 1)

            def project_half(seg, h):
                act.wait_ge(p_ready[h], seg.u + 1)
                if seg.gate is not None:
                    if h == 0:
                        act.wait_ge(y_done, seg.gate + 1)
                    nc.scalar.activation(gate[:, h * HALF:(h + 1) * HALF], PB[h][:, :], ACT.Tanh,
                                         scale=0.5).then_inc(tanh_done, 1)
                    return
                cp = nc.scalar.copy(half_in_order(seg.to, seg.order, h),
                                    like_order(PB[h][:, :], seg.order))
                if seg.also is not None:
                    cp = nc.scalar.copy(half_in_order(seg.also, 16, h), like_order(PB[h][:, :], 16))
                cp.then_inc(p_free[h], 1)

            def statistics(i, a):
                if a == 0:
                    act.wait_ge(soft_out, i * 16 + 16)
                act.wait_ge(soft_t, i * 2 + (a + 1))
                nc.scalar.copy(soft_rows[:, a, :], OB[a][0:3 * TILES, 0:P]).then_inc(o_free, 1)

            def exponentials(i):
                act.wait_ge(comb, i * COMB_STEPS + 6)
                nc.scalar.activation(weight[:, :, :], weight[:, :, :], ACT.Exp).then_inc(comb_exp, 1)

            def run(seg):
                for s in range(STEPS):
                    fill, t_s, t_t, t_o = riding(seg.job, s)
                    if fill is not None:
                        values(seg.job, fill)
                    for part in seg.parts:
                        if part.slot == s:
                            operand_hi(part)
                    if seg.combine is not None:
                        i, part = seg.combine
                        if part == 0 and 1 <= s < 3:
                            statistics(i, s - 1)
                        if part == 0 and s == 14:
                            exponentials(i)
                    if s == KT:
                        project_half(seg, 0)
                    if t_t is not None:
                        transposed(seg.job, t_t)
                    if t_s is not None:
                        exponential(seg.job, t_s)
                    if seg.job is not None and s == LAG_PV + 4:
                        output_half(seg.job, 0)
                    if s == seg.split:
                        split_hi((seg.slot + 1) % 2, seg.next_full)
                project_half(seg, 1)
                if seg.job is not None:
                    output_half(seg.job, 1)

            def branch(layer, more):
                c0, y0 = (C_OA, C_OB)[layer], layer * 2 * NE

                def y_tile(n, slot, full):
                    act.wait_ge(y_full[slot], full)
                    nc.scalar.copy(y_split[:, slot, 0, :], y_raw[:, slot, :]).then_inc(y_hi, 1)

                def next_w(n, slot, full):
                    act.wait_ge(out_step, n + (y0 + 1))
                    act.wait_ge(w_full[slot], full)
                    nc.scalar.copy(w_split[:, slot, 0, :], w_raw[:, slot, :]).then_inc(w_hi, 1)

                f_w, f_y = 16 * (c0 // 2), 16 * (y0 // 2)
                y_tile(0, 0, f_y + 16)
                with act.Fori(0, 2 * NE - 2, 2) as n:
                    next_w(n, 1, n * 8 + (f_w + 16))
                    y_tile(n + 1, 1, n * 8 + (f_y + 16))
                    next_w(n + 1, 0, n * 8 + (f_w + 32))
                    y_tile(n + 2, 0, n * 8 + (f_y + 32))
                n = 2 * NE - 2
                next_w(n, 1, n * 8 + (f_w + 16))
                y_tile(n + 1, 1, n * 8 + (f_y + 16))
                if more:
                    next_w(n + 1, 0, n * 8 + (f_w + 32))
                act.wait_ge(br_ready, 16 * (layer + 1))

            columns_hi(2, 0, 0)
            split_hi(0, 16)
            with act.Fori(0, DEPTH * MEM_HEADS) as i:
                for kv in range(2):
                    if kv == 0:
                        split_hi(1, i * 16 + 16)
                    else:
                        split_hi(0, i * 16 + 32)
                    act.wait_ge(p_ready[kv], i + 1)
                    if kv == 0:
                        nc.scalar.copy(mem_vT, PB[0][:, 0:MEM]).then_inc(p_free[0], 1)
                    else:
                        nc.scalar.copy(mem_k[:, bass.ds(i, 1), :].rearrange("p a n -> p (a n)"),
                                       PB[1][:, 0:MEM]).then_inc(p_free[1], 1)
                for f in range(2):
                    act.wait_ge(t_ready, i * 2 + (f + 1))
                    nc.scalar.copy(mem_v[:, bass.ds(i, 1), f * P:(f + 1) * P]
                                   .rearrange("p a n -> p (a n)"), TB[f][:, 0:P]
                                   ).then_inc(t_free, 1)
            columns_hi(TILES, 4, 0)
            with act.Fori(0, KV) as i:
                for seg in unit_a(i):
                    run(seg)
            with act.Fori(0, MEM_HEADS) as i:
                for seg in unit_mem(i):
                    run(seg)
            branch(0, True)
            columns_hi(TILES, 20, 0)
            act.wait_ge(rows_out, 16 * TILES)
            for seg in front_b(0):
                run(seg)
            with act.Fori(0, HEADS - 1) as i:
                for seg in back_b(i) + front_b(i + 1, combine=i):
                    run(seg)
            for seg in back_b(HEADS - 1):
                run(seg)
            for seg in memory_b():
                run(seg)
            branch(1, False)

        @block.vector
        def _(dve):
            dve.sem_inc(w_lo, 2)
            dve.sem_inc(xt_lo, BANKS_X)
            dve.sem_inc(s_free, 2)
            dve.sem_inc(y_done, 1)
            dve.sem_inc(y_lo, 2)
            dve.sem_inc(z_free, 8)
            dve.sem_inc(rope_done, 1)

            def split_lo(slot, c):
                dve.wait_ge(w_hi, c + 1)
                nc.vector.tensor_tensor(w_split[:, slot, 1, :], w_raw[:, slot, :],
                                        w_split[:, slot, 0, :].bitcast(F32),
                                        ALU.subtract).then_inc(w_lo, 1)

            def columns_lo(first, f0, f1):
                for f in range(f0, f1):
                    t, k0 = f // 2, 4 * (f % 2)
                    dve.wait_ge(xt_hi, first + f + 1)
                    nc.vector.tensor_tensor(xT[:, 1, k0:k0 + 4, t * P:(t + 1) * P],
                                            XB[f % BANKS_X][:, :].rearrange(
                                                "p (k n) -> p k n", k=4),
                                            xT[:, 0, k0:k0 + 4, t * P:(t + 1) * P].bitcast(F32),
                                            ALU.subtract).then_inc(xt_lo, 1)

            def operand_lo(part):
                cols = slice(part.first, part.first + part.size)
                dve.wait_ge(part_hi, part.n + 1)
                nc.vector.tensor_tensor(qk_split[:, part.dst, 1, cols], part.src,
                                        qk_split[:, part.dst, 0, cols].bitcast(F32),
                                        ALU.subtract).then_inc(part_lo, 1)

            swap = [(i + ROPE // 2) % ROPE for i in range(ROPE)]

            def rotate(seg, h):
                r = seg.rope + h
                v = half_in_order(seg.to[0:ROPE, :], seg.order, h)
                cos_h = like_order(cosb[:, h * HALF:(h + 1) * HALF], seg.order)
                sin_h = like_order(sinb[:, h * HALF:(h + 1) * HALF], seg.order)
                a, b = rope_a[0:ROPE, :], rope_b[0:ROPE, :]
                if seg.order > 1:
                    a = a.rearrange("p (r n) -> p r n", r=seg.order)
                    b = b.rearrange("p (r n) -> p r n", r=seg.order)
                dve.wait_ge(rope_done, r + 1)
                dve.wait_ge(p_free[h], seg.u + 2)
                nc.vector.tensor_tensor(a, v, cos_h, ALU.mult)
                nc.vector.stream_shuffle(b, v, swap).then_inc(rope_turned, 1)
                dve.wait_ge(rope_turned, r + 1)
                nc.vector.tensor_tensor(b, b, sin_h, ALU.mult).then_inc(rope_sine, 1)
                dve.wait_ge(rope_sine, r + 1)
                nc.vector.tensor_tensor(v, a, b, ALU.add).then_inc(rope_done, 1)

            def project_half(seg, h):
                if seg.rope is not None:
                    rotate(seg, h)
                if seg.gate is not None:
                    cols = slice(h * HALF, (h + 1) * HALF)
                    dve.wait_ge(tanh_done, seg.gate * 2 + (h + 1))
                    nc.vector.scalar_tensor_tensor(out=gate[:, cols], in0=gate[:, cols], scalar=1.0,
                                                   in1=PB[h][:, :], op0=ALU.add, op1=ALU.mult
                                                   ).then_inc(p_free[h], 1)

            def mask(job, t):
                n, m = job.tiles[t][2], job.tiles[t][3]
                dve.wait_ge(s_ready, job.a + (t + 1))
                dve.sem_inc(held, 1)
                src = SB[t % 2][:, 0:n]
                if m.ndim != src.ndim:
                    raise AssertionError
                nc.vector.tensor_tensor_reduce(s_sb[t % 3][:, 1:1 + n], src, m, 1.0, -3.0e38,
                                               ALU.add, ALU.max, rmax[:, job.stat, t:t + 1]
                                               ).then_inc(s_free, 1)

            def bias(job, t):
                dve.wait_ge(s_free, job.a + (t + 3))
                r, n = rmax[:, job.stat, t:t + 1], nmax[:, job.stat, t:t + 1]
                if job.sink is None:
                    ts = nc.vector.tensor_scalar(n, r, -SCALE, None, ALU.mult)
                else:
                    ts = nc.vector.tensor_scalar(n, r, -SCALE, sinks_neg[:, bass.ds(job.sink, 1)],
                                                 ALU.mult, ALU.min)
                ts.then_inc(negmax, 1)

            def invert(job, t):
                dve.wait_ge(exp_done, job.a + (t + 1))
                nc.vector.reciprocal(zinv[:, job.stat, t:t + 1], zsum[:, job.stat, t:t + 1]
                                     ).then_inc(zinv_done, 1)

            def normalise(job, t):
                n = job.tiles[t][2]
                dve.wait_ge(zinv_done, job.a + (t + 1))
                nc.vector.tensor_scalar(p_sb[t % 3][:, 1:1 + n], p_sb[t % 3][:, 1:1 + n],
                                        zinv[:, job.stat, t:t + 1], None, ALU.mult
                                        ).then_inc(p_done, 1)

            def combine_weights(i):
                n = i * COMB_STEPS
                dve.wait_ge(y_done, i + (G_B + 1))
                dve.wait_ge(soft_back, i * 96 + 96)
                for g, d in enumerate(DIL):
                    nc.vector.tensor_copy(
                        soft_tok[:, :, g, :].rearrange("b a (m r) -> b a m r", r=d),
                        soft_in[:, :, g, :].rearrange("b a (r m) -> b a m r", r=d)
                    ).then_inc(comb, 1)
                m, z = soft_tok[:, 0], soft_tok[:, 1]

                def for_groups(v):
                    return v.unsqueeze(1).broadcast_to([BLOCKS, 3, L // BLOCKS])

                dve.wait_ge(comb, n + 3)
                nc.vector.tensor_tensor(w_sum[:, :], m[:, 0, :], m[:, 1, :], ALU.min
                                        ).then_inc(comb, 1)
                dve.wait_ge(comb, n + 4)
                nc.vector.tensor_tensor(w_sum[:, :], w_sum[:, :], m[:, 2, :], ALU.min
                                        ).then_inc(comb, 1)
                dve.wait_ge(comb, n + 5)
                nc.vector.tensor_tensor(weight[:, :, :], for_groups(w_sum[:, :]), m, ALU.subtract
                                        ).then_inc(comb, 1)
                dve.wait_ge(comb_exp, i + 1)
                nc.vector.tensor_tensor(weight[:, :, :], weight[:, :, :], z, ALU.mult
                                        ).then_inc(comb, 1)
                dve.wait_ge(comb, n + 7)
                nc.vector.tensor_tensor(w_sum[:, :], weight[:, 0, :], weight[:, 1, :], ALU.add
                                        ).then_inc(comb, 1)
                dve.wait_ge(comb, n + 8)
                nc.vector.tensor_tensor(w_sum[:, :], w_sum[:, :], weight[:, 2, :], ALU.add
                                        ).then_inc(comb, 1)
                dve.wait_ge(comb, n + 9)
                nc.vector.reciprocal(w_sum[:, :], w_sum[:, :]).then_inc(comb, 1)
                dve.wait_ge(comb, n + 10)
                nc.vector.scalar_tensor_tensor(out=weight[:, :, :], in0=weight[:, :, :], scalar=0.5,
                                               in1=for_groups(w_sum[:, :]), op0=ALU.mult,
                                               op1=ALU.mult).then_inc(comb, 1)

            def combine_outputs(i):
                n = i * COMB_STEPS
                dve.wait_ge(weight_in, i * 16 + 16)
                for g in range(3):
                    nc.vector.tensor_tensor(oT[g], oT[g], wT[g], ALU.mult).then_inc(comb, 1)
                dve.wait_ge(comb, n + 13)
                nc.vector.tensor_tensor(oT[0], oT[0], oT[1], ALU.add).then_inc(comb, 1)
                dve.wait_ge(comb, n + 15)
                nc.vector.tensor_tensor(oT[0], oT[0], oT[2], ALU.add).then_inc(comb, 1)
                dve.wait_ge(comb, n + 16)
                nc.vector.tensor_tensor(oT[0], oT[0], gate, ALU.mult).then_inc(y_done, 1)

            def run(seg):
                job = seg.job
                for s in range(STEPS):
                    if seg.combine is not None:
                        i, part = seg.combine
                        if part == 0 and s == 13:
                            combine_weights(i)
                        if part == 2 and s == 1:
                            combine_outputs(i)
                    for part in seg.parts:
                        if part.slot == s:
                            operand_lo(part)
                    _, t, _, _ = riding(job, s)
                    if job is not None and job.sink is not None and s == LEAD - 1:
                        for b in range(3):
                            nc.vector.tensor_copy(s_sb[b][:, 0:1],
                                                  sinks_raw[:, bass.ds(job.sink, 1)])
                    if job is not None and LEAD <= s <= LEAD + TILES:
                        if t is not None:
                            mask(job, t)
                        if s > LEAD:
                            invert(job, s - LEAD - 1)
                        if t is not None:
                            bias(job, t)
                        if s > LEAD:
                            normalise(job, s - LEAD - 1)
                    if s == KT + 1:
                        project_half(seg, 0)
                    if s == seg.split:
                        split_lo((seg.slot + 1) % 2, seg.c + 1)
                project_half(seg, 1)
                if seg.y:
                    dve.wait_ge(o_free, job.o + 4)
                    dve.wait_ge(p_free[1], seg.u + 2)
                    nc.vector.scalar_tensor_tensor(out=oT[job.out], in0=oT[job.out], scalar=0.5,
                                                   in1=gate, op0=ALU.mult, op1=ALU.mult
                                                   ).then_inc(y_done, 1)

            def branch(layer, more):
                c0, y0 = (C_OA, C_OB)[layer], layer * 2 * NE

                def y_tile(n, slot):
                    dve.wait_ge(y_hi, n + (y0 + 1))
                    nc.vector.tensor_tensor(y_split[:, slot, 1, :], y_raw[:, slot, :],
                                            y_split[:, slot, 0, :].bitcast(F32),
                                            ALU.subtract).then_inc(y_lo, 1)

                def step(n, slot):
                    split_lo(slot, n + (c0 + 1))
                    y_tile(n + 1, slot)

                def add(h):
                    dve.wait_ge(res_in, 16 * (2 * layer + h + 1))
                    for b in range(8):
                        t, cols = 4 * h + b // 2, slice((b % 2) * HALF, (b % 2 + 1) * HALF)
                        dve.wait_ge(br_ready, layer * 16 + h * 8 + b + 1)
                        nc.vector.scalar_tensor_tensor(out=rows[:, t, cols], in0=rows[:, t, cols],
                                                       scalar=ALPHA, in1=bank[b][:, :],
                                                       op0=ALU.mult, op1=ALU.add
                                                       ).then_inc(z_free, 1)

                def statistics(t):
                    n = layer * TILES + t
                    dve.wait_ge(z_free, 8 + 2 * n + 2)
                    for k in range(2):
                        nc.vector.bn_stats(stats[:, t, k, :], rows[:, t, k * HALF:(k + 1) * HALF]
                                           ).then_inc(ln_stat, 1)
                    dve.wait_ge(ln_stat, 2 * n + 2)
                    nc.vector.bn_aggr(mv[:, t, :], stats[:, t, :, :].rearrange("p a b -> p (a b)")
                                      ).then_inc(ln_aggr, 1)

                def norm(t):
                    n = layer * TILES + t
                    dve.wait_ge(ln_rstd, n + 1)
                    nc.vector.tensor_scalar(rows[:, t, :], rows[:, t, :], mv[:, t, 0:1],
                                            rstd[:, t, 1:2], ALU.subtract, ALU.mult
                                            ).then_inc(ln_step, 1)
                    dve.wait_ge(ln_step, 2 * n + 1)
                    dve.wait_ge(gb_in, 32 * (layer + 1))
                    nc.vector.tensor_tensor(rows[:, t, :], rows[:, t, :], g_row,
                                            ALU.mult).then_inc(ln_step, 1)

                y_tile(0, 0)
                with dve.Fori(0, NE - 2, 2) as n:
                    step(n, 1)
                    step(n + 1, 0)
                step(NE - 2, 1)
                step(NE - 1, 0)
                add(0)
                for n in range(8):
                    step(NE + n, (n + 1) % 2)
                    if n < 4:
                        statistics(n)
                    else:
                        norm(n - 4)
                with dve.Fori(NE + 8, 2 * NE - 2, 2) as n:
                    step(n, 1)
                    step(n + 1, 0)
                step(2 * NE - 2, 1)
                if more:
                    split_lo(0, c0 + 2 * NE)
                add(1)
                if more:
                    columns_lo(20, 0, TILES)
                for t in range(4, TILES + 2):
                    if t < TILES:
                        statistics(t)
                    if 4 < t <= TILES:
                        norm(t - 1)
                    if more and t > 5:
                        columns_lo(20, 2 * (t - 2), 2 * (t - 2) + 2)

            columns_lo(0, 0, 4)
            split_lo(0, 0)
            with dve.Fori(0, DEPTH * MEM_HEADS) as i:
                split_lo(1, i * 2 + 1)
                split_lo(0, i * 2 + 2)
            columns_lo(4, 0, 2 * TILES)
            dve.wait_ge(const_in, 16 * 7)
            nc.vector.tensor_scalar(sinks_raw[:, :], sinks[:, :], 1.0 / SCALE, None,
                                    ALU.mult).then_inc(sink_consts, 1)
            nc.vector.tensor_scalar(sinks_neg[:, :], sinks[:, :], -1.0, None,
                                    ALU.mult).then_inc(sink_consts, 1)
            dve.wait_ge(sink_consts, 2)
            with dve.Fori(0, KV) as i:
                for seg in unit_a(i):
                    run(seg)
            with dve.Fori(0, MEM_HEADS) as i:
                for seg in unit_mem(i):
                    run(seg)
            branch(0, True)
            for seg in front_b(0):
                run(seg)
            with dve.Fori(0, HEADS - 1) as i:
                for seg in back_b(i) + front_b(i + 1, combine=i):
                    run(seg)
            for seg in back_b(HEADS - 1):
                run(seg)
            for seg in memory_b():
                run(seg)
            branch(1, False)


def shape_constants():
    half = ROPE // 2
    inv = (np.float64(THETA) ** (-np.arange(half, dtype=np.float32) / np.float32(half))
           ).astype(np.float32)
    ang = (np.arange(L, dtype=np.float32)[None, :] * inv[:, None]).astype(np.float32)
    cos, sin = np.cos(ang.astype(np.float64)), np.sin(ang.astype(np.float64))
    q = np.arange(P)[:, None]
    ka, kb, k2 = np.arange(3 * P)[None, :], np.arange(2 * P)[None, :], np.arange(P)[None, :]

    def masked(valid):
        return np.where(valid, 0.0, NEG).astype(np.float32)

    return {
        "rope_cos": np.concatenate([cos, cos]).astype(np.float32),
        "rope_sin": np.concatenate([-sin, sin]).astype(np.float32),
        "mask_a": masked(np.abs(ka - P - q) <= W_A),
        "mask_b": masked(np.abs(kb - W_B - q) <= W_B),
        "mask_b2": masked(q // W_B == k2 // W_B),
        "identity": np.eye(P, dtype=np.float32),
    }


_INS = ["x", "mem", "w_in_a", "sink_a", "w_in_b", "w_mkv", "w_out", "ln_g", "ln_b"]


def kernel(**inputs):
    import concourse.bacc as _bacc
    from concourse.bass_utils import run_bass_kernel_spmd as _run

    nc = _bacc.Bacc("TRN2", target_bir_lowering=False, num_devices=1,
                    dynamic_dma_scratch_size=1024)
    arrays, args = {}, []
    given = {name: np.ascontiguousarray(inputs[name]) for name in _INS}
    for name, a in {**given, **shape_constants()}.items():
        arrays[f"in_{name}"] = a
        args.append(nc.dram_tensor(f"in_{name}", a.shape, mybir.dt.from_np(a.dtype),
                                   kind="ExternalInput").ap())
    args.append(nc.dram_tensor("out_0", (1, L, D), F32, kind="ExternalOutput").ap())
    encoder(nc, *args)
    r = _run(nc, [arrays], core_ids=[0])
    return r.results[0]["out_0"]
```

```python
from contextlib import ExitStack

import numpy as np

import concourse.bass as bass
from concourse import mybir

F32 = mybir.dt.float32
F32R = mybir.dt.float32r
ALU = mybir.AluOpType
ACT = mybir.ActivationFunctionType

P = 128
D = 1024
L = 1024
MEM = 256
DH = 128
HEADS = 12
MEM_HEADS = 4
KV = 4
GROUP = HEADS // KV
D_INNER = 2 * D
DEPTH = 2
ALPHA = (2 * DEPTH) ** 0.25
LN_EPS = 1e-5
ROPE = DH // 4
THETA = 500000.0
SCALE = DH ** -0.5
NEG = -1e30
KT = D // P
HALF = 512
TILES = L // P
NE = D_INNER // P
W_A = 128
BLOCKS = 16
W_B = 64
DIL = (1, 4, 16)

A_Q, A_K = 0, HEADS * DH
A_V = A_K + KV * DH
A_MQ = A_V + KV * DH
A_G = A_MQ + MEM_HEADS * DH
B_Q, B_K = 0, 3 * HEADS * DH
B_V = B_K + HEADS * DH
B_MQ = B_V + HEADS * DH
B_G = B_MQ + MEM_HEADS * DH

C_A = 2 * DEPTH * MEM_HEADS
C_MA = C_A + 8 * KV
C_OA = C_MA + 2 * MEM_HEADS
C_B = C_OA + 2 * NE
C_MB = C_B + 6 * HEADS
C_OB = C_MB + 2 * MEM_HEADS
U_A = DEPTH * MEM_HEADS
U_MA = U_A + 8 * KV
U_B = U_MA + 2 * MEM_HEADS
U_MB = U_B + 6 * HEADS
T_A = 0
T_MA = T_A + GROUP * TILES * KV
T_B = T_MA + TILES * MEM_HEADS
T_MB = T_B + 3 * TILES * HEADS
X_A_PER = 2 + GROUP * TILES
X_B_G = (0, 3 + TILES, 6 + 2 * TILES)
X_B_PER = 8 + 3 * TILES
X_A = 2 * DEPTH * MEM_HEADS
X_MA = X_A + X_A_PER * KV
X_B = X_MA + TILES * MEM_HEADS
X_MB = X_B + X_B_PER * HEADS
O_A = 0
O_MA = O_A + 2 * GROUP * KV
O_B = O_MA + 2 * MEM_HEADS
O_MB = O_B + 8 * HEADS
R_A = 0
R_B = R_A + 8 * KV
S_A = 0
S_MA = S_A + 2 * (GROUP + 1) * KV
S_MB = S_MA + 3 * MEM_HEADS
G_A = 0
G_MA = G_A + GROUP * KV
G_B = G_MA + MEM_HEADS
G_MB = G_B + HEADS

VECTOR_ROWS = (0, 2)
BRANCH_BANKS = (2, 3, 0, 4, 5, 6, 7, 1)

MEM_B_ORDER = (("q", 0), ("q", 1), ("q", 2), ("g", 0), ("g", 1), ("g", 2), ("q", 3), ("g", 3))


class Job:

    def __init__(self, a, x, x_odd, o, stat, tiles, vbuf, fills=(), sink=None, queries=None,
                 v_use=None, split=None, copied=None, combined=None, group=0, out=0, stored=None):
        self.a, self.x, self.x_odd, self.o, self.stat = a, x, x_odd, o, stat
        self.tiles, self.vbuf, self.fills, self.sink = tiles, vbuf, fills, sink
        self.queries, self.v_use, self.split, self.copied = queries, v_use, split, copied
        self.combined = combined
        self.group, self.out, self.stored = group, out, stored


class Part:

    def __init__(self, slot, n, dst, first, size, src, rope=None, u=None, bank=0):
        self.slot, self.n, self.dst, self.first, self.size = slot, n, dst, first, size
        self.src, self.rope, self.u, self.bank = src, rope, u, bank


class Segment:

    def __init__(self, c, slot, next_full, u, to=None, order=1, also=None, rope=None, gate=None,
                 job=None, combine=None, y=False, parts=()):
        self.c, self.slot, self.next_full, self.u = c, slot, next_full, u
        self.to, self.order, self.also, self.rope, self.gate = to, order, also, rope, gate
        self.job, self.combine, self.y = job, combine, y
        self.parts = parts
        self.split = 0 if combine is not None and combine[1] == 2 else 12 if job is None else 11


STEPS = 2 * KT
LEAD, LAG_T, LAG_PV = 3, 6, 8
BANKS_X = 4
COMB_SLOT = 4
Y_SLOT = 14
COMB_STEPS = 15


def riding(job, s):
    if job is None:
        return None, None, None, None

    def due(lag):
        return s - lag if 0 <= s - lag < TILES else None

    return (s - 1 if 1 <= s <= len(job.fills) else None), due(LEAD), due(LAG_T), due(LAG_PV)


def dilated(v, d):
    return v.rearrange("p (n r) -> p r n", r=d)


def encoder(nc, x, mem, w_in_a, sink_a, w_in_b, w_mkv, w_out, ln_g, ln_b,
            rope_cos, rope_sin, mask_a, mask_b, mask_b2, identity, out):
    ctx = ExitStack()
    with ctx:
        def sb(name, shape, dt=F32):
            return ctx.enter_context(nc.sbuf_tensor(name, shape, dt))

        def sem(name):
            return ctx.enter_context(nc.semaphore(name))

        xT = sb("xT", [P, 2, KT, L], F32R)
        w_split = sb("w_split", [P, 2, 2, D], F32R)
        w_raw = sb("w_raw", [P, 2, D])
        y_split = sb("y_split", [P, 2, 2, HALF], F32R)
        mem_k = sb("mem_k", [P, DEPTH * MEM_HEADS, MEM])
        mem_v = sb("mem_v", [P, DEPTH * MEM_HEADS, MEM])
        head_mv = sb("head_mv", [P, MEM])
        qk_split = sb("qk_split", [P, 2, 2, L], F32R)
        cosb = sb("cosb", [ROPE, L])
        sinb = sb("sinb", [ROPE, L])
        m_a = sb("m_a", [P, 3 * W_A])
        m_b = sb("m_b", [P, 2 * P])
        m_b2 = sb("m_b2", [P, P])
        m_0 = sb("m_0", [P, MEM])
        ident = sb("ident", [P, P])
        sinks = sb("sinks", [P, HEADS])
        sinks_raw = sb("sinks_raw", [P, HEADS])
        sinks_neg = sb("sinks_neg", [P, HEADS])
        rmax = sb("rmax", [P, 3, TILES])
        soft = sb("soft", [P, 2, 3, TILES])
        nmax = soft[:, 0]
        zsum = soft[:, 1]
        zinv = sb("zinv", [P, 3, TILES])
        soft_rows = sb("soft_rows", [3 * TILES, 2, P])
        soft_in = sb("soft_in", [BLOCKS, 2, 3, L // BLOCKS])
        soft_tok = sb("soft_tok", [BLOCKS, 2, 3, L // BLOCKS])
        weight = sb("weight", [BLOCKS, 3, L // BLOCKS])
        w_sum = sb("w_sum", [BLOCKS, L // BLOCKS])
        y_raw = sb("y_raw", [P, 2, HALF])
        stats = sb("stats", [P, TILES, 2, 6])
        mv = sb("mv", [P, TILES, 2])
        rstd = sb("rstd", [P, TILES, 2])
        power = sb("power", [P, 3])
        WORDS = 17 * L + 768
        work = sb("work", [P, WORDS])
        at = [0]

        def take(n):
            at[0] += n
            return work[:, at[0] - n:at[0]]

        kT = take(L)
        qT = [take(L), take(L)]
        vT = take(L)
        vT16 = take(L)
        wT_all = take(3 * L)
        wT = [wT_all[:, g * L:(g + 1) * L] for g in range(3)]
        vbuf = [take(12 * DH), wT_all[:, 0:12 * DH]]
        s_sb = [take(388) for _ in range(3)]
        p_sb = [take(388) for _ in range(3)]
        pT = [take(3 * P), take(3 * P)]
        oT = [take(L) for _ in range(3)]
        gate = take(L)
        rope_a = take(HALF)
        rope_b = take(HALF)
        assert at[0] <= WORDS
        rows = work[:, 0:TILES * D].rearrange("p (t d) -> p t d", t=TILES)
        mem_rows = work[:, TILES * D:(TILES + 2) * D].rearrange("p (t d) -> p t d", t=2)
        mem_vT = gate[:, 0:MEM]
        g_row = work[:, 11 * D:12 * D]
        b_row = work[:, 12 * D:13 * D]

        bank = [ctx.enter_context(nc.psum_tensor(f"bank{i}", [P, HALF], F32)) for i in range(8)]
        PB, SB, TB, OB = bank[0:2], bank[2:4], bank[4:6], bank[6:8]
        XB = bank[4:8]
        BB = [bank[b] for b in BRANCH_BANKS]

        y_dram = nc.dram_tensor("y_scratch", [NE, P, L], F32, kind="Internal").ap()
        soft_dram = nc.dram_tensor("soft_scratch", [2, 3 * TILES, P], F32, kind="Internal").ap()
        weight_dram = nc.dram_tensor("weight_scratch", [3, L], F32, kind="Internal").ap()
        x1_dram = nc.dram_tensor("x1_scratch", [TILES, P, D], F32, kind="Internal").ap()

        const_in = sem("const_in")
        mem_in = [sem("mem_in0"), sem("mem_in1")]
        row_in = sem("row_in")
        consts = sem("consts")
        sink_consts = sem("sink_consts")
        w_full = [sem("w_full0"), sem("w_full1")]
        w_hi = sem("w_hi")
        w_lo = sem("w_lo")
        p_ready = [sem("p_ready0"), sem("p_ready1")]
        p_free = [sem("p_free0"), sem("p_free1")]
        xt_ready = sem("xt_ready")
        xt_hi = sem("xt_hi")
        xt_lo = sem("xt_lo")
        rope_cosine = sem("rope_cosine")
        rope_turned = sem("rope_turned")
        rope_sine = sem("rope_sine")
        rope_done = sem("rope_done")
        t_ready = sem("t_ready")
        t_free = sem("t_free")
        s_ready = sem("s_ready")
        s_free = sem("s_free")
        negmax = sem("negmax")
        exp_done = sem("exp_done")
        zinv_done = sem("zinv_done")
        p_done = sem("p_done")
        pv_done = sem("pv_done")
        o_free = sem("o_free")
        tanh_done = sem("tanh_done")
        y_done = sem("y_done")
        stored = [sem(f"stored{j}") for j in range(3)]
        part_hi = sem("part_hi")
        part_lo = sem("part_lo")
        memkv = sem("memkv")
        soft_t = sem("soft_t")
        soft_out = sem("soft_out")
        soft_back = sem("soft_back")
        comb = sem("comb")
        comb_exp = sem("comb_exp")
        comb_pool = sem("comb_pool")
        weight_out = sem("weight_out")
        weight_in = sem("weight_in")
        y_full = [sem("y_full0"), sem("y_full1")]
        y_hi = sem("y_hi")
        y_lo = sem("y_lo")
        out_step = sem("out_step")
        br_ready = sem("br_ready")
        z_free = sem("z_free")
        res_in = sem("res_in")
        gb_in = sem("gb_in")
        ln_stat = sem("ln_stat")
        ln_aggr = sem("ln_aggr")
        ln_eps = sem("ln_eps")
        ln_rstd = sem("ln_rstd")
        ln_mean = sem("ln_mean")
        ln_normal = [sem("ln_normal0"), sem("ln_normal1")]
        ln_scaled = sem("ln_scaled")
        ln_done = sem("ln_done")
        ln_done_v = sem("ln_done_v")
        rows_out = sem("rows_out")
        held = sem("held")

        def a_tiles():
            tiles = []
            for t in range(TILES):
                lo, hi = max(t - 1, 0), min(t + 2, TILES)
                m0 = (lo - t + 1) * P
                tiles.append((qT[0][:, t * P:(t + 1) * P], kT[:, lo * P:hi * P], (hi - lo) * P,
                              m_a[:, m0:m0 + (hi - lo) * P],
                              [(b, P, (b - lo) * P) for b in range(lo, hi)], (t * P, lo * P)))
            return tiles

        def mem_tiles(q):
            return [(q[:, t * P:(t + 1) * P], None, MEM, m_0[:, :],
                     [(0, P, 0), (1, P, P)], (t * P, 0)) for t in range(TILES)]

        def b_tiles(g):
            q = qT[g % 2]
            tiles = []
            if g == 0:
                for t in range(TILES):
                    lo, hi = max(t * P - W_B, 0), min((t + 1) * P + W_B, L)
                    m0 = lo - (t * P - W_B)
                    chunks = [(t - 1, P, 0)] if t > 0 else []
                    chunks += [(t, P, P if t else W_B)] if t < TILES - 1 else []
                    chunks += [(7, W_B, 0)] if t == 0 else []
                    chunks += [(8, W_B, P)] if t == TILES - 1 else []
                    tiles.append((q[:, t * P:(t + 1) * P], kT[:, lo:hi], hi - lo,
                                  m_b[:, m0:m0 + hi - lo], chunks, None))
            elif g == 1:
                qd, kd = dilated(q, 4), dilated(kT, 4)
                for r in range(4):
                    tiles.append((qd[:, r, 0:P], kd[:, r, 0:P + W_B], P + W_B,
                                  m_b[:, W_B:2 * P], [(2 * r, P, 0), (2 * r + 1, W_B, P)], None))
                    tiles.append((qd[:, r, P:2 * P], kd[:, r, W_B:2 * P], P + W_B,
                                  m_b[:, 0:P + W_B], [(2 * r + 1, P, W_B), (8 + r, W_B, 0)],
                                  None))
            else:
                kd = dilated(kT, 16)
                for j in range(TILES):
                    tiles.append((q[:, j * P:(j + 1) * P], kd[:, 2 * j:2 * j + 2, :], P,
                                  m_b2[:, :], [(j, P, 0)], None))
            return tiles

        def whole_tiles(v, first, last):
            return [(v[:, t * P:(t + 1) * P], P) for t in range(first, last)]

        def b_fills(g):
            if g == 0:
                s = [(vT[:, W_B + i * P:W_B + (i + 1) * P], P) for i in range(TILES - 1)]
                return [s[0:4], s[4:7], [(vT[:, 0:W_B], W_B), (vT[:, L - W_B:L], W_B)]]
            if g == 1:
                d = dilated(vT, 4)
                s = [(d[:, r, n * P:(n + 1) * P], P) for r in range(4) for n in range(2)]
                return [s[0:4], s[4:8], [(d[:, r, W_B:P], W_B) for r in range(4)]]
            return [whole_tiles(vT16, 0, 4), whole_tiles(vT16, 4, 8)]

        def half_in_order(v, d, h):
            if d == 1:
                return v[:, h * HALF:(h + 1) * HALF]
            n = HALF // d
            return v.rearrange("p (r n) -> p r n", r=d)[:, :, h * n:(h + 1) * n]

        def like_order(v, d):
            return v if d == 1 else dilated(v, d)

        def rope_views(seg, h):
            v = half_in_order(seg.to[0:ROPE, :], seg.order, h)
            cos_h = like_order(cosb[:, h * HALF:(h + 1) * HALF], seg.order)
            sin_h = like_order(sinb[:, h * HALF:(h + 1) * HALF], seg.order)
            a, b = rope_a[0:ROPE, :], rope_b[0:ROPE, :]
            if seg.order > 1:
                a = a.rearrange("p (r n) -> p r n", r=seg.order)
                b = b.rearrange("p (r n) -> p r n", r=seg.order)
            return v, cos_h, sin_h, a, b

        def half(slot, n, dst, h, src, **kw):
            return Part(slot, n, dst, h * HALF, HALF, src[:, h * HALF:(h + 1) * HALF], bank=h, **kw)

        def unit_a(i):
            def seg(k, **kw):
                return Segment(C_A + k + i * 8, k % 2, 16 * ((C_A + k + 1) // 2 + 1) + i * 64,
                               U_A + k + i * 8, **kw)

            r, n = R_A + i * 8, S_A + i * 8
            segs = [seg(0, to=kT, rope=r, parts=[half(13, n, 1, 0, kT, rope=r + 2)]),
                    seg(1, to=vT, parts=[half(3, n + 1, 1, 1, kT, rope=r + 3)])]
            for j in range(GROUP):
                segs.append(seg(2 + 2 * j, to=qT[0], rope=r + 2 + 2 * j, parts=[
                    half(13, n + 2 + 2 * j, 0, 0, qT[0], rope=r + 4 + 2 * j)]))
                fills = [whole_tiles(vT, 0, 4), whole_tiles(vT, 4, 8)] if j == 0 else []
                x0 = 0 if j == 0 else 2 + j * TILES
                job = Job(T_A + j * TILES + i * 24, X_A + x0 + i * X_A_PER, x0 % 2,
                          O_A + 2 * j + i * 6, j, a_tiles(), vbuf[0], fills, sink=i * GROUP + j,
                          queries=r + 5 + 2 * j, split=n + 3 + 2 * j, v_use=U_A + 3 + i * 8,
                          out=j, stored=16 + i * 16)
                segs.append(seg(3 + 2 * j, job=job, gate=G_A + j + i * GROUP, y=True, parts=[
                    half(3, n + 3 + 2 * j, 0, 1, qT[0], rope=r + 5 + 2 * j)]))
            return segs

        def mem_job(layer, i, q, values, copied=None):
            before = KV if layer == 0 else KV + MEM_HEADS + HEADS
            return Job((T_MA, T_MB)[layer] + i * TILES, (X_MA, X_MB)[layer] + i * TILES, 0,
                       (O_MA, O_MB)[layer] + i * 2, 0, mem_tiles(q), values,
                       split=(S_MA, S_MB)[layer] + 2 + i * 3, copied=copied,
                       stored=16 + 16 * before + i * 16)

        def mem_parts(layer, i, slot, q, u):
            n, head = (S_MA, S_MB)[layer] + i * 3, i + layer * MEM_HEADS
            keys = mem_k[:, bass.ds(head, 1), :].rearrange("p a n -> p (a n)")
            return ([Part(slot, n, 1, 0, MEM, keys), half(slot, n + 1, 0, 0, q, u=u)],
                    [half(1, n + 2, 0, 1, q, u=u)])

        def unit_mem(i):
            job = mem_job(0, i, qT[0], head_mv, copied=i + 1)
            first, second = mem_parts(0, i, 12, qT[0], U_MA + 2 + i * 2)
            return [Segment(C_MA + i * 2, 0, 16 * ((C_MA + 1) // 2 + 1) + i * 16, U_MA + i * 2,
                            to=qT[0], parts=first),
                    Segment(C_MA + 1 + i * 2, 1, 16 * ((C_MA + 2) // 2 + 1) + i * 16,
                            U_MA + 1 + i * 2, job=job, gate=G_MA + i, y=True, parts=second)]

        def memory_b():
            queries = [qT[0], qT[1], kT, qT[0]]
            place, segs = {}, []
            for n, (what, i) in enumerate(MEM_B_ORDER):
                if what == "q":
                    place[i] = n
                    kw = dict(to=queries[i], combine=(HEADS - 1, n) if n < 3 else None, parts=[])
                else:
                    job = mem_job(1, i, queries[i], mem_v[:, MEM_HEADS + i, :])
                    first, second = mem_parts(1, i, 13, queries[i], U_MB + place[i] + 2)
                    segs[-1].parts += first
                    kw = dict(job=job, gate=G_MB + i, y=True, parts=second)
                segs.append(Segment(C_MB + n, n % 2, 16 * ((C_MB + n + 1) // 2 + 1), U_MB + n,
                                    **kw))
            return segs

        def b_seg(i, k, **kw):
            return Segment(C_B + k + i * 6, k % 2, 16 * ((C_B + k + 1) // 2 + 1) + i * 48,
                           U_B + k + i * 6, **kw)

        def front_b(i, combine=None):
            r = R_B + i * 8
            part = [None if combine is None else (combine, n) for n in range(3)]
            return [b_seg(i, 0, to=kT, rope=r, combine=part[0]),
                    b_seg(i, 1, to=vT, also=vT16, combine=part[1]),
                    b_seg(i, 2, to=qT[0], rope=r + 2, combine=part[2])]

        def back_b(i):
            segs = []
            for g in range(3):
                job = Job(T_B + g * TILES + i * 24, X_B + X_B_G[g] + i * X_B_PER, X_B_G[g] % 2,
                          O_B + 2 * g + i * 8, g, b_tiles(g), vbuf[g % 2], b_fills(g),
                          queries=R_B + 5 + 2 * g + i * 8, v_use=U_B + 3 + i * 6, group=g, out=g,
                          combined=i + (G_B + 1) if g == 1 else None,
                          stored=16 + 16 * (KV + MEM_HEADS) + i * 16 if g == 0 else None)
                if g < 2:
                    segs.append(b_seg(i, 3 + g, to=qT[(g + 1) % 2], order=(1, 16)[g],
                                      rope=R_B + 4 + 2 * g + i * 8, job=job))
                else:
                    segs.append(b_seg(i, 5, job=job, gate=G_B + i))
            return segs

        block = ctx.enter_context(nc.Block())

        @block.sync
        def _(sp):
            nc.sync.dma_start(ident[:, :], identity).then_inc(const_in, 16)
            for t in range(MEM // P):
                nc.sync.dma_start(mem_rows[:, t, :], mem[0, t * P:(t + 1) * P, :]
                                  ).then_inc(mem_in[t], 16)

            def load(c, slot, src):
                sp.wait_ge(w_lo, c + 1)
                sp.sem_inc(held, 1)
                nc.sync.dma_start(w_raw[:, slot, :].rearrange("p (k n) -> p k n", k=KT),
                                  src).then_inc(w_full[slot], 16)

            def columns(w, col):
                return w.rearrange("(k p) n -> p k n", p=P)[:, :, bass.ds(col, P)]

            def store(j, row, y):
                sp.wait_ge(y_done, y + 2)
                sp.sem_inc(held, 1)
                nc.sync.dma_start(y_dram[bass.ds(row, 1)].rearrange("a p n -> p (a n)"),
                                  oT[j]).then_inc(stored[j], 16)

            x_rows = x[0].rearrange("(t p) d -> p t d", p=P)
            for layer in range(DEPTH):
                with sp.Fori(0, MEM_HEADS) as h:
                    c = h * 2 + layer * MEM_HEADS * 2
                    load(c, 0, columns(w_mkv[layer], h * DH + MEM_HEADS * DH))
                    load(c + 1, 1, columns(w_mkv[layer], h * DH))
                    if layer == 1:
                        nc.sync.dma_start(rows[:, bass.ds(h * 2, 2), :],
                                          x_rows[:, bass.ds(h * 2, 2), :]).then_inc(row_in, 16)
                if layer == 0:
                    for t, src in ((cosb, rope_cos), (sinb, rope_sin), (m_a, mask_a), (m_b, mask_b),
                                   (m_b2, mask_b2)):
                        nc.sync.dma_start(t[:, :], src).then_inc(const_in, 16)
                    nc.sync.dma_start(sinks[:, :], sink_a[0].partition_broadcast(P)
                                      ).then_inc(const_in, 16)

            def a_head(i, j):
                c = C_A + 2 + 2 * j + i * 8
                load(c, 0, columns(w_in_a[0], i * (GROUP * DH) + (A_Q + j * DH)))
                load(c + 1, 1, columns(w_in_a[0], i * (GROUP * DH) + (A_G + j * DH)))

            def a_key_value(i):
                load(C_A + i * 8, 0, columns(w_in_a[0], i * DH + A_K))
                load(C_A + 1 + i * 8, 1, columns(w_in_a[0], i * DH + A_V))

            def a_heads(i):
                a_head(i, 0)
                for j in range(1, GROUP):
                    a_head(i, j)
                    store(j - 1, i * GROUP + (j - 1), G_A + (j - 1) + i * GROUP)

            def mem_head(i):
                c = C_MA + i * 2
                load(c, 0, columns(w_in_a[0], i * DH + A_MQ))
                load(c + 1, 1, columns(w_in_a[0], i * DH + (A_G + HEADS * DH)))

            a_key_value(0)
            with sp.Fori(0, KV - 1) as i:
                a_heads(i)
                a_key_value(i + 1)
                store(GROUP - 1, i * GROUP + (GROUP - 1), G_A + (GROUP - 1) + i * GROUP)
            a_heads(KV - 1)
            mem_head(0)
            store(GROUP - 1, HEADS - 1, G_A + HEADS - 1)

            with sp.Fori(1, MEM_HEADS) as i:
                mem_head(i)
                store(0, i + (HEADS - 1), i + (G_MA - 1))

            def branch(layer, totals, residual, ahead, dst):
                w = w_out[layer].rearrange("(e p) n -> e p n", p=P)
                c0, y0 = (C_OA, C_OB)[layer], layer * 2 * NE

                def load_w(h, e, s):
                    sp.wait_ge(w_lo, h * NE + e + (c0 + s + 1))
                    sp.sem_inc(held, 1)
                    nc.sync.dma_start(w_raw[:, s, :], w[bass.ds(e + s, 1)]
                                      .rearrange("a p n -> p (a n)")).then_inc(w_full[s], 16)

                def load_y(h, e, s):
                    sp.wait_ge(y_lo, h * NE + e + (y0 + s + 1))
                    sp.sem_inc(held, 1)
                    nc.sync.dma_start(y_raw[:, s, :], y_dram[bass.ds(e + s, 1)]
                                      .rearrange("a p n -> p (a n)")[:, bass.ds(h * HALF, HALF)]
                                      ).then_inc(y_full[s], 16)

                def load_pairs(h, first, last):
                    with sp.Fori(first // 2, last // 2) as pair:
                        for s in range(2):
                            load_w(h, pair * 2, s)
                            load_y(h, pair * 2, s)

                load_w(0, 0, 0)
                load_w(0, 0, 1)
                for j in range(3):
                    sp.wait_ge(stored[j], 16 * totals[j] + (16 if j > 0 else 0))
                load_y(0, 0, 0)
                load_y(0, 0, 1)
                store(0, NE - 1, (G_MA, G_MB)[layer] + MEM_HEADS - 1)
                load_pairs(0, 2, 8)
                sp.wait_ge(stored[0], 16 + 16 * totals[0])
                if layer == 1:
                    sp.wait_ge(rows_out, 16 * TILES)
                nc.sync.dma_start(rows[:, 0:4, :], residual[:, 0:4, :]).then_inc(res_in, 16)
                nc.sync.dma_start(g_row, ln_g[layer].partition_broadcast(P)).then_inc(gb_in, 16)
                nc.sync.dma_start(b_row, ln_b[layer].partition_broadcast(P)).then_inc(gb_in, 16)
                load_pairs(0, 8, NE)
                load_pairs(1, 0, 8)
                nc.sync.dma_start(rows[:, 4:8, :], residual[:, 4:8, :]).then_inc(res_in, 16)
                load_pairs(1, 8, NE)
                ahead()
                by_vector = VECTOR_ROWS[layer]
                with sp.Fori(0, TILES - by_vector) as t:
                    sp.wait_ge(ln_done, t + (layer * TILES + 1))
                    sp.sem_inc(held, 1)
                    nc.sync.dma_start(dst[bass.ds(t, 1)].rearrange("a p d -> p (a d)"),
                                      rows[:, bass.ds(t, 1), :].rearrange("p a d -> p (a d)")
                                      ).then_inc(rows_out, 16)
                for t in range(TILES - by_vector, TILES):
                    sp.wait_ge(ln_done_v, t - (TILES - by_vector) + 1)
                    nc.sync.dma_start(dst[t], rows[:, t, :]).then_inc(rows_out, 16)

            def b_load(i, k, col):
                load(C_B + k + i * 6, k % 2, columns(w_in_b[0], i * DH + col))

            def exchange_statistics(i):
                sp.wait_ge(o_free, i * 8 + (O_B + 8 + 2))
                sp.sem_inc(held, 1)
                nc.sync.dma_start(soft_dram.rearrange("a g n -> g a n"), soft_rows[:, :, :]
                                  ).then_inc(soft_out, 16)
                sp.wait_ge(soft_out, i * 16 + 32)
                sp.sem_inc(held, 1)
                for g, d in enumerate(DIL):
                    for a in range(2):
                        src = soft_dram[a, g * TILES:(g + 1) * TILES, :].rearrange("t n -> (t n)")
                        nc.sync.dma_start(
                            soft_in[:, a, g, :].rearrange("b (r m) -> b r m", r=d),
                            src.rearrange("(r b m) -> b r m", r=d, b=BLOCKS)
                        ).then_inc(soft_back, 16)

            def exchange_weights(i):
                sp.wait_ge(comb, i * COMB_STEPS + 11)
                sp.sem_inc(held, 1)
                nc.sync.dma_start(weight_dram.rearrange("g (b m) -> b g m", b=BLOCKS),
                                  weight[:, :, :]).then_inc(weight_out, 16)
                sp.wait_ge(weight_out, i * 16 + 16)
                sp.sem_inc(held, 1)
                nc.sync.dma_start(wT_all, weight_dram.rearrange("g n -> (g n)")
                                  .partition_broadcast(P)).then_inc(weight_in, 16)

            branch(0, (KV + MEM_HEADS, KV, KV), x[0].rearrange("(t p) d -> p t d", p=P),
                   lambda: (b_load(0, 0, B_K), b_load(0, 1, B_V)), x1_dram)
            b_load(0, 2, B_Q)
            b_load(0, 3, B_Q + HEADS * DH)
            b_load(0, 4, B_Q + 2 * HEADS * DH)
            b_load(0, 5, B_G)
            with sp.Fori(0, HEADS - 1) as i:
                b_load(i + 1, 0, B_K)
                b_load(i + 1, 1, B_V)
                b_load(i + 1, 2, B_Q)
                exchange_statistics(i)
                b_load(i + 1, 3, B_Q + HEADS * DH)
                exchange_weights(i)
                b_load(i + 1, 4, B_Q + 2 * HEADS * DH)
                store(0, i, i + G_B)
                b_load(i + 1, 5, B_G)

            def mem_load(n):
                what, i = MEM_B_ORDER[n]
                col = B_MQ + i * DH if what == "q" else B_G + (HEADS + i) * DH
                load(C_MB + n, n % 2, columns(w_in_b[0], col))

            for n in range(3):
                mem_load(n)
            exchange_statistics(HEADS - 1)
            mem_load(3)
            exchange_weights(HEADS - 1)
            mem_load(4)
            store(0, HEADS - 1, G_B + HEADS - 1)
            mem_load(5)
            for i in range(MEM_HEADS - 1):
                store(0, HEADS + i, G_MB + i)
                if i < 2:
                    mem_load(6 + i)
            branch(1, (KV + MEM_HEADS + HEADS + MEM_HEADS, KV, KV),
                   x1_dram.rearrange("t p d -> p t d"), lambda: None,
                   out[0].rearrange("(t p) d -> t p d", p=P))
            sp.wait_ge(rows_out, 16 * TILES * DEPTH)

        @block.gpsimd
        def _(pool):
            nc.gpsimd.memset(m_0[:, :], 0.0).then_inc(consts, 1)
            nc.gpsimd.memset(power[:, 0:1], LN_EPS).then_inc(consts, 1)
            nc.gpsimd.memset(power[:, 1:2], -0.5).then_inc(consts, 1)
            nc.gpsimd.memset(power[:, 2:3], -1.0).then_inc(consts, 1)
            pool.wait_ge(consts, 4)
            pool.wait_ge(t_free, X_A + 2)

            def run(seg):
                for h in range(2):
                    if h == 0 and seg.combine is not None and seg.combine[1] == 2:
                        pool.wait_ge(weight_in, seg.combine[0] * 16 + 16)
                        pool.sem_inc(held, 1)
                        nc.gpsimd.tensor_tensor(oT[2], oT[2], wT[2], ALU.mult
                                                ).then_inc(comb_pool, 1)
                    if seg.rope is None:
                        continue
                    v, cos_h, _, a, _ = rope_views(seg, h)
                    pool.wait_ge(p_free[h], seg.u + 2)
                    pool.wait_ge(rope_done, seg.rope + h + 1)
                    pool.sem_inc(held, 1)
                    nc.gpsimd.tensor_tensor(a, v, cos_h, ALU.mult).then_inc(rope_cosine, 1)

            pool.wait_ge(const_in, 16 * 7)
            with pool.Fori(0, KV) as i:
                for seg in unit_a(i):
                    run(seg)
            with pool.Fori(0, MEM_HEADS) as i:
                pool.wait_ge(pv_done, i * TILES + T_MA)
                pool.sem_inc(held, 1)
                nc.gpsimd.tensor_copy(head_mv[:, :], mem_v[:, bass.ds(i, 1), :]
                                      .rearrange("p a n -> p (a n)")).then_inc(memkv, 1)

            def norms(layer):
                for h in range(2):
                    for t in range(4 * h, 4 * h + 4):
                        n = layer * TILES + t
                        pool.wait_ge(ln_aggr, n + 1)
                        nc.gpsimd.tensor_tensor(rstd[:, t, 0:1], mv[:, t, 1:2], power[:, 0:1],
                                                ALU.add).then_inc(ln_eps, 1)
                        pool.wait_ge(ln_eps, n + 1)
                        nc.gpsimd.tensor_tensor(rstd[:, t, 1:2], rstd[:, t, 0:1], power[:, 1:2],
                                                ALU.pow).then_inc(ln_rstd, 1)
                        if h == 1:
                            pool.wait_ge(ln_rstd, n + 1)
                            nc.gpsimd.tensor_tensor(rstd[:, t, 0:1], mv[:, t, 0:1],
                                                    rstd[:, t, 1:2], ALU.mult).then_inc(ln_mean, 1)
                            m = layer * 4 + t - 4
                            pool.wait_ge(ln_mean, 2 * m + 1)
                            nc.gpsimd.tensor_tensor(rstd[:, t, 0:1], rstd[:, t, 0:1],
                                                    power[:, 2:3], ALU.mult).then_inc(ln_mean, 1)
                    for t in range(4 * h, 4 * h + 4 - (VECTOR_ROWS[layer] if h == 1 else 0)):
                        pool.wait_ge(ln_scaled, layer * TILES + t + 1)
                        nc.gpsimd.tensor_tensor(rows[:, t, :], rows[:, t, :], b_row,
                                                ALU.add).then_inc(ln_done, 1)

            norms(0)
            for seg in front_b(0):
                run(seg)
            with pool.Fori(0, HEADS - 1) as i:
                for seg in back_b(i) + front_b(i + 1, combine=i):
                    run(seg)
            for seg in back_b(HEADS - 1) + memory_b():
                run(seg)
            norms(1)

        @block.tensor
        def _(pe):

            def rows_to_columns(src, f0, f1, first, ready=None):
                for f in range(f0, f1):
                    t, k0 = f // 2, 4 * (f % 2)
                    if ready is not None:
                        ready(f)
                    pe.wait_ge(xt_lo, first + f + 1)
                    for k in range(4):
                        mm = nc.tensor.transpose(XB[f % BANKS_X][:, k * P:(k + 1) * P],
                                                 src[:, t, (k0 + k) * P:(k0 + k + 1) * P],
                                                 ident[:, :])
                    mm.then_inc(xt_ready, 1)

            def step(dst, cols, slot, k):
                w_h = w_split[:, slot, 0, k * P:(k + 1) * P]
                w_l = w_split[:, slot, 1, k * P:(k + 1) * P]
                nc.tensor.matmul(dst, w_h, xT[:, 0, k, cols], start=(k == 0), stop=False)
                nc.tensor.matmul(dst, w_h, xT[:, 1, k, cols], start=False, stop=False)
                return nc.tensor.matmul(dst, w_l, xT[:, 0, k, cols], start=False,
                                        stop=(k == KT - 1))

            def values(job, f):
                if f == 0:
                    pe.wait_ge(p_free[0], job.v_use)
                    pe.wait_ge(p_free[1], job.v_use)
                pe.wait_ge(t_free, job.x + (f + 1))
                if job.fills[f][0][1] < P:
                    pe.sem_inc(held, 1)
                for n, (src, rows_) in enumerate(job.fills[f]):
                    mm = nc.tensor.transpose(TB[(job.x_odd + f) % 2][0:rows_, n * P:(n + 1) * P],
                                             src, ident[:, :])
                mm.then_inc(t_ready, 1)

            def scores(job, t):
                q, k, n, _, _, at = job.tiles[t]
                if t == 0 and job.copied is not None:
                    pe.wait_ge(memkv, job.copied)
                if job.queries is not None:
                    if DIL[job.group] > 1:
                        if t == 0:
                            pe.wait_ge(rope_done, job.queries)
                    elif t % 4 == 0:
                        pe.wait_ge(rope_done, job.queries - 1 + t // 4)
                if job.split is not None and t % 4 == 0:
                    pe.wait_ge(part_lo, job.split + t // 4)
                pe.wait_ge(s_free, job.a + (t + 1))
                dst = SB[t % 2][:, 0:n]
                if job.split is None:
                    nc.tensor.matmul(dst, q, k, start=True, stop=True).then_inc(s_ready, 1)
                    return
                (q_h, q_l), (k_h, k_l) = ([qk_split[:, w, part, at[w]:at[w] + size]
                                           for part in range(2)] for w, size in ((0, P), (1, n)))
                nc.tensor.matmul(dst, q_h, k_h, start=True, stop=False)
                nc.tensor.matmul(dst, q_h, k_l, start=False, stop=False)
                nc.tensor.matmul(dst, q_l, k_h, start=False, stop=True).then_inc(s_ready, 1)

            def transposes(job, t):
                n = len(job.fills) + t
                pe.wait_ge(t_free, job.x + (n + 1))
                pe.wait_ge(p_done, job.a + (t + 1))
                for c, (_, keys, k0) in enumerate(job.tiles[t][4]):
                    mm = nc.tensor.transpose(TB[(job.x_odd + n) % 2][0:keys, c * P:(c + 1) * P],
                                             p_sb[t % 3][:, 1 + k0:1 + k0 + keys], ident[:, :])
                mm.then_inc(t_ready, 1)

            def outputs(job, t):
                h, chunks = t // 4, job.tiles[t][4]
                if t % 4 == 0:
                    pe.wait_ge(o_free, job.o + (h + 1))
                pe.wait_ge(t_free, job.x + (len(job.fills) + t + 3))
                for c, (v, keys, _) in enumerate(chunks):
                    mm = nc.tensor.matmul(OB[h][:, (t % 4) * P:(t % 4 + 1) * P],
                                          job.vbuf[0:keys, v * DH:(v + 1) * DH],
                                          pT[t % 2][0:keys, c * P:(c + 1) * P],
                                          start=(c == 0), stop=(c == len(chunks) - 1))
                mm.then_inc(pv_done, 1)

            def statistics(i, a):
                pe.wait_ge(o_free, i * 8 + (O_B + 7 + a))
                if a == 0:
                    pe.wait_ge(exp_done, i * 24 + (T_B + 24))
                pe.sem_inc(held, 1)
                nc.tensor.transpose(OB[a][0:3 * TILES, 0:P],
                                    soft[:, a].rearrange("p g t -> p (g t)"), ident[:, :]
                                    ).then_inc(soft_t, 1)

            def run(seg, second_half=None):
                pe.wait_ge(w_lo, seg.c + 3)
                for s in range(STEPS):
                    h, k = s // KT, s % KT
                    if s == KT and second_half is not None:
                        second_half()
                    if k == 0:
                        pe.wait_ge(p_free[h], seg.u + 1)
                    mm = step(PB[h][:, :], slice(h * HALF, (h + 1) * HALF), seg.slot, k)
                    if k == KT - 1:
                        mm.then_inc(p_ready[h], 1)
                    if seg.combine is not None and seg.combine[1] == 0 and 1 <= s < 3:
                        statistics(seg.combine[0], s - 1)
                    fill, t_s, t_t, t_o = riding(seg.job, s)
                    if fill is not None:
                        values(seg.job, fill)
                    if t_o is not None:
                        outputs(seg.job, t_o)
                    if t_t is not None:
                        transposes(seg.job, t_t)
                    if t_s is not None:
                        scores(seg.job, t_s)

            def branch(layer):
                c0, y0 = (C_OA, C_OB)[layer], layer * 2 * NE

                t_end = (T_MA, T_MB)[layer] + MEM_HEADS * TILES + 2
                x_end = (X_MA, X_MB)[layer] + MEM_HEADS * TILES + 2
                u_end = (U_MA, U_MB)[layer] + 2 * MEM_HEADS + 1
                o_end = (O_MA, O_MB)[layer] + 2 * MEM_HEADS + 2
                copied_out = [(s_free, t_end), (s_free, t_end), (p_free[0], u_end),
                              (t_free, x_end), (t_free, x_end), (o_free, o_end), (o_free, o_end),
                              (p_free[1], u_end)]

                def is_split(h, e):
                    pe.wait_ge(w_lo, h * NE + e + (c0 + 3))
                    pe.wait_ge(y_lo, h * NE + e + (y0 + 3))

                def add_to(h, b, slot, first=False, last=False, step_begins=False):
                    t, cols = b // 2, slice((b % 2) * HALF, (b % 2 + 1) * HALF)
                    if first:
                        pe.wait_ge(*copied_out[b])
                        pe.wait_ge(z_free, h * 8 + (layer * 16 + b + 1))
                    y_h = y_split[:, slot, 0, t * P:(t + 1) * P]
                    y_l = y_split[:, slot, 1, t * P:(t + 1) * P]
                    mm = nc.tensor.matmul(BB[b][:, :], y_h, w_split[:, slot, 0, cols],
                                          start=first, stop=False)
                    if step_begins:
                        mm.then_inc(out_step, 1)
                    nc.tensor.matmul(BB[b][:, :], y_h, w_split[:, slot, 1, cols],
                                     start=False, stop=False)
                    mm = nc.tensor.matmul(BB[b][:, :], y_l, w_split[:, slot, 0, cols],
                                          start=False, stop=last)
                    if last:
                        mm.then_inc(br_ready, 1)

                def out_e(h, e, slot, first=False):
                    is_split(h, e)
                    for b in range(8):
                        add_to(h, b, slot, first=first, step_begins=(b == 0))

                def last_two(h):
                    lead = 5
                    is_split(h, NE - 2)
                    for b in range(lead):
                        add_to(h, b, 0, step_begins=(b == 0))
                    is_split(h, NE - 1)
                    for b in range(8):
                        add_to(h, b, 1, last=True, step_begins=(b == 8 - lead))
                        if b + lead < 8:
                            add_to(h, b + lead, 0)

                with pe.Fori(0, 2) as h:
                    out_e(h, 0, 0, first=True)
                    with pe.Fori(1, NE - 3, 2) as e:
                        out_e(h, e, 1)
                        out_e(h, e + 1, 0)
                    out_e(h, NE - 3, 1)
                    last_two(h)

            pe.wait_ge(const_in, 16)
            rows_to_columns(mem_rows, 0, 4, 0, lambda f: pe.wait_ge(mem_in[f // 2], 16))
            pe.wait_ge(xt_lo, 4 + BANKS_X)
            with pe.Fori(0, DEPTH * MEM_HEADS) as i:
                for kv in range(2):
                    pe.wait_ge(w_lo, i * 2 + (kv + 3))
                    pe.wait_ge(p_free[kv], i + 1)
                    for k in range(KT):
                        mm = step(PB[kv][:, 0:MEM], slice(0, MEM), kv, k)
                    mm.then_inc(p_ready[kv], 1)
                pe.wait_ge(p_free[0], i + 2)
                for f in range(2):
                    pe.wait_ge(t_free, i * 2 + (f + 1))
                    nc.tensor.transpose(TB[f][:, 0:P], mem_vT[:, f * P:(f + 1) * P],
                                        ident[:, :]).then_inc(t_ready, 1)
            pe.wait_ge(row_in, 16 * 4)
            pe.wait_ge(const_in, 16 * 7)
            pe.wait_ge(t_free, X_A + 2)
            def x_half(first, h, ready=None):
                rows_to_columns(rows, h * TILES, (h + 1) * TILES, first, ready)
                pe.wait_ge(xt_lo, first + (h + 1) * TILES + BANKS_X)

            x_half(4, 0)
            run(unit_a(0)[0], lambda: x_half(4, 1))
            for seg in unit_a(0)[1:]:
                run(seg)
            with pe.Fori(1, KV) as i:
                for seg in unit_a(i):
                    run(seg)
            with pe.Fori(0, MEM_HEADS) as i:
                for seg in unit_mem(i):
                    run(seg)
            branch(0)
            def row_ready(f):
                pe.wait_ge(ln_done, f // 2 + 1)
                if f < BANKS_X:
                    pe.wait_ge(z_free, 8 + 8 + BRANCH_BANKS.index(4 + f) + 1)
                if f == TILES:
                    pe.wait_ge(z_free, 8 + 8 + 8)

            x_half(20, 0, row_ready)
            run(front_b(0)[0], lambda: x_half(20, 1, row_ready))
            for seg in front_b(0)[1:]:
                run(seg)
            with pe.Fori(0, HEADS - 1) as i:
                for seg in back_b(i) + front_b(i + 1, combine=i):
                    run(seg)
            for seg in back_b(HEADS - 1):
                run(seg)
            for seg in memory_b():
                run(seg)
            branch(1)

        @block.scalar
        def _(act):
            act.sem_inc(p_free[0], 1)
            act.sem_inc(p_free[1], 1)
            act.sem_inc(t_free, 2)
            act.sem_inc(o_free, 2)
            act.sem_inc(soft_out, 16)
            for j in range(3):
                act.sem_inc(stored[j], 16)

            def split_hi(slot, full):
                act.wait_ge(w_full[slot], full)
                nc.scalar.copy(w_split[:, slot, 0, :], w_raw[:, slot, :]).then_inc(w_hi, 1)

            def columns_hi(first, f0, f1):
                for f in range(f0, f1):
                    t, k0 = f // 2, 4 * (f % 2)
                    act.wait_ge(xt_ready, first + f + 1)
                    nc.scalar.copy(xT[:, 0, k0:k0 + 4, t * P:(t + 1) * P],
                                   XB[f % BANKS_X][:, :].rearrange("p (k n) -> p k n", k=4)
                                   ).then_inc(xt_hi, 1)

            def operand_hi(part):
                if part.rope is not None:
                    act.wait_ge(rope_done, part.rope)
                if part.u is not None:
                    act.wait_ge(p_free[part.bank], part.u)
                nc.scalar.copy(qk_split[:, part.dst, 0, part.first:part.first + part.size],
                               part.src).then_inc(part_hi, 1)

            def values(job, f):
                rows_ = job.fills[f][0][1]
                n = len(job.fills[f]) * P
                v0 = sum(len(g) for g in job.fills[:f]) * DH
                if f == 0 and job.combined is not None:
                    act.wait_ge(y_done, job.combined)
                act.wait_ge(t_ready, job.x + (f + 1))
                nc.scalar.copy(job.vbuf[0:rows_, v0:v0 + n],
                               TB[(job.x_odd + f) % 2][0:rows_, 0:n]).then_inc(t_free, 1)

            def exponential(job, t):
                n = job.tiles[t][2]
                c0 = 1 if job.sink is None else 0
                act.wait_ge(negmax, job.a + (t + 1))
                nc.scalar.activation(p_sb[t % 3][:, c0:1 + n], s_sb[t % 3][:, c0:1 + n], ACT.Exp,
                                     bias=nmax[:, job.stat, t:t + 1], scale=SCALE,
                                     accum_out=zsum[:, job.stat, t:t + 1]).then_inc(exp_done, 1)

            def transposed(job, t):
                n = len(job.fills) + t
                src, chunks = TB[(job.x_odd + n) % 2], job.tiles[t][4]
                whole = sum(keys == P for _, keys, _ in chunks)
                act.wait_ge(t_ready, job.x + (n + 1))
                cp = nc.scalar.copy(pT[t % 2][:, 0:whole * P], src[:, 0:whole * P])
                if whole < len(chunks):
                    cp = nc.scalar.copy(pT[t % 2][0:W_B, whole * P:(whole + 1) * P],
                                        src[0:W_B, whole * P:(whole + 1) * P])
                cp.then_inc(t_free, 1)

            def in_group_order(v, g, h):
                d = DIL[g]
                if d == 1:
                    return v[:, h * HALF:(h + 1) * HALF]
                return dilated(v, d)[:, h * d // 2:(h + 1) * d // 2, :]

            def group_bank(b, g):
                d = DIL[g]
                return b[:, :] if d == 1 else b[:, :].rearrange("p (r n) -> p r n", r=d // 2)

            def output_half(job, h):
                if h == 0 and job.stored is not None:
                    act.wait_ge(stored[job.out], job.stored)
                act.wait_ge(pv_done, job.a + 4 * (h + 1))
                nc.scalar.copy(in_group_order(oT[job.out], job.group, h),
                               group_bank(OB[h], job.group)).then_inc(o_free, 1)

            def project_half(seg, h):
                act.wait_ge(p_ready[h], seg.u + 1)
                if seg.gate is not None:
                    if h == 0:
                        act.wait_ge(y_done, seg.gate + 1)
                    nc.scalar.activation(gate[:, h * HALF:(h + 1) * HALF], PB[h][:, :], ACT.Tanh,
                                         scale=0.5).then_inc(tanh_done, 1)
                    return
                cp = nc.scalar.copy(half_in_order(seg.to, seg.order, h),
                                    like_order(PB[h][:, :], seg.order))
                if seg.also is not None:
                    cp = nc.scalar.copy(half_in_order(seg.also, 16, h), like_order(PB[h][:, :], 16))
                cp.then_inc(p_free[h], 1)

            def statistics(i, a):
                if a == 0:
                    act.wait_ge(soft_out, i * 16 + 16)
                act.wait_ge(soft_t, i * 2 + (a + 1))
                nc.scalar.copy(soft_rows[:, a, :], OB[a][0:3 * TILES, 0:P]).then_inc(o_free, 1)

            def exponentials(i):
                act.wait_ge(comb, i * COMB_STEPS + 6)
                nc.scalar.activation(weight[:, :, :], weight[:, :, :], ACT.Exp
                                     ).then_inc(comb_exp, 1)

            def y_tile(slot, full):
                act.wait_ge(y_full[slot], full)
                nc.scalar.copy(y_split[:, slot, 0, :], y_raw[:, slot, :]).then_inc(y_hi, 1)

            def run(seg, branch_next=None):
                for s in range(STEPS):
                    fill, t_s, t_t, t_o = riding(seg.job, s)
                    if fill is not None:
                        values(seg.job, fill)
                    for part in seg.parts:
                        if part.slot == s:
                            operand_hi(part)
                    if seg.combine is not None:
                        i, part = seg.combine
                        if part == 0 and 1 <= s < 3:
                            statistics(i, s - 1)
                        if part == 0 and s == 14:
                            exponentials(i)
                    if s == KT:
                        project_half(seg, 0)
                    if t_t is not None:
                        transposed(seg.job, t_t)
                    if t_s is not None:
                        exponential(seg.job, t_s)
                    if seg.job is not None and s == LAG_PV + 4:
                        output_half(seg.job, 0)
                    if s == seg.split:
                        split_hi((seg.slot + 1) % 2, seg.next_full)
                    if s == Y_SLOT and branch_next is not None:
                        y_tile(0, 16 * (branch_next * NE + 1))
                project_half(seg, 1)
                if seg.job is not None:
                    output_half(seg.job, 1)

            def branch(layer, more):
                c0, y0 = (C_OA, C_OB)[layer], layer * 2 * NE

                def next_w(n, slot, full):
                    act.wait_ge(out_step, n + (y0 + 1))
                    act.wait_ge(w_full[slot], full)
                    nc.scalar.copy(w_split[:, slot, 0, :], w_raw[:, slot, :]).then_inc(w_hi, 1)

                f_w, f_y = 16 * (c0 // 2), 16 * (y0 // 2)
                with act.Fori(0, 2 * NE - 2, 2) as n:
                    next_w(n, 1, n * 8 + (f_w + 16))
                    y_tile(1, n * 8 + (f_y + 16))
                    next_w(n + 1, 0, n * 8 + (f_w + 32))
                    y_tile(0, n * 8 + (f_y + 32))
                n = 2 * NE - 2
                next_w(n, 1, n * 8 + (f_w + 16))
                y_tile(1, n * 8 + (f_y + 16))
                if more:
                    next_w(n + 1, 0, n * 8 + (f_w + 32))

                def normalise(t):
                    act.wait_ge(ln_mean, 2 * (layer * 4 + t - 3))
                    nc.scalar.activation(rows[:, t, :], rows[:, t, :], ACT.Identity,
                                         bias=rstd[:, t, 0:1], scale=rstd[:, t, 1:2]
                                         ).then_inc(ln_normal[1], 1)

                act.wait_ge(br_ready, 16 * (layer + 1))
                normalise(4)
                normalise(5)
                if more:
                    columns_hi(20, 0, 2)
                normalise(6)
                if more:
                    columns_hi(20, 2, 4)
                normalise(7)
                if more:
                    columns_hi(20, 4, 2 * TILES)

            columns_hi(0, 0, 4)
            split_hi(0, 16)
            split_hi(1, 16)

            def memory_head(i, last=False):
                for kv in range(2):
                    act.wait_ge(p_ready[kv], i + 1)
                    if kv == 0 or not last:
                        split_hi(kv, i * 16 + 32)
                    if kv == 0:
                        nc.scalar.copy(mem_vT, PB[0][:, 0:MEM]).then_inc(p_free[0], 1)
                    else:
                        nc.scalar.copy(mem_k[:, bass.ds(i, 1), :].rearrange("p a n -> p (a n)"),
                                       PB[1][:, 0:MEM]).then_inc(p_free[1], 1)
                for f in range(2):
                    act.wait_ge(t_ready, i * 2 + (f + 1))
                    nc.scalar.copy(mem_v[:, bass.ds(i, 1), f * P:(f + 1) * P]
                                   .rearrange("p a n -> p (a n)"), TB[f][:, 0:P]
                                   ).then_inc(t_free, 1)

            with act.Fori(0, DEPTH * MEM_HEADS - 1) as i:
                memory_head(i)
            memory_head(DEPTH * MEM_HEADS - 1, last=True)
            columns_hi(4, 0, 2 * TILES)
            with act.Fori(0, KV) as i:
                for seg in unit_a(i):
                    run(seg)
            with act.Fori(0, MEM_HEADS - 1) as i:
                for seg in unit_mem(i):
                    run(seg)
            for n, seg in enumerate(unit_mem(MEM_HEADS - 1)):
                run(seg, branch_next=0 if n == 1 else None)
            branch(0, True)
            act.wait_ge(rows_out, 16 * TILES)
            for seg in front_b(0):
                run(seg)
            with act.Fori(0, HEADS - 1) as i:
                for seg in back_b(i) + front_b(i + 1, combine=i):
                    run(seg)
            for seg in back_b(HEADS - 1):
                run(seg)
            for n, seg in enumerate(memory_b()):
                run(seg, branch_next=1 if n == len(MEM_B_ORDER) - 1 else None)
            branch(1, False)

        @block.vector
        def _(dve):
            dve.sem_inc(w_lo, 2)
            dve.sem_inc(xt_lo, BANKS_X)
            dve.sem_inc(s_free, 2)
            dve.sem_inc(y_done, 1)
            dve.sem_inc(y_lo, 2)
            dve.sem_inc(z_free, 8)
            dve.sem_inc(rope_done, 1)

            def split_lo(slot, c):
                dve.wait_ge(w_hi, c + 1)
                nc.vector.tensor_tensor(w_split[:, slot, 1, :], w_raw[:, slot, :],
                                        w_split[:, slot, 0, :].bitcast(F32),
                                        ALU.subtract).then_inc(w_lo, 1)

            def columns_lo(first, f0, f1):
                for f in range(f0, f1):
                    t, k0 = f // 2, 4 * (f % 2)
                    dve.wait_ge(xt_hi, first + f + 1)
                    nc.vector.tensor_tensor(xT[:, 1, k0:k0 + 4, t * P:(t + 1) * P],
                                            XB[f % BANKS_X][:, :].rearrange(
                                                "p (k n) -> p k n", k=4),
                                            xT[:, 0, k0:k0 + 4, t * P:(t + 1) * P].bitcast(F32),
                                            ALU.subtract).then_inc(xt_lo, 1)

            def operand_lo(part):
                cols = slice(part.first, part.first + part.size)
                dve.wait_ge(part_hi, part.n + 1)
                nc.vector.tensor_tensor(qk_split[:, part.dst, 1, cols], part.src,
                                        qk_split[:, part.dst, 0, cols].bitcast(F32),
                                        ALU.subtract).then_inc(part_lo, 1)

            swap = [(i + ROPE // 2) % ROPE for i in range(ROPE)]

            def rotate(seg, h):
                r = seg.rope + h
                v, _, sin_h, a, b = rope_views(seg, h)
                dve.wait_ge(p_free[h], seg.u + 2)
                dve.wait_ge(rope_done, r + 1)
                dve.sem_inc(held, 1)
                nc.vector.stream_shuffle(b, v, swap).then_inc(rope_turned, 1)
                dve.wait_ge(rope_turned, r + 1)
                nc.vector.tensor_tensor(b, b, sin_h, ALU.mult).then_inc(rope_sine, 1)
                dve.wait_ge(rope_sine, r + 1)
                dve.wait_ge(rope_cosine, r + 1)
                nc.vector.tensor_tensor(v, a, b, ALU.add).then_inc(rope_done, 1)

            def project_half(seg, h):
                if seg.rope is not None:
                    rotate(seg, h)
                if seg.gate is not None:
                    cols = slice(h * HALF, (h + 1) * HALF)
                    dve.wait_ge(tanh_done, seg.gate * 2 + (h + 1))
                    nc.vector.scalar_tensor_tensor(out=gate[:, cols], in0=gate[:, cols], scalar=1.0,
                                                   in1=PB[h][:, :], op0=ALU.add, op1=ALU.mult
                                                   ).then_inc(p_free[h], 1)

            def mask(job, t):
                n, m = job.tiles[t][2], job.tiles[t][3]
                dve.wait_ge(s_ready, job.a + (t + 1))
                dve.sem_inc(held, 1)
                src = SB[t % 2][:, 0:n]
                if m.ndim != src.ndim:
                    raise AssertionError
                nc.vector.tensor_tensor_reduce(s_sb[t % 3][:, 1:1 + n], src, m, 1.0, -3.0e38,
                                               ALU.add, ALU.max, rmax[:, job.stat, t:t + 1]
                                               ).then_inc(s_free, 1)

            def bias(job, t):
                dve.wait_ge(s_free, job.a + (t + 3))
                r, n = rmax[:, job.stat, t:t + 1], nmax[:, job.stat, t:t + 1]
                if job.sink is None:
                    ts = nc.vector.tensor_scalar(n, r, -SCALE, None, ALU.mult)
                else:
                    ts = nc.vector.tensor_scalar(n, r, -SCALE, sinks_neg[:, bass.ds(job.sink, 1)],
                                                 ALU.mult, ALU.min)
                ts.then_inc(negmax, 1)

            def invert(job, t):
                dve.wait_ge(exp_done, job.a + (t + 1))
                nc.vector.reciprocal(zinv[:, job.stat, t:t + 1], zsum[:, job.stat, t:t + 1]
                                     ).then_inc(zinv_done, 1)

            def normalise(job, t):
                n = job.tiles[t][2]
                dve.wait_ge(zinv_done, job.a + (t + 1))
                nc.vector.tensor_scalar(p_sb[t % 3][:, 1:1 + n], p_sb[t % 3][:, 1:1 + n],
                                        zinv[:, job.stat, t:t + 1], None, ALU.mult
                                        ).then_inc(p_done, 1)

            def combine_weights(i):
                n = i * COMB_STEPS
                dve.wait_ge(y_done, i + (G_B + 1))
                dve.wait_ge(soft_back, i * 96 + 96)
                for g, d in enumerate(DIL):
                    nc.vector.tensor_copy(
                        soft_tok[:, :, g, :].rearrange("b a (m r) -> b a m r", r=d),
                        soft_in[:, :, g, :].rearrange("b a (r m) -> b a m r", r=d)
                    ).then_inc(comb, 1)
                m, z = soft_tok[:, 0], soft_tok[:, 1]

                def for_groups(v):
                    return v.unsqueeze(1).broadcast_to([BLOCKS, 3, L // BLOCKS])

                dve.wait_ge(comb, n + 3)
                nc.vector.tensor_tensor(w_sum[:, :], m[:, 0, :], m[:, 1, :], ALU.min
                                        ).then_inc(comb, 1)
                dve.wait_ge(comb, n + 4)
                nc.vector.tensor_tensor(w_sum[:, :], w_sum[:, :], m[:, 2, :], ALU.min
                                        ).then_inc(comb, 1)
                dve.wait_ge(comb, n + 5)
                nc.vector.tensor_tensor(weight[:, :, :], for_groups(w_sum[:, :]), m, ALU.subtract
                                        ).then_inc(comb, 1)
                dve.wait_ge(comb_exp, i + 1)
                nc.vector.tensor_tensor(weight[:, :, :], weight[:, :, :], z, ALU.mult
                                        ).then_inc(comb, 1)
                dve.wait_ge(comb, n + 7)
                nc.vector.tensor_tensor(w_sum[:, :], weight[:, 0, :], weight[:, 1, :], ALU.add
                                        ).then_inc(comb, 1)
                dve.wait_ge(comb, n + 8)
                nc.vector.tensor_tensor(w_sum[:, :], w_sum[:, :], weight[:, 2, :], ALU.add
                                        ).then_inc(comb, 1)
                dve.wait_ge(comb, n + 9)
                nc.vector.reciprocal(w_sum[:, :], w_sum[:, :]).then_inc(comb, 1)
                dve.wait_ge(comb, n + 10)
                nc.vector.scalar_tensor_tensor(out=weight[:, :, :], in0=weight[:, :, :], scalar=0.5,
                                               in1=for_groups(w_sum[:, :]), op0=ALU.mult,
                                               op1=ALU.mult).then_inc(comb, 1)

            def combine_outputs(i):
                n = i * COMB_STEPS
                dve.wait_ge(weight_in, i * 16 + 16)
                for g in range(2):
                    nc.vector.tensor_tensor(oT[g], oT[g], wT[g], ALU.mult).then_inc(comb, 1)
                dve.wait_ge(comb, n + 13)
                nc.vector.tensor_tensor(oT[0], oT[0], oT[1], ALU.add).then_inc(comb, 1)
                dve.wait_ge(comb, n + 14)
                dve.wait_ge(comb_pool, i + 1)
                nc.vector.tensor_tensor(oT[0], oT[0], oT[2], ALU.add).then_inc(comb, 1)
                dve.wait_ge(comb, n + 15)
                nc.vector.tensor_tensor(oT[0], oT[0], gate, ALU.mult).then_inc(y_done, 1)

            def y_tile(y0, n, slot):
                dve.wait_ge(y_hi, n + (y0 + 1))
                nc.vector.tensor_tensor(y_split[:, slot, 1, :], y_raw[:, slot, :],
                                        y_split[:, slot, 0, :].bitcast(F32),
                                        ALU.subtract).then_inc(y_lo, 1)

            def run(seg, branch_next=None):
                job = seg.job
                for s in range(STEPS):
                    if seg.combine is not None:
                        i, part = seg.combine
                        if part == 0 and s == 13:
                            combine_weights(i)
                    for part in seg.parts:
                        if part.slot == s:
                            operand_lo(part)
                    _, t, _, _ = riding(job, s)
                    if job is not None and job.sink is not None and s == LEAD - 1:
                        for b in range(3):
                            nc.vector.tensor_copy(s_sb[b][:, 0:1],
                                                  sinks_raw[:, bass.ds(job.sink, 1)])
                    if job is not None and LEAD <= s <= LEAD + TILES:
                        if t is not None:
                            mask(job, t)
                        if s > LEAD:
                            invert(job, s - LEAD - 1)
                        if t is not None:
                            bias(job, t)
                        if s > LEAD:
                            normalise(job, s - LEAD - 1)
                    if s == KT + 1:
                        project_half(seg, 0)
                    if seg.combine is not None and seg.combine[1] == 2 and s == COMB_SLOT:
                        combine_outputs(seg.combine[0])
                    if s == seg.split:
                        split_lo((seg.slot + 1) % 2, seg.c + 1)
                    if s == Y_SLOT and branch_next is not None:
                        y_tile(branch_next * 2 * NE, 0, 0)
                project_half(seg, 1)
                if seg.y:
                    dve.wait_ge(o_free, job.o + 4)
                    dve.wait_ge(p_free[1], seg.u + 2)
                    nc.vector.scalar_tensor_tensor(out=oT[job.out], in0=oT[job.out], scalar=0.5,
                                                   in1=gate, op0=ALU.mult, op1=ALU.mult
                                                   ).then_inc(y_done, 1)

            def branch(layer, more):
                c0, y0 = (C_OA, C_OB)[layer], layer * 2 * NE

                def step(n, slot):
                    split_lo(slot, n + (c0 + 1))
                    y_tile(y0, n + 1, slot)

                def add(h, b):
                    t, cols = 4 * h + b // 2, slice((b % 2) * HALF, (b % 2 + 1) * HALF)
                    if b == 0:
                        dve.wait_ge(res_in, 16 * (2 * layer + h + 1))
                    dve.wait_ge(br_ready, layer * 16 + h * 8 + b + 1)
                    nc.vector.scalar_tensor_tensor(out=rows[:, t, cols], in0=rows[:, t, cols],
                                                   scalar=ALPHA, in1=BB[b][:, :],
                                                   op0=ALU.mult, op1=ALU.add).then_inc(z_free, 1)

                def statistics(t):
                    n = layer * TILES + t
                    dve.wait_ge(z_free, 8 + 2 * n + 2)
                    for k in range(2):
                        nc.vector.bn_stats(stats[:, t, k, :], rows[:, t, k * HALF:(k + 1) * HALF]
                                           ).then_inc(ln_stat, 1)
                    dve.wait_ge(ln_stat, 2 * n + 2)
                    nc.vector.bn_aggr(mv[:, t, :], stats[:, t, :, :].rearrange("p a b -> p (a b)")
                                      ).then_inc(ln_aggr, 1)

                def norm(t):
                    h, m = t // 4, layer * 4 + t % 4 + 1
                    if h == 0:
                        dve.wait_ge(ln_rstd, layer * TILES + t + 1)
                        nc.vector.tensor_scalar(rows[:, t, :], rows[:, t, :], mv[:, t, 0:1],
                                                rstd[:, t, 1:2], ALU.subtract, ALU.mult
                                                ).then_inc(ln_normal[0], 1)
                    dve.wait_ge(ln_normal[h], m)
                    dve.wait_ge(gb_in, 32 * (layer + 1))
                    nc.vector.tensor_tensor(rows[:, t, :], rows[:, t, :], g_row,
                                            ALU.mult).then_inc(ln_scaled, 1)
                    if t >= TILES - VECTOR_ROWS[layer]:
                        dve.wait_ge(ln_scaled, layer * TILES + t + 1)
                        nc.vector.tensor_tensor(rows[:, t, :], rows[:, t, :], b_row,
                                                ALU.add).then_inc(ln_done_v, 1)

                with dve.Fori(0, NE - 2, 2) as n:
                    step(n, 1)
                    step(n + 1, 0)
                step(NE - 2, 1)
                for b in range(3):
                    add(0, b)
                step(NE - 1, 0)
                for b in range(3, 8):
                    add(0, b)
                for n in range(8):
                    step(NE + n, (n + 1) % 2)
                    if n < 4:
                        statistics(n)
                    else:
                        norm(n - 4)
                with dve.Fori(NE + 8, 2 * NE - 2, 2) as n:
                    step(n, 1)
                    step(n + 1, 0)
                step(2 * NE - 2, 1)
                for b in range(8):
                    add(1, b)
                    if b % 2 == 1:
                        statistics(4 + b // 2)
                    if b == 2 and more:
                        split_lo(0, c0 + 2 * NE)
                norm(4)
                if more:
                    columns_lo(20, 0, TILES)
                for t in range(5, TILES):
                    norm(t)
                    if more and t > 5:
                        columns_lo(20, 2 * (t - 2), 2 * (t - 2) + 2)
                if more:
                    columns_lo(20, 2 * (TILES - 2), 2 * TILES)

            columns_lo(0, 0, 4)
            split_lo(0, 0)
            with dve.Fori(0, DEPTH * MEM_HEADS) as i:
                split_lo(1, i * 2 + 1)
                split_lo(0, i * 2 + 2)
            columns_lo(4, 0, 2 * TILES)
            dve.wait_ge(const_in, 16 * 7)
            nc.vector.tensor_scalar(sinks_raw[:, :], sinks[:, :], 1.0 / SCALE, None,
                                    ALU.mult).then_inc(sink_consts, 1)
            nc.vector.tensor_scalar(sinks_neg[:, :], sinks[:, :], -1.0, None,
                                    ALU.mult).then_inc(sink_consts, 1)
            dve.wait_ge(sink_consts, 2)
            with dve.Fori(0, KV) as i:
                for seg in unit_a(i):
                    run(seg)
            with dve.Fori(0, MEM_HEADS - 1) as i:
                for seg in unit_mem(i):
                    run(seg)
            for n, seg in enumerate(unit_mem(MEM_HEADS - 1)):
                run(seg, branch_next=0 if n == 1 else None)
            branch(0, True)
            for seg in front_b(0):
                run(seg)
            with dve.Fori(0, HEADS - 1) as i:
                for seg in back_b(i) + front_b(i + 1, combine=i):
                    run(seg)
            for seg in back_b(HEADS - 1):
                run(seg)
            for n, seg in enumerate(memory_b()):
                run(seg, branch_next=1 if n == len(MEM_B_ORDER) - 1 else None)
            branch(1, False)


def shape_constants():
    half = ROPE // 2
    inv = (np.float64(THETA) ** (-np.arange(half, dtype=np.float32) / np.float32(half))
           ).astype(np.float32)
    ang = (np.arange(L, dtype=np.float32)[None, :] * inv[:, None]).astype(np.float32)
    cos, sin = np.cos(ang.astype(np.float64)), np.sin(ang.astype(np.float64))
    q = np.arange(P)[:, None]
    ka, kb, k2 = np.arange(3 * P)[None, :], np.arange(2 * P)[None, :], np.arange(P)[None, :]

    def masked(valid):
        return np.where(valid, 0.0, NEG).astype(np.float32)

    return {
        "rope_cos": np.concatenate([cos, cos]).astype(np.float32),
        "rope_sin": np.concatenate([-sin, sin]).astype(np.float32),
        "mask_a": masked(np.abs(ka - P - q) <= W_A),
        "mask_b": masked(np.abs(kb - W_B - q) <= W_B),
        "mask_b2": masked(q // W_B == k2 // W_B),
        "identity": np.eye(P, dtype=np.float32),
    }


_INS = ["x", "mem", "w_in_a", "sink_a", "w_in_b", "w_mkv", "w_out", "ln_g", "ln_b"]


def kernel(**inputs):
    import concourse.bacc as _bacc
    from concourse.bass_utils import run_bass_kernel_spmd as _run

    nc = _bacc.Bacc("TRN2", target_bir_lowering=False, num_devices=1,
                    dynamic_dma_scratch_size=1024)
    arrays, args = {}, []
    given = {name: np.ascontiguousarray(inputs[name]) for name in _INS}
    for name, a in {**given, **shape_constants()}.items():
        arrays[f"in_{name}"] = a
        args.append(nc.dram_tensor(f"in_{name}", a.shape, mybir.dt.from_np(a.dtype),
                                   kind="ExternalInput").ap())
    args.append(nc.dram_tensor("out_0", (1, L, D), F32, kind="ExternalOutput").ap())
    encoder(nc, *args)
    r = _run(nc, [arrays], core_ids=[0])
    return r.results[0]["out_0"]
```
